# Optimizing a Trainium2 kernel written in Bass

```python
import math
import jax, jax.numpy as jnp
from jax import lax
import numpy as np

D_MODEL = 1024
BATCH = 1
SEQ = 256
DEPTH = 2

HY_WIDTH = 768
HY_EMB = 33
HY_FFN = 64
HY_FAST_DECAY_PCT = 0.3
HY_SLOW_DECAY_PCT = 1.5
HY_TARGET = 1e-2

HEAD_DIM = 64
ATT_GROUPS = ((128, 1), (512, 4), (2048, 16))
HEADS_PER_GROUP = 4
N_HEADS = HEADS_PER_GROUP * len(ATT_GROUPS)
ATT_WIDTH = N_HEADS * HEAD_DIM
ATT_OUT = HEADS_PER_GROUP * HEAD_DIM
ROPE_THETA = 10000.0

N_BRANCHES = 2
IN_SPLITS = (3 * HY_WIDTH, ATT_WIDTH, ATT_WIDTH, ATT_WIDTH, D_MODEL, D_MODEL)
IN_COLS = sum(IN_SPLITS)

N_EXPERTS = 16
N_GROUPS = 4
EXPERTS_PER_GROUP = N_EXPERTS // N_GROUPS
TOP_K = 2
D_EXPERT = 512

NORM_EPS = 1e-6
MASK_VALUE = -1e30

kernel_name = "hybrid_hyena_dilated_attn_grouped_moe_encoder"

def rms_norm(x, g):
    xf = x.astype(jnp.float32)
    y = xf * lax.rsqrt(jnp.mean(xf * xf, axis=-1, keepdims=True) + NORM_EPS)
    return (y * g.astype(jnp.float32)).astype(x.dtype)

def modulate(h, shift, scale):
    return h * (1 + scale[:, None, :]) + shift[:, None, :]

def short_conv(u, w, b):
    L = u.shape[1]
    up = jnp.pad(u, ((0, 0), (1, 1), (0, 0)))
    return up[:, :L] * w[0] + up[:, 1:L + 1] * w[1] + up[:, 2:] * w[2] + b

def hyena_filters(L, w1, b1, w2, b2, w3, b3, w4, freq):
    f32 = jnp.float32
    t = jnp.linspace(0.0, 1.0, L, dtype=f32)[:, None]
    bands = (HY_EMB - 1) // 2
    w = 2.0 * math.pi * jnp.arange(L, dtype=f32)[:, None] / L
    f = jnp.linspace(1e-4, bands - 1, bands, dtype=f32)[None, :]
    z = jnp.concatenate([t, jnp.cos(f * w), -jnp.sin(f * w)], axis=-1)
    fr = freq.astype(f32)
    h = jnp.sin(fr * (z @ w1.astype(f32) + b1.astype(f32)))
    h = jnp.sin(fr * (h @ w2.astype(f32) + b2.astype(f32)))
    h = jnp.sin(fr * (h @ w3.astype(f32) + b3.astype(f32)))
    k = (h @ w4.astype(f32)).reshape(L, 2, HY_WIDTH)
    max_decay = math.log(HY_TARGET) / HY_FAST_DECAY_PCT
    min_decay = math.log(HY_TARGET) / HY_SLOW_DECAY_PCT
    deltas = jnp.linspace(min_decay, max_decay, HY_WIDTH, dtype=f32)
    decay = jnp.exp(-t * jnp.abs(deltas)[None, :])
    k = k * decay[:, None, :]
    return k[:, 0], k[:, 1]

def bidir_long_conv(z, k_fwd, k_bwd):
    L, C = k_fwd.shape
    kern = jnp.concatenate([k_fwd, jnp.zeros((1, C), jnp.float32), k_bwd[:0:-1]], axis=0)
    kf = jnp.fft.rfft(kern, axis=0)
    zf = jnp.fft.rfft(z.astype(jnp.float32), n=2 * L, axis=1)
    y = jnp.fft.irfft(zf * kf[None], n=2 * L, axis=1)[:, :L]
    return y.astype(z.dtype)

def hyena_mixer(u, w_sc, b_sc, w1, b1, w2, b2, w3, b3, w4, freq, hy_bias):
    L = u.shape[1]
    u = short_conv(u, w_sc, b_sc)
    x0, x1, v = jnp.split(u, 3, axis=-1)
    zv = v * x1
    k_fwd, k_bwd = hyena_filters(L, w1, b1, w2, b2, w3, b3, w4, freq)
    y = bidir_long_conv(zv, k_fwd, k_bwd) + zv * hy_bias
    return y * x0

def rope(x, pos):
    half = HEAD_DIM // 2
    inv = ROPE_THETA ** (-jnp.arange(half, dtype=jnp.float32) / half)
    ang = pos.astype(jnp.float32)[:, None] * inv[None, :]
    cos = jnp.cos(ang)[None, :, None, :]
    sin = jnp.sin(ang)[None, :, None, :]
    xf = x.astype(jnp.float32)
    a, b = xf[..., :half], xf[..., half:]
    return jnp.concatenate([a * cos - b * sin, b * cos + a * sin], axis=-1).astype(x.dtype)

def dilated_band_attention(q, k, v, dil, radius):
    B, L, H, Dh = q.shape
    Ls = L // dil
    nb = -(-Ls // radius)
    Lp = nb * radius

    def strided(t):
        return t.reshape(B, Ls, dil, H, Dh).transpose(0, 2, 3, 1, 4)

    pad4 = ((0, 0), (0, 0), (0, 0))
    qs = jnp.pad(strided(q), pad4 + ((0, Lp - Ls), (0, 0))).reshape(B, dil, H, nb, radius, Dh)
    kp = jnp.pad(strided(k), pad4 + ((radius, Lp - Ls + radius), (0, 0))).reshape(B, dil, H, nb + 2, radius, Dh)
    vp = jnp.pad(strided(v), pad4 + ((radius, Lp - Ls + radius), (0, 0))).reshape(B, dil, H, nb + 2, radius, Dh)

    def band(t):
        return jnp.concatenate([t[:, :, :, 0:nb], t[:, :, :, 1:nb + 1], t[:, :, :, 2:nb + 2]], axis=4)

    kb, vb = band(kp), band(vp)
    s = jnp.einsum('bghnqd,bghnkd->bghnqk', qs, kb, preferred_element_type=jnp.float32) * (Dh ** -0.5)
    blk = jnp.arange(nb)[:, None] * radius
    qpos = blk + jnp.arange(radius)[None, :]
    kpos = blk - radius + jnp.arange(3 * radius)[None, :]
    mask = ((jnp.abs(qpos[:, :, None] - kpos[:, None, :]) <= radius)
            & (kpos[:, None, :] >= 0) & (kpos[:, None, :] < Ls))
    s = jnp.where(mask, s, MASK_VALUE)
    m = jnp.max(s, axis=-1, keepdims=True)
    p = jnp.where(mask, jnp.exp(s - m), 0.0)
    den = jnp.maximum(jnp.sum(p, axis=-1, keepdims=True), 1e-30)
    o = jnp.einsum('bghnqk,bghnkd->bghnqd', (p / den).astype(v.dtype), vb)
    lse = (m + jnp.log(den))[..., 0]
    o = o.reshape(B, dil, H, Lp, Dh)[:, :, :, :Ls].transpose(0, 3, 1, 2, 4).reshape(B, L, H, Dh)
    lse = lse.reshape(B, dil, H, Lp)[:, :, :, :Ls].transpose(0, 3, 1, 2).reshape(B, L, H)
    return o, lse

def dilated_attention_mixer(q, k, v):
    B, L = q.shape[:2]
    outs, lses = [], []
    for g, (win, dil) in enumerate(ATT_GROUPS):
        sl = slice(g * HEADS_PER_GROUP, (g + 1) * HEADS_PER_GROUP)
        o, l = dilated_band_attention(q[:, :, sl], k[:, :, sl], v[:, :, sl], dil, win // (2 * dil))
        outs.append(o)
        lses.append(l)
    alpha = jax.nn.softmax(jnp.stack(lses, axis=0), axis=0)
    o = jnp.sum(alpha[..., None].astype(q.dtype) * jnp.stack(outs, axis=0), axis=0)
    return o.reshape(B, L, ATT_OUT)

def grouped_moe(h, router_w, router_bias, w1, w3, w2):
    B, L, D = h.shape
    t = h.reshape(B * L, D)
    scores = jax.nn.sigmoid(jnp.matmul(t, router_w, preferred_element_type=jnp.float32))
    biased = scores + router_bias.astype(jnp.float32)
    grp = biased.reshape(-1, N_GROUPS, EXPERTS_PER_GROUP)
    grp_score = jnp.sum(lax.top_k(grp, TOP_K)[0], axis=-1)
    sel = jnp.argmax(grp_score, axis=-1)
    in_grp = jnp.arange(N_GROUPS)[None, :] == sel[:, None]
    masked = jnp.where(in_grp[:, :, None], grp, MASK_VALUE).reshape(-1, N_EXPERTS)
    _, idx = lax.top_k(masked, TOP_K)
    wts = jnp.take_along_axis(scores, idx, axis=-1)
    wts = wts / jnp.sum(wts, axis=-1, keepdims=True)
    gates = jnp.sum(jax.nn.one_hot(idx, N_EXPERTS, dtype=jnp.float32) * wts[..., None], axis=1)
    gates = gates.astype(t.dtype)
    y = jnp.zeros_like(t)
    for e in range(N_EXPERTS):
        a = jax.nn.silu(t @ w1[e]) * (t @ w3[e])
        y = y + gates[:, e:e + 1] * (a @ w2[e])
    return y.reshape(B, L, D)

def setup_inputs(seed: int = 0) -> dict:
    key = jax.random.key(seed)
    ks = iter(jax.random.split(key, 32))

    def nrm(shape, scale):
        return jax.random.normal(next(ks), shape, jnp.float32) * scale

    D, E, F = D_MODEL, N_EXPERTS, D_EXPERT
    C3 = 3 * HY_WIDTH
    return {
        "x": nrm((BATCH, SEQ, D), 1.0),
        "c": nrm((BATCH, D), 1.0),
        "norm1_g": 1.0 + nrm((DEPTH, D), 0.02),
        "norm2_g": 1.0 + nrm((DEPTH, D), 0.02),
        "w_ada": nrm((DEPTH, D, 6 * D), D ** -0.5),
        "b_ada": nrm((DEPTH, 6 * D), 0.02),
        "w_in": nrm((DEPTH, D, IN_COLS), D ** -0.5),
        "w_sc": nrm((DEPTH, 3, C3), 3 ** -0.5),
        "b_sc": nrm((DEPTH, C3), 0.02),
        "hf_w1": nrm((DEPTH, HY_EMB, HY_FFN), HY_EMB ** -0.5),
        "hf_b1": nrm((DEPTH, HY_FFN), 0.1),
        "hf_w2": nrm((DEPTH, HY_FFN, HY_FFN), HY_FFN ** -0.5),
        "hf_b2": nrm((DEPTH, HY_FFN), 0.1),
        "hf_w3": nrm((DEPTH, HY_FFN, HY_FFN), HY_FFN ** -0.5),
        "hf_b3": nrm((DEPTH, HY_FFN), 0.1),
        "hf_w4": nrm((DEPTH, HY_FFN, 2 * HY_WIDTH), 0.01),
        "hf_freq": 1.0 + nrm((DEPTH, HY_FFN), 0.01),
        "hy_bias": nrm((DEPTH, HY_WIDTH), 0.5),
        "w_br_h": nrm((DEPTH, HY_WIDTH, D), HY_WIDTH ** -0.5),
        "w_br_a": nrm((DEPTH, ATT_OUT, D), ATT_OUT ** -0.5),
        "w_out": nrm((DEPTH, D, D), D ** -0.5),
        "router_w": nrm((D, E), D ** -0.5),
        "router_bias": nrm((E,), 0.01),
        "moe_w1": nrm((DEPTH, E, D, F), D ** -0.5),
        "moe_w3": nrm((DEPTH, E, D, F), D ** -0.5),
        "moe_w2": nrm((DEPTH, E, F, D), F ** -0.5),
        "final_g": 1.0 + nrm((D,), 0.02),
    }

def reference(x, c, norm1_g, norm2_g, w_ada, b_ada, w_in, w_sc, b_sc,
              hf_w1, hf_b1, hf_w2, hf_b2, hf_w3, hf_b3, hf_w4, hf_freq, hy_bias,
              w_br_h, w_br_a, w_out, router_w, router_bias, moe_w1, moe_w3, moe_w2, final_g):
    B, L, D = x.shape
    pos = jnp.arange(L)
    split_idx = [int(v) for v in np.cumsum(IN_SPLITS)[:-1]]
    c_act = jax.nn.silu(c)
    for i in range(DEPTH):
        mod = c_act @ w_ada[i] + b_ada[i]
        sh1, sc1, g1, sh2, sc2, g2 = jnp.split(mod, 6, axis=-1)

        h = modulate(rms_norm(x, norm1_g[i]), sh1, sc1)
        proj = h @ w_in[i]
        u_hy, q, k, v, gate_hy, gate_at = jnp.split(proj, split_idx, axis=-1)
        y_hy = hyena_mixer(u_hy, w_sc[i], b_sc[i], hf_w1[i], hf_b1[i], hf_w2[i], hf_b2[i],
                           hf_w3[i], hf_b3[i], hf_w4[i], hf_freq[i], hy_bias[i])
        q = rope(q.reshape(B, L, N_HEADS, HEAD_DIM), pos)
        k = rope(k.reshape(B, L, N_HEADS, HEAD_DIM), pos)
        v = v.reshape(B, L, N_HEADS, HEAD_DIM)
        y_at = dilated_attention_mixer(q, k, v)
        merged = (jax.nn.sigmoid(gate_hy) * (y_hy @ w_br_h[i])
                  + jax.nn.sigmoid(gate_at) * (y_at @ w_br_a[i]))
        x = x + g1[:, None, :] * (merged @ w_out[i])

        h = modulate(rms_norm(x, norm2_g[i]), sh2, sc2)
        x = x + g2[:, None, :] * grouped_moe(h, router_w, router_bias, moe_w1[i], moe_w3[i], moe_w2[i])
    return rms_norm(x, final_g)


_drawn_inputs = setup_inputs


def setup_inputs(seed=0):
    import zlib

    import numpy as np

    out = dict(_drawn_inputs(seed))
    spreads = {}
    factors = {'hf_freq': 8.0, 'final_g': 2.796}
    for name, (base, spread) in spreads.items():
        noise = np.random.default_rng([zlib.crc32(name.encode()), seed]).standard_normal(out[name].shape)
        drawn = base * np.exp(spread * noise) if base else spread * noise
        out[name] = __import__('jax').numpy.asarray(drawn.astype(out[name].dtype))
    for name, factor in factors.items():
        out[name] = (out[name] * factor).astype(out[name].dtype)
    return out
```

```python
from contextlib import ExitStack

import numpy as np

import concourse.bass as bass
from concourse import mybir

F32 = mybir.dt.float32
I32 = mybir.dt.int32
ALU = mybir.AluOpType
ACT = mybir.ActivationFunctionType
AX = mybir.AxisListType

P = 128
D = 1024
SEQ = 256
DEPTH = 2
NT = SEQ // P
ND = D // P
HY = 768
NH_CH = HY // P
NSC = 3 * NH_CH
EMB = 33
FFN = 64
HD = 64
HALF = HD // 2
GROUPS = 3
HPG = 4
HEADS = GROUPS * HPG
GW = HPG * HD
RADIUS = 64
DILATION = (1, 4, 16)
NE = 16
NG = 4
EPG = NE // NG
FE = 512
NF = FE // P
EPS = 1e-6
NEG = -1e30
CAP = 64
EXTRA = SEQ // CAP - 1
PAIRS = NE // 2
W = 512
HW2 = HY // 2
SCALE = HD ** -0.5

N_ADA = 6 * D // W
IN_A = 9
N_HEAD = N_ADA + IN_A + 7 + 2
BPP = 6
N_BLOCKS = N_HEAD + BPP * PAIRS
RING = 6
PER_SLOT = N_BLOCKS // RING
assert N_BLOCKS % RING == 0 and N_HEAD % RING == 0

C_ID = 0
C_CT = C_ID + P
C_ST = C_CT + NT * SEQ
C_IC = C_ST + NT * SEQ
C_IS = C_IC + NT * SEQ
C_COS = C_IS + NT * SEQ
C_SIN = C_COS + SEQ
C_MASK = C_SIN + 2 * SEQ
C_TRI = C_MASK + (NT + 2) * SEQ
C_ONE = C_TRI + P
C_IOTA = C_ONE + P
C_DESC = C_IOTA + CAP
C_ALL = C_DESC + NE

R_N1 = 0
R_N2 = R_N1 + ND
R_WSC = R_N2 + ND
R_BSC = R_WSC + 3 * NSC
R_HYB = R_BSC + NSC
R_ALL = R_HYB + NH_CH

INV2PI = float(np.float32(1.0 / (2.0 * np.pi)))
MAGIC = 1.5 * 2.0 ** 23
N_START = 6
N_SMALL = 16
N_CHAIN = 130

TWOPI_HI = 6.28125
TWOPI_LO = float(2.0 * np.pi - 6.28125)
PI_SAFE = 3.1415925


def constants():
    f64 = np.float64
    tab = np.zeros((P, C_ALL), f64)
    tab[:, C_ID:C_ID + P] = np.eye(P)
    tok = np.arange(SEQ)
    fr = np.arange(SEQ)
    cos = np.cos(2 * np.pi * ((tok[:, None] * fr[None, :]) % (2 * SEQ)) / (2 * SEQ))
    sin = np.sin(2 * np.pi * ((tok[:, None] * fr[None, :]) % (2 * SEQ)) / (2 * SEQ))
    sin[:, 0] = (-1.0) ** tok
    wt = np.full(SEQ, 2.0)
    wt[0] = 1.0
    for t in range(NT):
        rows = slice(t * P, (t + 1) * P)
        tab[:, C_CT + t * SEQ:C_CT + (t + 1) * SEQ] = cos[rows]
        tab[:, C_ST + t * SEQ:C_ST + (t + 1) * SEQ] = sin[rows]
        tab[:, C_IC + t * SEQ:C_IC + (t + 1) * SEQ] = (cos * wt).T[rows] / (2 * SEQ)
        tab[:, C_IS + t * SEQ:C_IS + (t + 1) * SEQ] = (sin * wt).T[rows] / (2 * SEQ)
    f32 = np.float32
    inv = f32(10000.0) ** (-np.arange(HALF, dtype=f32) / f32(HALF))
    ang = (tok.astype(f32)[None, :] * inv[:, None]).astype(f64)
    tab[:, C_COS:C_COS + SEQ] = np.tile(np.cos(ang), (P // HALF, 1))
    tab[:, C_SIN:C_SIN + SEQ] = -np.tile(np.sin(ang), (P // HALF, 1))
    tab[:, C_SIN + SEQ:C_SIN + 2 * SEQ] = np.tile(np.sin(ang), (P // HALF, 1))
    for t in range(NT):
        q = t * P + np.arange(P)
        tab[:, C_MASK + t * SEQ:C_MASK + (t + 1) * SEQ] = np.where(np.abs(q[:, None] - tok[None, :]) <= RADIUS, 0, NEG)
    for n, dil in enumerate(DILATION[1:]):
        q = np.arange(P)
        c = C_MASK + (NT + n) * SEQ
        tab[:, c:c + SEQ] = np.where((q[:, None] - tok[None, :]) % dil == 0, 0, NEG)
    tab[:, C_TRI:C_TRI + P] = np.triu(np.ones((P, P)), 1)
    tab[:, C_ONE:C_ONE + P] = 1.0
    tab[:, C_IOTA:C_IOTA + CAP] = np.arange(CAP)
    tab[:, C_DESC:C_DESC + NE] = NE - np.arange(NE)
    t = np.linspace(0.0, 1.0, SEQ, dtype=f32).astype(f64)
    deltas = np.linspace(np.log(1e-2) / 1.5, np.log(1e-2) / 0.3, HY, dtype=f32).astype(f64)
    dec = np.exp(-t[:, None] * np.abs(deltas)[None, :])
    dec_b = dec.copy()
    dec_b[0] = 0.0
    decay = np.stack([dec.reshape(NT, P, HY), dec_b.reshape(NT, P, HY)]).transpose(2, 0, 1, 3)
    bands = (EMB - 1) // 2
    ww = (f32(2.0 * np.pi) * tok.astype(f32)[:, None] / f32(SEQ))
    ff = np.linspace(1e-4, bands - 1, bands, dtype=f32)[None, :]
    zz = np.concatenate([t[:, None], np.cos((ff * ww).astype(f64)), -np.sin((ff * ww).astype(f64))], axis=1)
    return (tab.astype(f32), np.ascontiguousarray(decay.astype(f32)), np.ascontiguousarray(zz.T.astype(f32)))


def trunk_kernel(nc, t, out):
    with ExitStack() as ctx:
        def sb(name, shape, dt=F32):
            return ctx.enter_context(nc.sbuf_tensor(name, shape, dt))

        def sem(name):
            return ctx.enter_context(nc.semaphore(name))

        ring = [sb(f"ring{r}", [P, 8 * W]) for r in range(RING)]
        cst = sb("cst", [P, C_ALL])
        x = sb("x", [P, NT, D])
        xn = sb("xn", [P, NT, D])
        hT = sb("hT", [P, ND, SEQ])
        g1b = sb("g1b", [P, D])
        g2b = sb("g2b", [P, D])
        Kr = sb("Kr", [P, 2, HY])
        Ks = sb("Ks", [P, 2, HY])
        KX = sb("KX", [P, HY])
        x0T = sb("x0T", [P, NH_CH, SEQ])
        zvT = sb("zvT", [P, NH_CH, SEQ])
        router = sb("router", [P, ND, NE])
        rbias = sb("rbias", [P, NE])
        cpad = sb("cpad", [P, ND, 32])
        vrow = sb("vrow", [P, P])
        brow = sb("brow", [6 * ND, P])
        hrow = sb("hrow", [4, FFN])
        vT = sb("vT", [P, R_ALL])
        bT = sb("bT", [P, 6 * ND])
        hvT = sb("hvT", [FFN, 4])
        modT = sb("modT", [P, 6 * ND])
        A1 = sb("A1", [P, ND])
        A2 = sb("A2", [P, ND])
        hw1 = sb("hw1", [EMB, FFN])
        hw2 = sb("hw2", [FFN, FFN])
        hw3 = sb("hw3", [FFN, FFN])
        ss = sb("ss", [P, NT])
        rs = sb("rs", [P, NT])
        eps = sb("eps", [P, 1])
        stat = sb("stat", [P, 12, 32])
        crow = stat[0:ND, 8:12, :].rearrange("k a b -> k (a b)")
        yatT = sb("yatT", [P, 2, SEQ])
        cnt_i = sb("cnt_i", [P, PAIRS], I32)
        AREA = 6656
        area = sb("area", [P, AREA])

        cut = [0]

        def region(size):
            a = area[:, cut[0]:cut[0] + size]
            cut[0] += size
            assert cut[0] <= AREA, cut[0]
            return a

        decay = region(2 * NT * HY).rearrange("p (b t c) -> p b t c", b=2, t=NT)
        kfb = [a[:, :, :].rearrange("p k n -> p (k n)").rearrange("p (t c) -> p t c", t=NT) for a in (x0T, zvT)]
        acc = region(2 * W).rearrange("p (b n) -> p b n", b=2)
        fu = region(SEQ)
        fk = region(SEQ)
        zpos = region(SEQ)
        fh = region(SEQ)
        hw4 = xn[:, :, :].rearrange("p t d -> p (t d)")[0:FFN, 0:2 * HY]
        cut[0] = 0
        qr = region(GROUPS * 2 * SEQ).rearrange("p (g x n) -> p g x n", g=GROUPS, x=2)
        kr = region(GROUPS * 2 * SEQ).rearrange("p (g x n) -> p g x n", g=GROUPS, x=2)
        vv = region(NT * HY).rearrange("p (t n) -> p t n", t=NT)
        qm = xn[:, :, :].rearrange("p t d -> p (t d)").rearrange("p (x h n) -> p x h n", x=2, h=HPG)
        sm = region(2 * SEQ).rearrange("p (t n) -> p t n", t=NT)
        pT = region(2 * SEQ).rearrange("p (t n) -> p t n", t=NT)
        tmp = region(2 * SEQ)
        yat = region(NT * GW).rearrange("p (t n) -> p t n", t=NT)
        cut[0] = 0
        ztok = region(NT * HY).rearrange("p (t c) -> p t c", t=NT)
        Yr = region(2 * HY).rearrange("p (m c) -> p m c", m=2)
        Ys = region(2 * HY).rearrange("p (m c) -> p m c", m=2)
        ct = [region(HW2) for _ in range(4)]
        cut[0] = 0
        merged = region(NT * D).rearrange("p (t d) -> p t d", t=NT)
        mT = xn[:, :, :].rearrange("p t d -> p (t d)").rearrange("p (k n) -> p k n", k=ND)
        sg = region(2 * NT * W).rearrange("p (b t n) -> p b t n", b=2, t=NT)
        mtmp = region(W)
        cut[0] = 0
        yacc = region(NT * D).rearrange("p (t d) -> p t d", t=NT)
        hg = hT[:, :, 0:P]
        sel = region(NT * P).rearrange("p (t s) -> p t s", t=NT)
        selg = region(NT * P).rearrange("p (t s) -> p t s", t=NT)
        selT = region(SEQ)
        sil = region(FE)
        act = region(FE)
        actT = region(FE).rearrange("p (f s) -> p f s", f=NF)
        yS = region(D)
        posc = region(NT * 2).rearrange("p (t j) -> p t j", t=NT)
        gatec = region(NT * 2).rearrange("p (t j) -> p t j", t=NT)
        rt = [region(NT * NE) for _ in range(13)]
        rb = [r.rearrange("p (t e) -> p t e", t=NT) for r in rt]
        g4 = [r.rearrange("p (t g e) -> p t g e", t=NT, g=NG) for r in rt]
        score, biased, pair, tA, tB, oh1, oh2, oh, tC, tD, gate_, pos_, tE = range(13)
        fing = g1b[:, :]

        bank = [ctx.enter_context(nc.psum_tensor(f"bank{i}", [P, 512], F32)) for i in range(8)]

        ident = cst[:, C_ID:C_ID + P]
        ctab = cst[:, C_CT:C_CT + NT * SEQ].rearrange("p (t f) -> p t f", t=NT)
        stab = cst[:, C_ST:C_ST + NT * SEQ].rearrange("p (t f) -> p t f", t=NT)
        ictab = cst[:, C_IC:C_IC + NT * SEQ].rearrange("p (t f) -> p t f", t=NT)
        istab = cst[:, C_IS:C_IS + NT * SEQ].rearrange("p (t f) -> p t f", t=NT)
        rcos = cst[:, C_COS:C_COS + SEQ]
        rsin = cst[:, C_SIN:C_SIN + 2 * SEQ]
        tri = cst[:, C_TRI:C_TRI + P]
        ones = cst[:, C_ONE:C_ONE + P]
        iota = cst[:, C_IOTA:C_IOTA + CAP]
        desc = cst[:, C_DESC:C_DESC + NE]

        def mask(g, qt):
            c = C_MASK + (qt if g == 0 else NT + g - 1) * SEQ
            return cst[:, c:c + SEQ]

        slot_in = [sem(f"slot_in{r}") for r in range(RING)]
        slots_free = sem("slots_free")
        s_start = sem("s_start")
        s_small = sem("s_small")
        s_gbias = sem("s_gbias")
        s_out = sem("s_out")
        s_fing = sem("s_fing")
        v_chain = sem("v_chain")
        v_moe = sem("v_moe")
        v_ovf = sem("v_ovf")
        a_chain = sem("a_chain")
        p_c = sem("p_c")
        v_c = sem("v_c")
        a_c = sem("a_c")
        p_vec = sem("p_vec")
        v_vec = sem("v_vec")
        p_ada = sem("p_ada")
        v_ada = sem("v_ada")
        p_mod = sem("p_mod")
        v_mod = sem("v_mod")
        p_fil = sem("p_fil")
        v_fu = sem("v_fu")
        a_fh = sem("a_fh")
        p_kt = sem("p_kt")
        v_kt = sem("v_kt")
        p_ks = sem("p_ks")
        a_ks = sem("a_ks")
        v_kx = sem("v_kx")
        a_sq = sem("a_sq")
        v_xn = sem("v_xn")
        p_tr = sem("p_tr")
        v_hT = sem("v_hT")
        p_u = sem("p_u")
        a_u = sem("a_u")
        v_u = sem("v_u")
        p_qk = sem("p_qk")
        v_qk = sem("v_qk")
        p_v = sem("p_v")
        a_v = sem("a_v")
        g_qm = sem("g_qm")
        v_qm = sem("v_qm")
        p_s = sem("p_s")
        v_s = sem("v_s")
        a_p = sem("a_p")
        p_pt = sem("p_pt")
        a_pt = sem("a_pt")
        p_o = sem("p_o")
        v_md = sem("v_md")
        a_me = sem("a_me")
        v_yat = sem("v_yat")
        p_yat = sem("p_yat")
        a_yat = sem("a_yat")
        p_zt = sem("p_zt")
        a_zt = sem("a_zt")
        p_z = sem("p_z")
        v_z = sem("v_z")
        p_y = sem("p_y")
        v_y = sem("v_y")
        p_gate = sem("p_gate")
        a_gate = sem("a_gate")
        p_br = sem("p_br")
        v_br = sem("v_br")
        p_mt = sem("p_mt")
        a_mt = sem("a_mt")
        p_wo = sem("p_wo")
        v_wo = sem("v_wo")
        p_lg = sem("p_lg")
        a_lg = sem("a_lg")
        v_oh = sem("v_oh")
        p_pos = sem("p_pos")
        v_rt = sem("v_rt")
        v_layer = sem("v_layer")
        v_fin = sem("v_fin")

        def block_sems(tag):
            return {n: sem(f"{n}_{tag}") for n in (
                "v_sel", "p_selT", "p_hg", "a_selT", "a_hg", "v_hg", "p_up", "a_sil", "v_act", "p_actT", "a_actT",
                "p_down", "a_yS", "v_yS", "p_sc", "v_acc")}

        def skip(eng, signals, at, times):
            for name, k in signals.items():
                at.wait_before(eng, name)
                eng.sem_inc(at.s[name], times * k)

        def first_credit(eng, signals):
            for sems in (main, ovf):
                for name in signals:
                    eng.sem_inc(sems[name], 1)

        main = block_sems("m")
        ovf = block_sems("x")
        PE_SIGNALS = {"p_selT": 1, "p_hg": 2, "p_up": 1, "p_actT": 1, "p_down": 2, "p_sc": 4}
        ACT_SIGNALS = {"a_selT": 1, "a_hg": 1, "a_sil": 1, "a_actT": 1, "a_yS": 1}
        DVE_SIGNALS = {"v_sel": 1, "v_hg": 1, "v_act": 1, "v_yS": 1, "v_acc": 4}
        SIGNALS = {**PE_SIGNALS, **ACT_SIGNALS, **DVE_SIGNALS}

        class At:
            def __init__(self, sems, n):
                self.s, self.n = sems, n

            def wait(self, eng, name, k=None):
                k = SIGNALS[name] if k is None else k
                eng.wait_ge(self.s[name], self.n * SIGNALS[name] + (k + 1))

            def wait_before(self, eng, name):
                eng.wait_ge(self.s[name], self.n * SIGNALS[name] + 1)

        s_settled = sem("s_settled")

        def settle(eng):
            eng.sem_inc(s_settled, 1)

        block = ctx.enter_context(nc.Block())

        @block.sync
        def _(sp):
            sp.sem_inc(slots_free, RING)
            with sp.Fori(0, DEPTH) as L:
                def load(n, dst, src):
                    sp.wait_ge(slots_free, L * N_BLOCKS + (n + 1))
                    sp.dma_start(dst, src).then_inc(slot_in[n % RING], 16)

                n = 0
                for b in range(N_ADA):
                    load(n, ring[n % RING][:, :].rearrange("p (k f) -> p k f", f=W),
                         t["w_ada"][L, :, b * W:(b + 1) * W].rearrange("(k p) f -> p k f", p=P))
                    n += 1
                order = [("in", b) for b in range(IN_A)] + [("in", 9), ("brh", 0), ("in", 10), ("brh", 1),
                                                          ("in", 11), ("in", 12), ("bra", 0), ("out", 0), ("out", 1)]
                for kind, b in order:
                    if kind == "bra":
                        load(n, ring[n % RING][:, 0:2 * D].rearrange("p (k f) -> p k f", f=D),
                             t["w_br_a"][L, :, :].rearrange("(k p) f -> p k f", p=P))
                    elif kind == "brh":
                        load(n, ring[n % RING][:, 0:NH_CH * W].rearrange("p (k f) -> p k f", f=W),
                             t["w_br_h"][L, :, b * W:(b + 1) * W].rearrange("(k p) f -> p k f", p=P))
                    else:
                        src = t["w_in"] if kind == "in" else t["w_out"]
                        load(n, ring[n % RING][:, :].rearrange("p (k f) -> p k f", f=W),
                             src[L, :, b * W:(b + 1) * W].rearrange("(k p) f -> p k f", p=P))
                    n += 1
                assert n == N_HEAD
                with sp.Fori(0, PAIRS) as pr:
                    for j in range(BPP):
                        name = ("moe_w1", "moe_w3", "moe_w2")[j // 2]
                        f = FE if j < 4 else D
                        sp.wait_ge(slots_free, L * N_BLOCKS + pr * BPP + (N_HEAD + j + 1))
                        sp.dma_start(ring[j][:, :].rearrange("p (k f) -> p k f", f=f),
                                     t[name][L, pr * 2 + j % 2, :, :].rearrange("(k p) f -> p k f", p=P))\
                          .then_inc(slot_in[j], 16)

        @block.gpsimd
        def _(pool):
            with pool.Fori(0, DEPTH) as L:
                pool.wait_ge(v_layer, L + 1)
                loads = [
                    (vrow[R_N1:R_N1 + ND, :], t["norm1_g"][L, :].rearrange("(k p) -> k p", p=P)),
                    (vrow[R_N2:R_N2 + ND, :], t["norm2_g"][L, :].rearrange("(k p) -> k p", p=P)),
                    (vrow[R_WSC:R_BSC, :], t["w_sc"][L, :, :].rearrange("j (k p) -> (j k) p", p=P)),
                    (vrow[R_BSC:R_HYB, :], t["b_sc"][L, :].rearrange("(k p) -> k p", p=P)),
                    (vrow[R_HYB:R_ALL, :], t["hy_bias"][L, :].rearrange("(k p) -> k p", p=P)),
                    (brow[:, :], t["b_ada"][L, :].rearrange("(k p) -> k p", p=P)),
                    (hrow[0:1, :], t["hf_b1"][L, :].rearrange("(a n) -> a n", a=1)),
                    (hrow[1:2, :], t["hf_b2"][L, :].rearrange("(a n) -> a n", a=1)),
                    (hrow[2:3, :], t["hf_b3"][L, :].rearrange("(a n) -> a n", a=1)),
                    (hrow[3:4, :], t["hf_freq"][L, :].rearrange("(a n) -> a n", a=1)),
                    (hw1[:, :], t["hf_w1"][L, :, :]),
                    (hw2[:, :], t["hf_w2"][L, :, :]),
                    (hw3[:, :], t["hf_w3"][L, :, :]),
                    (hw4, t["hf_w4"][L, :, :]),
                    (zpos[0:EMB, :], t["zpos"]),
                    (decay, t["decay"]),
                ]
                assert len(loads) == N_SMALL
                for dst, src in loads:
                    pool.dma_start(dst, src).then_inc(s_small, 16)
                for n, g in ((2, g1b), (5, g2b)):
                    pool.dma_start(g[:, :], t["b_ada"][L, n * D:(n + 1) * D].rearrange("(a n) -> a n", a=1)
                                   .to_broadcast([P, D])).then_inc(s_gbias, 16)
                pool.wait_ge(a_ks, (L + 1) * 8)
                pool.wait_ge(v_kx, (L + 1) * 2)
                pool.wait_ge(p_tr, L * 8 + 4)
                settle(pool)
                pool.memset(qm, 0.0).then_inc(g_qm, 1)
            pool.wait_ge(s_out, 16 * NT)

        @block.tensor
        def _(pe):
            def mm(dst, lhsT, rhs, start, stop):
                return pe.matmul(dst, lhsT, rhs, start=start, stop=stop, skip_group_check=True)

            first_credit(pe, PE_SIGNALS)
            pe.wait_ge(s_start, 16 * N_START)
            pe.transpose(bank[0][:, 0:ND], crow, ident[0:ND, 0:ND]).then_inc(p_c, 1)
            pe.wait_ge(v_c, 2)

            def free_after(done, value, n=1):
                pe.wait_ge(done, value)
                pe.sem_inc(slots_free, n)

            with pe.Fori(0, DEPTH) as L:
                def landed(n):
                    pe.wait_ge(slot_in[n % RING], (L * PER_SLOT + (n // RING + 1)) * 16)
                    return ring[n % RING]

                pe.wait_ge(s_small, (L + 1) * (16 * N_SMALL))
                pe.wait_ge(v_layer, L + 1)
                pe.transpose(bank[6][:, 0:R_ALL], vrow[0:R_ALL, :], ident[0:R_ALL, 0:R_ALL])
                pe.transpose(bank[6][:, P:P + 6 * ND], brow[:, :], ident[0:6 * ND, 0:6 * ND])
                pe.transpose(bank[6][0:FFN, 2 * P:2 * P + 4], hrow[:, :], ident[0:4, 0:4]).then_inc(p_vec, 1)

                pe.wait_ge(v_vec, (L + 1) * 3)
                settle(pe)
                mm(bank[7][0:FFN, 0:SEQ], hw1[:, :], zpos[0:EMB, :], True, True).then_inc(p_fil, 1)
                for s, w in ((1, hw2), (2, hw3)):
                    pe.wait_ge(a_fh, L * 3 + s)
                    settle(pe)
                    mm(bank[7][0:FFN, 0:SEQ], w[:, :], fh[0:FFN, :], True, True).then_inc(p_fil, 1)
                pe.wait_ge(a_fh, (L + 1) * 3)
                u = 0
                for b in range(2):
                    for lt in range(NT):
                        for n in range(2):
                            if u >= 4:
                                pe.wait_ge(v_kt, L * 10 + u - 3)
                            mm(bank[u % 4][:, 0:HW2], fh[0:FFN, lt * P:(lt + 1) * P],
                               hw4[:, b * HY + n * HW2:b * HY + (n + 1) * HW2], True, True).then_inc(p_kt, 1)
                            u += 1
                pe.wait_ge(v_kt, (L + 1) * 10)
                u = 0
                for b, tab in ((0, ctab), (1, stab)):
                    for m in range(2):
                        for n in range(2):
                            if u >= 4:
                                pe.wait_ge(a_ks, L * 8 + u - 3)
                            for lt in range(NT):
                                last = mm(bank[u % 4][:, 0:HW2], tab[:, lt, m * P:(m + 1) * P],
                                          decay[:, b, lt, n * HW2:(n + 1) * HW2], lt == 0, lt == NT - 1)
                            last.then_inc(p_ks, 1)
                            u += 1
                for n in range(2):
                    for lt in range(NT):
                        last = mm(bank[4 + n][0:1, 0:HW2], stab[:, lt, 0:1],
                                  decay[:, 0, lt, n * HW2:(n + 1) * HW2], lt == 0, lt == NT - 1)
                last.then_inc(p_ks, 1)

                def ada_post(n):
                    pe.wait_ge(v_ada, L * N_ADA + n + 1)
                    if n // 2 in (2, 5):
                        q = (n // 2 == 5) * 2 + n % 2
                        if q >= 1:
                            pe.wait_ge(v_mod, L * 5 + q)
                        mm(bank[5][:, :], ones, acc[:, n % 2, :], True, True).then_inc(p_mod, 1)
                    else:
                        for j in range(4):
                            last = mm(bank[6][:, n * 4 + j:n * 4 + j + 1], acc[:, n % 2, j * P:(j + 1) * P],
                                      ones[:, 0:1], True, True)
                        last.then_inc(p_mod, 1)

                pe.wait_ge(a_ks, (L + 1) * 8)
                pe.wait_ge(v_kx, (L + 1) * 2)
                for n in range(N_ADA):
                    w = landed(n)[:, :].rearrange("p (k f) -> p k f", f=W)
                    if n >= 2:
                        pe.wait_ge(v_ada, L * N_ADA + n - 1)
                    for h in range(2):
                        for j in range(4):
                            k = h * 4 + j
                            last = mm(bank[n % 2][32 * j:32 * j + 32, :], cpad[:, k, :], w[:, k, :], h == 0, h == 1)
                    last.then_inc(slots_free, 1)
                    if n >= 1:
                        ada_post(n - 1)
                ada_post(N_ADA - 1)

                def transposes_to_h(q):
                    pe.wait_ge(v_xn, L * 2 + q + 1)
                    for k in range(ND):
                        for tt in range(NT):
                            last = pe.transpose(bank[k // 2][:, (k % 2) * SEQ + tt * P:(k % 2) * SEQ + (tt + 1) * P],
                                                xn[:, tt, k * P:(k + 1) * P], ident)
                        if k % 2:
                            last.then_inc(p_tr, 1)

                pe.wait_ge(v_mod, (L + 1) * 5)
                transposes_to_h(0)
                pe.wait_ge(v_hT, L * 8 + 4)

                nb = N_ADA
                for c in range(NSC):
                    b = c // 4
                    w = landed(nb + b)[:, :].rearrange("p (k f) -> p k f", f=W)
                    if c >= 4:
                        pe.wait_ge(v_u, L * NSC + c - 3)
                    for k in range(ND):
                        last = mm(bank[c % 4][:, 0:SEQ], w[:, k, (c % 4) * P:(c % 4 + 1) * P], hT[:, k, :],
                                  k == 0, k == ND - 1)
                    last.then_inc(p_u, 1)
                    if c % 4 == 3:
                        free_after(p_u, L * NSC + c + 1)
                for g in range(2 * GROUPS):
                    col = NSC * P + g * GW
                    b, o = col // W, col % W
                    w = landed(nb + b)[:, :].rearrange("p (k f) -> p k f", f=W)
                    if g >= 2:
                        pe.wait_ge(v_qk, L * 6 + g - 1)
                    for xx in range(2):
                        for k in range(ND):
                            for hh in range(HPG):
                                a = o + hh * HD + xx * HALF
                                last = mm(bank[4 + g % 2][hh * HALF:(hh + 1) * HALF, xx * SEQ:(xx + 1) * SEQ],
                                          w[:, k, a:a + HALF], hT[:, k, :], k == 0, k == ND - 1)
                    last.then_inc(p_qk, 1)
                    if o + GW == W:
                        free_after(p_qk, L * 6 + g + 1)
                for tt in range(NT):
                    for half in range(2):
                        b, o, n = (7, GW, GW) if half == 0 else (8, 0, W)
                        w = landed(nb + b)[:, :].rearrange("p (k f) -> p k f", f=W)
                        for k in range(ND):
                            last = mm(bank[6 + half][:, 0:n], hT[:, k, tt * P:(tt + 1) * P], w[:, k, o:o + n],
                                      k == 0, k == ND - 1)
                        last.then_inc(p_v, 1)
                    if tt == 0:
                        pe.wait_ge(a_v, L * 4 + 2)
                free_after(p_v, L * 4 + 4, 2)

                pe.wait_ge(v_u, (L + 1) * NSC)
                pe.wait_ge(v_qk, (L + 1) * 6)
                pe.wait_ge(a_v, (L + 1) * 4)

                def scores(h):
                    g = h // HPG
                    pe.wait_ge(v_qm, L * GROUPS + g + 1)
                    if h >= 2:
                        pe.wait_ge(v_s, L * HEADS + h - 1)
                    for qt in range(NT):
                        for xx in range(2):
                            last = mm(bank[h % 2][:, qt * SEQ:(qt + 1) * SEQ], qm[:, xx, h % HPG, qt * P:(qt + 1) * P],
                                      kr[:, g, xx, :], xx == 0, xx == 1)
                    last.then_inc(p_s, 1)

                def attend(h):
                    pe.wait_ge(a_p, L * HEADS + h + 1)
                    if h >= 2:
                        pe.wait_ge(a_pt, L * HEADS + h - 1)
                    for qt in range(NT):
                        for kt in range(NT):
                            last = pe.transpose(bank[2 + h % 2][:, kt * SEQ + qt * P:kt * SEQ + (qt + 1) * P],
                                                sm[:, qt, kt * P:(kt + 1) * P], ident)
                    last.then_inc(p_pt, 1)

                def values(h):
                    pe.wait_ge(a_pt, L * HEADS + h + 1)
                    for qt in range(NT):
                        for kt in range(NT):
                            last = mm(bank[4 + 2 * qt + h // 8][:, (h % 8) * HD:(h % 8 + 1) * HD],
                                      pT[:, kt, qt * P:(qt + 1) * P], vv[:, kt, h * HD:(h + 1) * HD],
                                      kt == 0, kt == NT - 1)
                    last.then_inc(p_o, 1)

                scores(0)
                for h in range(HEADS):
                    if h + 1 < HEADS:
                        scores(h + 1)
                    attend(h)
                    values(h)
                pe.wait_ge(v_yat, L + 1)
                for c in range(2):
                    for tt in range(NT):
                        last = pe.transpose(bank[0][:, c * SEQ + tt * P:c * SEQ + (tt + 1) * P],
                                            yat[:, tt, c * P:(c + 1) * P], ident)
                last.then_inc(p_yat, 1)

                for tt in range(NT):
                    for half in range(2):
                        for j in range(3):
                            c = half * 3 + j
                            last = pe.transpose(bank[1 + tt * 2 + half][:, j * P:(j + 1) * P],
                                                zvT[:, c, tt * P:(tt + 1) * P], ident)
                        last.then_inc(p_zt, 1)
                pe.wait_ge(a_zt, (L + 1) * 4)
                u = 0
                for m in range(2):
                    for n in range(2):
                        if u >= 2:
                            pe.wait_ge(v_z, L * 4 + u - 1)
                        if u == 0:
                            pe.wait_ge(a_yat, L + 1)
                        for s, tab in enumerate((ctab, stab)):
                            for tt in range(NT):
                                last = mm(bank[2 * (u % 2) + s][:, 0:HW2], tab[:, tt, m * P:(m + 1) * P],
                                          ztok[:, tt, n * HW2:(n + 1) * HW2], tt == 0, tt == NT - 1)
                        last.then_inc(p_z, 1)
                        u += 1
                pe.wait_ge(v_z, (L + 1) * 4)
                for c in range(NH_CH):
                    if c >= 4:
                        pe.wait_ge(v_y, L * NH_CH + c - 3)
                    q = 0
                    for spec, tab in ((Yr, ictab), (Ys, istab)):
                        for m in range(2):
                            last = mm(bank[4 + c % 4][:, 0:SEQ], spec[:, m, c * P:(c + 1) * P], tab[:, m, :],
                                      q == 0, q == 3)
                            q += 1
                    last.then_inc(p_y, 1)

                nb = N_ADA + IN_A

                def gate(q, n):
                    w = landed(n)[:, :].rearrange("p (k f) -> p k f", f=W)
                    if q >= 1:
                        pe.wait_ge(a_gate, L * 8 + 2 * q)
                    for tt in range(NT):
                        for k in range(ND):
                            last = mm(bank[tt][:, :], hT[:, k, tt * P:(tt + 1) * P], w[:, k, :], k == 0, k == ND - 1)
                        if tt == NT - 1:
                            last.then_inc(p_gate, 1)
                        else:
                            last.then_inc(p_gate, 1)
                    free_after(p_gate, L * 8 + 2 * q + 2)

                def branch(q, w, src, ks, o):
                    if q >= 1:
                        pe.wait_ge(v_br, L * 8 + 2 * q)
                    for tt in range(NT):
                        for k in range(ks):
                            last = mm(bank[2 + tt][:, :], src[:, k, tt * P:(tt + 1) * P], w[:, k, o:o + W],
                                      k == 0, k == ks - 1)
                        last.then_inc(p_br, 1)

                pe.wait_ge(v_y, (L + 1) * NH_CH)
                for q in range(2):
                    gate(q, nb + 2 * q)
                    wv = landed(nb + 2 * q + 1)[:, 0:NH_CH * W].rearrange("p (k f) -> p k f", f=W)
                    branch(q, wv, x0T, NH_CH, 0)
                    free_after(p_br, L * 8 + 2 * q + 2)
                gate(2, nb + 4)
                gate(3, nb + 5)
                wv = landed(nb + 6)[:, 0:2 * D].rearrange("p (k f) -> p k f", f=D)
                branch(2, wv, yatT, 2, 0)
                branch(3, wv, yatT, 2, W)
                free_after(p_br, L * 8 + 8)
                pe.wait_ge(v_br, (L + 1) * 8)
                for k in range(ND):
                    for tt in range(NT):
                        last = pe.transpose(bank[4 + k // 2][:, (k % 2) * SEQ + tt * P:(k % 2) * SEQ + (tt + 1) * P],
                                            merged[:, tt, k * P:(k + 1) * P], ident)
                    if k % 2:
                        last.then_inc(p_mt, 1)
                pe.wait_ge(a_mt, (L + 1) * 4)
                for n in range(2):
                    w = landed(nb + 7 + n)[:, :].rearrange("p (k f) -> p k f", f=W)
                    for tt in range(NT):
                        for k in range(ND):
                            last = mm(bank[2 * n + tt][:, :], mT[:, k, tt * P:(tt + 1) * P], w[:, k, :],
                                      k == 0, k == ND - 1)
                        last.then_inc(p_wo, 1)
                    free_after(p_wo, L * 4 + 2 * n + 2)

                pe.wait_ge(v_wo, (L + 1) * 4)
                transposes_to_h(1)
                pe.wait_ge(v_hT, (L + 1) * 8)
                for tt in range(NT):
                    for k in range(ND):
                        last = mm(bank[4][:, tt * NE:(tt + 1) * NE], hT[:, k, tt * P:(tt + 1) * P], router[:, k, :],
                                  k == 0, k == ND - 1)
                last.then_inc(p_lg, 1)
                pe.wait_ge(v_oh, L + 1)
                mm(bank[5][:, 0:NE], tri, rb[oh][:, 0, :], True, True)
                mm(bank[5][:, NE:2 * NE], ones, rb[oh][:, 0, :], True, False)
                mm(bank[5][:, NE:2 * NE], tri, rb[oh][:, 1, :], False, True)
                mm(bank[5][:, 2 * NE:3 * NE], ones, rb[oh][:, 0, :], True, False)
                mm(bank[5][:, 2 * NE:3 * NE], ones, rb[oh][:, 1, :], False, True).then_inc(p_pos, 1)
                pe.wait_ge(v_rt, L + 1)
                settle(pe)

                def expert_block(at, free):
                    at.wait(pe, "v_sel")
                    at.wait_before(pe, "v_acc")
                    for tt in range(NT):
                        last = pe.transpose(bank[4][:, tt * P:(tt + 1) * P], selg[:, tt, :], ident)
                    last.then_inc(at.s["p_selT"], 1)
                    for k in range(ND):
                        for tt in range(NT):
                            last = mm(bank[2 + k // 4][:, (k % 4) * P:(k % 4 + 1) * P], xn[:, tt, k * P:(k + 1) * P],
                                      sel[:, tt, :], tt == 0, tt == NT - 1)
                        if k % 4 == 3:
                            last.then_inc(at.s["p_hg"], 1)
                    at.wait(pe, "a_hg")
                    at.wait(pe, "v_hg")
                    for which in range(2):
                        for k in range(ND):
                            for e in range(2):
                                w = ring[2 * which + e][:, :].rearrange("p (k f) -> p k f", f=FE)
                                last = mm(bank[which][CAP * e:CAP * (e + 1), :], hg[:, k, CAP * e:CAP * (e + 1)],
                                          w[:, k, :], k == 0, k == ND - 1)
                        if which == 1:
                            last.then_inc(at.s["p_up"], 1)
                    if free:
                        at.wait(pe, "p_up")
                        pe.sem_inc(slots_free, 4)
                    at.wait(pe, "v_act")
                    for f in range(NF):
                        last = pe.transpose(bank[5][:, f * P:(f + 1) * P], act[:, f * P:(f + 1) * P], ident)
                    last.then_inc(at.s["p_actT"], 1)
                    at.wait(pe, "a_actT")
                    for n in range(2):
                        for f in range(NF):
                            for e in range(2):
                                w = ring[4 + e][:, :].rearrange("p (k f) -> p k f", f=D)
                                last = mm(bank[6 + n][CAP * e:CAP * (e + 1), :], actT[:, f, CAP * e:CAP * (e + 1)],
                                          w[:, f, n * W:(n + 1) * W], f == 0, f == NF - 1)
                        last.then_inc(at.s["p_down"], 1)
                    if free:
                        at.wait(pe, "p_down")
                        pe.sem_inc(slots_free, 2)
                    at.wait(pe, "a_yS")
                    at.wait(pe, "v_yS")
                    at.wait(pe, "a_selT")
                    for tt in range(NT):
                        for n in range(2):
                            mm(bank[2 + 2 * tt + n][:, :], selT[:, tt * P:(tt + 1) * P], yS[:, n * W:(n + 1) * W],
                               True, True).then_inc(at.s["p_sc"], 1)

                with pe.Fori(0, PAIRS) as pr:
                    n = pe.value_load(cnt_i[0:1, bass.ds(pr, 1)], min_val=0, max_val=SEQ)
                    for j in range(BPP):
                        pe.wait_ge(slot_in[j], (L * PER_SLOT + pr + (N_HEAD // RING + 1)) * 16)
                    run = L * PAIRS + pr
                    At(ovf, run * EXTRA).wait_before(pe, "v_acc")
                    with pe.If(n <= CAP):
                        expert_block(At(main, run), True)
                        skip(pe, PE_SIGNALS, At(ovf, run * EXTRA), EXTRA)
                    with pe.Else():
                        expert_block(At(main, run), False)
                        with pe.Fori(0, EXTRA) as b:
                            with pe.If(n > b * CAP + CAP):
                                At(main, run).wait(pe, "v_acc")
                                expert_block(At(ovf, run * EXTRA + b), False)
                            with pe.Else():
                                skip(pe, PE_SIGNALS, At(ovf, run * EXTRA + b), 1)
                        At(ovf, run * EXTRA + (EXTRA - 1)).wait(pe, "p_sc")
                        pe.sem_inc(slots_free, BPP)

        @block.scalar
        def _(sc):
            starts = [
                (cst[:, :], t["cst"]),
                (crow, t["c"][0, :].rearrange("(k p) -> k p", p=P)),
                (router[:, :, :], t["router_w"].rearrange("(k p) e -> p k e", p=P)),
                (rbias[:, :], t["router_bias"].rearrange("(a n) -> a n", a=1).to_broadcast([P, NE])),
                (x[:, 0, :], t["x"][0, 0:P, :]),
                (x[:, 1, :], t["x"][0, P:2 * P, :]),
            ]
            assert len(starts) == N_START
            for dst, src in starts:
                sc.dma_start(dst, src).then_inc(s_start, 16)
            first_credit(sc, ACT_SIGNALS)
            sc.wait_ge(p_c, 1)
            sc.activation(stat[:, 0, 0:ND], bank[0][:, 0:ND], ACT.Sigmoid).then_inc(a_c, 1)
            sc.wait_ge(s_start, 16 * N_START)

            with sc.Fori(0, DEPTH) as L:
                for s in range(3):
                    sc.wait_ge(v_fu, L * 3 + s + 1)
                    sc.activation(fh[0:FFN, :], fu[0:FFN, :], ACT.Sin).then_inc(a_fh, 1)
                u = 0
                for dst in (Kr, Ks):
                    for m in range(2):
                        for n in range(2):
                            sc.wait_ge(p_ks, L * 9 + u + 1)
                            sc.activation(dst[:, m, n * HW2:(n + 1) * HW2], bank[u % 4][:, 0:HW2], ACT.Copy)\
                              .then_inc(a_ks, 1)
                            u += 1

                def squares(q):
                    for tt in range(NT):
                        last = sc.activation(xn[:, tt, :], x[:, tt, :], ACT.Square, scale=D ** -0.5,
                                             accum_out=ss[:, tt:tt + 1])
                    last.then_inc(a_chain, 1)
                    sc.wait_ge(a_chain, L * 2 + q + 1)
                    sc.activation(rs[:, :], ss[:, :], ACT.Sqrt, bias=eps[:, :]).then_inc(a_sq, 1)

                sc.wait_ge(p_kt, (L + 1) * 8)
                sc.wait_ge(v_layer, L + 1)
                squares(0)
                for c in range(NSC):
                    sc.wait_ge(p_u, L * NSC + c + 1)
                    if c >= 2 * NH_CH + 1:
                        sc.wait_ge(v_u, L * NSC + c)
                    dst = x0T[:, c, :] if c < NH_CH else zvT[:, c - NH_CH, :] if c < 2 * NH_CH else tmp[:, 0:SEQ]
                    sc.activation(dst, bank[c % 4][:, 0:SEQ], ACT.Identity,
                                  bias=vT[:, R_BSC + c:R_BSC + c + 1],
                                  scale=vT[:, R_WSC + NSC + c:R_WSC + NSC + c + 1]).then_inc(a_u, 1)
                for tt in range(NT):
                    for half in range(2):
                        sc.wait_ge(p_v, L * 4 + 2 * tt + half + 1)
                        o, n = (0, GW) if half == 0 else (GW, W)
                        sc.activation(vv[:, tt, o:o + n], bank[6 + half][:, 0:n], ACT.Copy).then_inc(a_v, 1)
                for h in range(HEADS):
                    sc.wait_ge(v_s, L * HEADS + h + 1)
                    for qt in range(NT):
                        last = sc.activation(sm[:, qt, :], sm[:, qt, :], ACT.Exp,
                                             bias=stat[:, 2, h * NT + qt:h * NT + qt + 1], scale=SCALE,
                                             accum_out=stat[:, 1, h * NT + qt:h * NT + qt + 1])
                    last.then_inc(a_p, 1)
                    sc.wait_ge(p_pt, L * HEADS + h + 1)
                    if h >= 1:
                        sc.wait_ge(p_o, L * HEADS + h)
                    sc.activation(pT[:, :, :].rearrange("p t n -> p (t n)"), bank[2 + h % 2][:, :], ACT.Copy)\
                      .then_inc(a_pt, 1)
                sc.wait_ge(v_md, L + 1)
                sc.activation(stat[:, 4, 0:HEADS * NT], stat[:, 3, 0:HEADS * NT], ACT.Exp, scale=SCALE).then_inc(a_me, 1)
                sc.wait_ge(p_yat, L + 1)
                sc.activation(yatT[:, :, :].rearrange("p c n -> p (c n)"), bank[0][:, :], ACT.Copy).then_inc(a_yat, 1)
                for tt in range(NT):
                    for half in range(2):
                        sc.wait_ge(p_zt, L * 4 + 2 * tt + half + 1)
                        sc.activation(ztok[:, tt, half * HW2:(half + 1) * HW2],
                                      bank[1 + tt * 2 + half][:, 0:HW2], ACT.Copy).then_inc(a_zt, 1)
                for q in range(4):
                    if q >= 2:
                        sc.wait_ge(v_br, L * 8 + 2 * (q - 1))
                    for tt in range(NT):
                        sc.wait_ge(p_gate, L * 8 + 2 * q + tt + 1)
                        sc.activation(sg[:, q % 2, tt, :], bank[tt][:, :], ACT.Sigmoid).then_inc(a_gate, 1)
                for j in range(4):
                    sc.wait_ge(p_mt, L * 4 + j + 1)
                    sc.activation(mT[:, 2 * j:2 * j + 2, :].rearrange("p k n -> p (k n)"), bank[4 + j][:, :], ACT.Copy)\
                      .then_inc(a_mt, 1)
                sc.wait_ge(v_wo, (L + 1) * 4)
                squares(1)
                sc.wait_ge(p_lg, L + 1)
                sc.activation(rt[score], bank[4][:, 0:NT * NE], ACT.Sigmoid).then_inc(a_lg, 1)

                def expert_block(at):
                    at.wait(sc, "p_selT")
                    sc.activation(selT, bank[4][:, 0:SEQ], ACT.Copy).then_inc(at.s["a_selT"], 1)
                    at.wait(sc, "p_hg", 1)
                    for k in range(4):
                        last = sc.activation(hg[:, k, :], bank[2][:, k * P:(k + 1) * P], ACT.Identity,
                                             bias=modT[:, 3 * ND + k:3 * ND + k + 1], scale=A2[:, k:k + 1])
                    last.then_inc(at.s["a_hg"], 1)
                    at.wait(sc, "p_up")
                    sc.activation(sil, bank[0][:, :], ACT.Silu).then_inc(at.s["a_sil"], 1)
                    at.wait(sc, "p_actT")
                    sc.activation(actT[:, :, :].rearrange("p f s -> p (f s)"), bank[5][:, :], ACT.Copy)\
                      .then_inc(at.s["a_actT"], 1)
                    at.wait(sc, "p_down", 1)
                    sc.activation(yS[:, 0:W], bank[6][:, :], ACT.Copy).then_inc(at.s["a_yS"], 1)

                sc.wait_ge(v_rt, L + 1)
                with sc.Fori(0, PAIRS) as pr:
                    n = sc.value_load(cnt_i[0:1, bass.ds(pr, 1)], min_val=0, max_val=SEQ)
                    run = L * PAIRS + pr
                    At(ovf, run * EXTRA).wait_before(sc, "p_sc")
                    expert_block(At(main, run))
                    with sc.If(n <= CAP):
                        skip(sc, ACT_SIGNALS, At(ovf, run * EXTRA), EXTRA)
                    with sc.Else():
                        with sc.Fori(0, EXTRA) as b:
                            with sc.If(n > b * CAP + CAP):
                                At(main, run).wait(sc, "p_sc")
                                At(ovf, run * EXTRA + b).wait_before(sc, "p_sc")
                                expert_block(At(ovf, run * EXTRA + b))
                            with sc.Else():
                                skip(sc, ACT_SIGNALS, At(ovf, run * EXTRA + b), 1)
            sc.wait_ge(v_layer, DEPTH + 1)
            sc.dma_start(fing, t["final_g"].rearrange("(a n) -> a n", a=1).to_broadcast([P, D])).then_inc(s_fing, 16)
            sc.wait_ge(v_layer, DEPTH + 1)
            for tt in range(NT):
                last = sc.activation(xn[:, tt, :], x[:, tt, :], ACT.Square, scale=D ** -0.5,
                                     accum_out=ss[:, tt:tt + 1])
            last.then_inc(a_chain, 1)
            sc.wait_ge(a_chain, 2 * DEPTH + 1)
            sc.activation(rs[:, :], ss[:, :], ACT.Sqrt, bias=eps[:, :]).then_inc(a_sq, 1)
            for tt in range(NT):
                sc.wait_ge(v_fin, tt + 1)
                sc.dma_start(out[0, tt * P:(tt + 1) * P, :], xn[:, tt, :]).then_inc(s_out, 16)
            sc.wait_ge(s_out, 16 * NT)

        @block.vector
        def _(dv):
            first_credit(dv, DVE_SIGNALS)
            dv.sem_inc(v_layer, 1)
            dv.memset(eps[:, :], EPS)
            dv.memset(cpad[:, :, :], 0.0).then_inc(v_c, 1)
            dv.wait_ge(a_c, 1)
            dv.wait_ge(v_c, 1)
            dv.tensor_tensor(cpad[:, :, 0:1].rearrange("p k a -> p (k a)"), bank[0][:, 0:ND], stat[:, 0, 0:ND], ALU.mult)\
              .then_inc(v_c, 1)
            dv.wait_ge(s_start, 16 * N_START)

            count = [0]

            def rsqrt(link):
                link(dv.reciprocal(rs[:, :], rs[:, :]))
                link(dv.tensor_scalar(ss[:, :], ss[:, :], EPS, -0.5, ALU.add, ALU.mult))
                link(dv.tensor_tensor(ss[:, :], ss[:, :], rs[:, :], ALU.mult))
                link(dv.tensor_tensor(ss[:, :], ss[:, :], rs[:, :], ALU.mult))
                link(dv.scalar_tensor_tensor(rs[:, :], ss[:, :], 1.5, rs[:, :], ALU.add, ALU.mult))

            with dv.Fori(0, DEPTH) as L:
                def link(ins):
                    count[0] += 1
                    ins.then_inc(v_chain, 1)
                    dv.wait_ge(v_chain, L * N_CHAIN + count[0])

                dv.wait_ge(p_vec, L + 1)
                dv.tensor_copy(vT[:, :], bank[6][:, 0:R_ALL]).then_inc(v_vec, 1)
                dv.tensor_copy(bT[:, :], bank[6][:, P:P + 6 * ND]).then_inc(v_vec, 1)
                dv.tensor_copy(hvT[:, :], bank[6][0:FFN, 2 * P:2 * P + 4]).then_inc(v_vec, 1)
                dv.wait_ge(v_vec, (L + 1) * 3)
                u_, k_ = fu[0:FFN, :], fk[0:FFN, :]
                for s in range(3):
                    dv.wait_ge(p_fil, L * 3 + s + 1)
                    if s >= 1:
                        dv.wait_ge(a_fh, L * 3 + s)
                    link(dv.tensor_scalar(u_, bank[7][0:FFN, 0:SEQ], hvT[:, s:s + 1], hvT[:, 3:4], ALU.add, ALU.mult))
                    link(dv.tensor_scalar(k_, u_, INV2PI, MAGIC, ALU.mult, ALU.add))
                    link(dv.tensor_scalar(k_, k_, MAGIC, None, ALU.subtract))
                    link(dv.scalar_tensor_tensor(u_, k_, -TWOPI_HI, u_, ALU.mult, ALU.add))
                    link(dv.scalar_tensor_tensor(u_, k_, -TWOPI_LO, u_, ALU.mult, ALU.add))
                    dv.tensor_scalar(u_, u_, PI_SAFE, -PI_SAFE, ALU.min, ALU.max).then_inc(v_fu, 1)
                u = 0
                for b in range(2):
                    for lt in range(NT):
                        for n in range(2):
                            dv.wait_ge(p_kt, L * 8 + u + 1)
                            cols = slice(n * HW2, (n + 1) * HW2)
                            dv.tensor_tensor(kfb[b][:, lt, cols], bank[u % 4][:, 0:HW2], decay[:, b, lt, cols], ALU.mult)\
                              .then_inc(v_kt, 1)
                            u += 1
                dv.wait_ge(v_kt, L * 10 + 8)
                dv.tensor_tensor(decay[:, 0, :, :], kfb[0], kfb[1], ALU.add).then_inc(v_kt, 1)
                dv.tensor_tensor(decay[:, 1, :, :], kfb[0], kfb[1], ALU.subtract).then_inc(v_kt, 1)
                dv.wait_ge(a_ks, (L + 1) * 8)
                dv.wait_ge(p_ks, (L + 1) * 9)
                link(dv.tensor_copy(KX[:, :], Kr[:, 0, :]))
                for n in range(2):
                    last = dv.tensor_copy(KX[0:1, n * HW2:(n + 1) * HW2], bank[4 + n][0:1, 0:HW2])
                last.then_inc(v_kx, 1)
                dv.memset(Ks[0:1, 0, :], 0.0).then_inc(v_kx, 1)

                dv.wait_ge(s_gbias, (L + 1) * 32)
                for n in range(N_ADA):
                    def post(n):
                        if n // 2 in (2, 5):
                            q = (n // 2 == 5) * 2 + n % 2
                            g = g1b if n // 2 == 2 else g2b
                            dv.wait_ge(p_mod, L * N_ADA + n + 1)
                            dv.tensor_tensor(g[:, (n % 2) * W:(n % 2 + 1) * W], bank[5][:, :],
                                             g[:, (n % 2) * W:(n % 2 + 1) * W], ALU.add).then_inc(v_mod, 1)
                    dv.wait_ge(slots_free, L * N_BLOCKS + (RING + n + 1))
                    if n >= 2:
                        dv.wait_ge(p_mod, L * N_ADA + n - 1)
                    dv.tensor_copy(acc[:, n % 2, :], bank[n % 2][:, :]).then_inc(v_ada, 1)
                    if n >= 1:
                        post(n - 1)
                post(N_ADA - 1)
                for cols in (slice(0, 2 * ND), slice(3 * ND, 5 * ND)):
                    link(dv.tensor_tensor(modT[:, cols], bank[6][:, cols], bT[:, cols], ALU.add))
                link(dv.scalar_tensor_tensor(A1[:, :], modT[:, ND:2 * ND], 1.0, vT[:, R_N1:R_N1 + ND], ALU.add, ALU.mult))
                dv.scalar_tensor_tensor(A2[:, :], modT[:, 4 * ND:5 * ND], 1.0, vT[:, R_N2:R_N2 + ND],
                                        ALU.add, ALU.mult).then_inc(v_mod, 1)
                dv.wait_ge(v_mod, (L + 1) * 5)

                def norm(q, nsq):
                    dv.wait_ge(a_sq, nsq)
                    rsqrt(link)
                    for tt in range(NT):
                        last = dv.tensor_scalar(xn[:, tt, :], x[:, tt, :], rs[:, tt:tt + 1], None, ALU.mult)
                    return last

                def to_h(q, A, shift):
                    for j in range(4):
                        dv.wait_ge(p_tr, L * 8 + 4 * q + j + 1)
                        for k in (2 * j, 2 * j + 1):
                            last = dv.tensor_scalar(hT[:, k, :], bank[j][:, (k % 2) * SEQ:(k % 2 + 1) * SEQ],
                                                    A[:, k:k + 1], modT[:, shift + k:shift + k + 1], ALU.mult, ALU.add)
                        last.then_inc(v_hT, 1)

                norm(0, L * 2 + 1).then_inc(v_xn, 1)
                to_h(0, A1, 0)

                for c in range(NSC):
                    dv.wait_ge(a_u, L * NSC + c + 1)
                    dst = x0T[:, c, :] if c < NH_CH else zvT[:, c - NH_CH, :] if c < 2 * NH_CH else tmp[:, 0:SEQ]
                    src = bank[c % 4]
                    link(dv.scalar_tensor_tensor(dst[:, 1:SEQ], src[:, 0:SEQ - 1], vT[:, R_WSC + c:R_WSC + c + 1],
                                                 dst[:, 1:SEQ], ALU.mult, ALU.add))
                    w2c = R_WSC + 2 * NSC + c
                    last = dv.scalar_tensor_tensor(dst[:, 0:SEQ - 1], src[:, 1:SEQ], vT[:, w2c:w2c + 1],
                                                   dst[:, 0:SEQ - 1], ALU.mult, ALU.add)
                    if c >= 2 * NH_CH:
                        link(last)
                        z = zvT[:, c - 2 * NH_CH, :]
                        last = dv.tensor_tensor(z, z, dst, ALU.mult)
                    last.then_inc(v_u, 1)
                dv.wait_ge(v_u, (L + 1) * NSC)
                for g in range(2 * GROUPS):
                    dv.wait_ge(p_qk, L * 6 + g + 1)
                    dst = (qr if g < GROUPS else kr)[:, g % GROUPS, :, :]
                    src = bank[4 + g % 2]
                    tv = tmp.rearrange("p (x n) -> p x n", x=2)
                    for xx in range(2):
                        dv.tensor_tensor(dst[:, xx, :], src[:, xx * SEQ:(xx + 1) * SEQ], rcos, ALU.mult)
                    for xx in range(2):
                        last = dv.tensor_tensor(tv[:, xx, :], src[:, (1 - xx) * SEQ:(2 - xx) * SEQ],
                                                rsin[:, xx * SEQ:(xx + 1) * SEQ], ALU.mult)
                    link(last)
                    dv.tensor_tensor(dst, dst, tv, ALU.add).then_inc(v_qk, 1)
                    dv.wait_ge(v_qk, L * 6 + g + 1)
                dv.wait_ge(g_qm, L + 1)
                for h in range(HEADS):
                    g = h // HPG
                    if h % HPG == 0:
                        if h:
                            dv.wait_ge(p_s, L * HEADS + h)
                        for hh in range(HPG):
                            rows = slice(hh * HALF, (hh + 1) * HALF)
                            last = dv.tensor_copy(qm[rows, :, hh, :], qr[rows, g, :, :])
                        last.then_inc(v_qm, 1)
                    dv.wait_ge(p_s, L * HEADS + h + 1)
                    if h:
                        dv.wait_ge(p_pt, L * HEADS + h)
                    settle(dv)
                    for qt in range(NT):
                        last = dv.tensor_tensor_reduce(out=sm[:, qt, :], in0=bank[h % 2][:, qt * SEQ:(qt + 1) * SEQ],
                                                       in1=mask(g, qt), scale=1.0, scalar=-3e38, op0=ALU.add, op1=ALU.max,
                                                       accum_out=stat[:, 0, h * NT + qt:h * NT + qt + 1])
                    link(last)
                    dv.tensor_scalar(stat[:, 2, h * NT:(h + 1) * NT], stat[:, 0, h * NT:(h + 1) * NT], -SCALE, None,
                                     ALU.mult).then_inc(v_s, 1)
                n8 = HPG * NT
                m_ = stat[:, 0, 0:GROUPS * n8].rearrange("p (g a) -> p g a", g=GROUPS)
                d_ = stat[:, 3, 0:GROUPS * n8].rearrange("p (g a) -> p g a", g=GROUPS)
                e_ = stat[:, 4, 0:GROUPS * n8].rearrange("p (g a) -> p g a", g=GROUPS)
                s_ = stat[:, 1, 0:GROUPS * n8].rearrange("p (g a) -> p g a", g=GROUPS)
                w_ = stat[:, 5, 0:GROUPS * n8].rearrange("p (g a) -> p g a", g=GROUPS)
                M_ = stat[:, 6, 0:n8]
                dv.wait_ge(v_s, (L + 1) * HEADS)
                link(dv.tensor_tensor(M_, m_[:, 0, :], m_[:, 1, :], ALU.max))
                link(dv.tensor_tensor(M_, M_, m_[:, 2, :], ALU.max))
                for g in range(GROUPS):
                    last = dv.tensor_tensor(d_[:, g, :], m_[:, g, :], M_, ALU.subtract)
                last.then_inc(v_md, 1)
                dv.wait_ge(a_me, L + 1)
                dv.wait_ge(a_p, (L + 1) * HEADS)
                link(dv.tensor_scalar(stat[:, 1, 0:GROUPS * n8], stat[:, 1, 0:GROUPS * n8], 1e-30, None, ALU.max))
                link(dv.tensor_tensor(stat[:, 5, 0:GROUPS * n8], stat[:, 4, 0:GROUPS * n8],
                                      stat[:, 1, 0:GROUPS * n8], ALU.mult))
                link(dv.tensor_tensor(M_, w_[:, 0, :], w_[:, 1, :], ALU.add))
                link(dv.tensor_tensor(M_, M_, w_[:, 2, :], ALU.add))
                link(dv.reciprocal(M_, M_))
                for g in range(GROUPS):
                    last = dv.tensor_tensor(w_[:, g, :], e_[:, g, :], M_, ALU.mult)
                link(last)
                dv.wait_ge(p_o, (L + 1) * HEADS)
                for qt in range(NT):
                    for g in range(GROUPS):
                        for hh in range(HPG):
                            h = g * HPG + hh
                            o = bank[4 + 2 * qt + h // 8][:, (h % 8) * HD:(h % 8 + 1) * HD]
                            dst = yat[:, qt, hh * HD:(hh + 1) * HD]
                            wq = w_[:, g, hh * NT + qt:hh * NT + qt + 1]
                            if g == 0:
                                last = dv.tensor_scalar(dst, o, wq, None, ALU.mult)
                            else:
                                last = dv.scalar_tensor_tensor(dst, o, wq, dst, ALU.mult, ALU.add)
                        if g < GROUPS - 1:
                            link(last)
                last.then_inc(v_yat, 1)
                u = 0
                for m in range(2):
                    for n in range(2):
                        dv.wait_ge(p_z, L * 4 + u + 1)
                        if u:
                            dv.wait_ge(v_z, L * 4 + u)
                        cols = slice(n * HW2, (n + 1) * HW2)
                        zr, zs = bank[2 * (u % 2)][:, 0:HW2], bank[2 * (u % 2) + 1][:, 0:HW2]
                        kx = KX[:, cols] if m == 0 else Kr[:, 1, cols]
                        dv.tensor_tensor(ct[0], zr, Kr[:, m, cols], ALU.mult)
                        dv.tensor_tensor(ct[1], zs, Ks[:, m, cols], ALU.mult)
                        dv.tensor_tensor(ct[2], zr, Ks[:, m, cols], ALU.mult)
                        link(dv.tensor_tensor(ct[3], zs, kx, ALU.mult))
                        dv.tensor_tensor(Yr[:, m, cols], ct[0], ct[1], ALU.subtract)
                        dv.tensor_tensor(Ys[:, m, cols], ct[2], ct[3], ALU.add).then_inc(v_z, 1)
                        u += 1
                for c in range(NH_CH):
                    dv.wait_ge(p_y, L * NH_CH + c + 1)
                    link(dv.scalar_tensor_tensor(zvT[:, c, :], zvT[:, c, :], vT[:, R_HYB + c:R_HYB + c + 1],
                                                 bank[4 + c % 4][:, 0:SEQ], ALU.mult, ALU.add))
                    dv.tensor_tensor(x0T[:, c, :], x0T[:, c, :], zvT[:, c, :], ALU.mult).then_inc(v_y, 1)
                for q in range(4):
                    for tt in range(NT):
                        dv.wait_ge(a_gate, L * 8 + 2 * q + tt + 1)
                        dv.wait_ge(p_br, L * 8 + 2 * q + tt + 1)
                        cols = slice((q % 2) * W, (q % 2 + 1) * W)
                        if q < 2:
                            dv.tensor_tensor(merged[:, tt, cols], bank[2 + tt][:, :], sg[:, q % 2, tt, :], ALU.mult)\
                              .then_inc(v_br, 1)
                        else:
                            link(dv.tensor_tensor(mtmp, bank[2 + tt][:, :], sg[:, q % 2, tt, :], ALU.mult))
                            dv.tensor_tensor(merged[:, tt, cols], merged[:, tt, cols], mtmp, ALU.add).then_inc(v_br, 1)
                            dv.wait_ge(v_br, L * 8 + 2 * q + tt + 1)
                for n in range(2):
                    for tt in range(NT):
                        dv.wait_ge(p_wo, L * 4 + 2 * n + tt + 1)
                        cols = slice(n * W, (n + 1) * W)
                        link(dv.tensor_tensor(mtmp, bank[2 * n + tt][:, :], g1b[:, cols], ALU.mult))
                        link_last = dv.tensor_tensor(x[:, tt, cols], x[:, tt, cols], mtmp, ALU.add)
                        link_last.then_inc(v_wo, 1)
                        dv.wait_ge(v_wo, L * 4 + 2 * n + tt + 1)
                norm(1, L * 2 + 2).then_inc(v_xn, 1)
                to_h(1, A2, 3 * ND)
                link(dv.memset(yacc, 0.0))
                dv.wait_ge(a_lg, L + 1)
                for tt in range(NT):
                    last = dv.tensor_tensor(rb[biased][:, tt, :], rb[score][:, tt, :], rbias[:, :], ALU.add)
                link(last)
                b4, p4, q4 = g4[biased], g4[pair], g4[tA]
                for tt in range(NT):
                    dv.tensor_tensor(p4[:, tt, :, 0:3], b4[:, tt, :, 0:3], b4[:, tt, :, 1:4], ALU.add)
                    dv.tensor_tensor(p4[:, tt, :, 3:4], b4[:, tt, :, 0:1], b4[:, tt, :, 3:4], ALU.add)
                    last = dv.tensor_tensor(q4[:, tt, :, 0:2], b4[:, tt, :, 0:2], b4[:, tt, :, 2:4], ALU.add)
                link(last)
                gs = rt[tB][:, 0:NT * NG]
                gs2 = rt[tB][:, NT * NG:2 * NT * NG]
                dv.tensor_reduce(gs, rt[pair].rearrange("p (a e) -> p a e", e=EPG), AX.X, ALU.max)
                link(dv.tensor_reduce(gs2, rt[tA].rearrange("p (a e) -> p a e", e=EPG)[:, :, 0:2], AX.X, ALU.max))
                link(dv.tensor_tensor(gs, gs, gs2, ALU.max))

                def first_max(dst, src, width, mx, key):
                    link(dv.tensor_reduce(mx, src, AX.X, ALU.max))
                    for tt in range(NT):
                        last = dv.scalar_tensor_tensor(key[:, tt, :], src[:, tt, :], mx[:, tt:tt + 1],
                                                       desc[:, 0:width], ALU.is_equal, ALU.mult)
                    link(last)
                    link(dv.tensor_reduce(mx, key, AX.X, ALU.max))
                    for tt in range(NT):
                        last = dv.tensor_scalar(dst[:, tt, :], key[:, tt, :], mx[:, tt:tt + 1], None, ALU.is_equal)
                    link(last)

                mx = stat[:, 7, 0:NT]
                gsv = gs.rearrange("p (t g) -> p t g", t=NT)
                gk = rt[tC][:, 0:NT * NG].rearrange("p (t g) -> p t g", t=NT)
                gm = rt[tC][:, NT * NG:2 * NT * NG]
                first_max(gm.rearrange("p (t g) -> p t g", t=NT), gsv, NG, mx, gk)
                gmv = gm.rearrange("p (t g) -> p t g", t=NT)
                for e in range(EPG):
                    dv.tensor_tensor(g4[tA][:, :, :, e], g4[biased][:, :, :, e], gmv, ALU.mult)
                    last = dv.tensor_scalar(g4[pair][:, :, :, e], gmv, 1.0, -NEG, ALU.subtract, ALU.mult)
                link(last)
                link(dv.tensor_tensor(rt[tA], rt[tA], rt[pair], ALU.add))
                first_max(rb[oh1], rb[tA], NE, mx, rb[tD])
                link(dv.scalar_tensor_tensor(rt[tA], rt[oh1], 3.0 * NEG, rt[tA], ALU.mult, ALU.add))
                first_max(rb[oh2], rb[tA], NE, mx, rb[tD])
                dv.tensor_tensor(rt[oh], rt[oh1], rt[oh2], ALU.add).then_inc(v_oh, 1)
                dv.wait_ge(v_oh, L + 1)
                link(dv.tensor_tensor(rt[gate_], rt[oh], rt[score], ALU.mult))
                link(dv.tensor_reduce(mx, rb[gate_], AX.X, ALU.add))
                link(dv.reciprocal(mx, mx))
                for tt in range(NT):
                    last = dv.tensor_scalar(rb[gate_][:, tt, :], rb[gate_][:, tt, :], mx[:, tt:tt + 1], None, ALU.mult)
                link(last)
                dv.wait_ge(p_pos, L + 1)
                link(dv.scalar_tensor_tensor(rt[pos_], bank[5][:, 0:NT * NE], 1.0, rt[oh], ALU.add, ALU.mult))
                link(dv.tensor_scalar(rt[pos_], rt[pos_], 1.0, None, ALU.subtract))
                link(dv.tensor_copy(rt[tE][:, 0:NE], bank[5][:, 2 * NE:3 * NE]))
                dv.tensor_reduce(cnt_i[:, :], rt[tE][:, 0:NE].rearrange("p (a e) -> p a e", e=2), AX.X, ALU.max)\
                  .then_inc(v_rt, 1)
                dv.wait_ge(v_rt, L + 1)
                settle(dv)

                def expert_block(at, sems_link, base, first):
                    k = [0]

                    def blink(ins):
                        k[0] += 1
                        ins.then_inc(sems_link, 1)
                        dv.wait_ge(sems_link, base + k[0])

                    if not first:
                        blink(dv.tensor_scalar(posc, posc, float(CAP), None, ALU.subtract))
                    for tt in range(NT):
                        for j in range(2):
                            cols = slice(j * CAP, (j + 1) * CAP)
                            dv.tensor_scalar(sel[:, tt, cols], iota, posc[:, tt, j:j + 1], None, ALU.is_equal)
                            last = dv.tensor_scalar(selg[:, tt, cols], iota, posc[:, tt, j:j + 1],
                                                    gatec[:, tt, j:j + 1], ALU.is_equal, ALU.mult)
                    last.then_inc(at.s["v_sel"], 1)
                    at.wait(dv, "p_hg")
                    for kk in range(4, ND):
                        last = dv.tensor_scalar(hg[:, kk, :], bank[3][:, (kk - 4) * P:(kk - 3) * P], A2[:, kk:kk + 1],
                                                modT[:, 3 * ND + kk:3 * ND + kk + 1], ALU.mult, ALU.add)
                    last.then_inc(at.s["v_hg"], 1)
                    at.wait(dv, "a_sil")
                    dv.tensor_tensor(act, bank[1][:, :], sil, ALU.mult).then_inc(at.s["v_act"], 1)
                    at.wait(dv, "p_down")
                    dv.tensor_copy(yS[:, W:2 * W], bank[7][:, :]).then_inc(at.s["v_yS"], 1)
                    for tt in range(NT):
                        for n in range(2):
                            cols = slice(n * W, (n + 1) * W)
                            at.wait(dv, "p_sc", 2 * tt + n + 1)
                            dv.tensor_tensor(yacc[:, tt, cols], yacc[:, tt, cols], bank[2 + 2 * tt + n][:, :], ALU.add)\
                              .then_inc(at.s["v_acc"], 1)
                    at.wait(dv, "v_acc")
                    settle(dv)
                    assert k[0] == (0 if first else 1)

                with dv.Fori(0, PAIRS) as pr:
                    n = dv.value_load(cnt_i[0:1, bass.ds(pr, 1)], min_val=0, max_val=SEQ)
                    run = L * PAIRS + pr
                    for tt in range(NT):
                        dv.tensor_copy(posc[:, tt, :], rb[pos_][:, tt, bass.ds(pr * 2, 2)])
                        last = dv.tensor_copy(gatec[:, tt, :], rb[gate_][:, tt, bass.ds(pr * 2, 2)])
                    last.then_inc(v_moe, 1)
                    dv.wait_ge(v_moe, run + 1)
                    expert_block(At(main, run), None, None, True)
                    with dv.If(n <= CAP):
                        skip(dv, DVE_SIGNALS, At(ovf, run * EXTRA), EXTRA)
                        dv.sem_inc(v_ovf, EXTRA)
                    with dv.Else():
                        with dv.Fori(0, EXTRA) as b:
                            with dv.If(n > b * CAP + CAP):
                                ob = run * EXTRA + b
                                expert_block(At(ovf, ob), v_ovf, ob, False)
                            with dv.Else():
                                skip(dv, DVE_SIGNALS, At(ovf, run * EXTRA + b), 1)
                                dv.sem_inc(v_ovf, 1)
                for tt in range(NT):
                    link(dv.tensor_tensor(yacc[:, tt, :], yacc[:, tt, :], g2b[:, :], ALU.mult))
                    last = dv.tensor_tensor(x[:, tt, :], x[:, tt, :], yacc[:, tt, :], ALU.add)
                last.then_inc(v_layer, 1)
                assert count[0] == N_CHAIN, count[0]
            L = DEPTH
            dv.wait_ge(a_sq, 2 * DEPTH + 1)

            def link_end(ins):
                count[0] += 1
                ins.then_inc(v_chain, 1)
                dv.wait_ge(v_chain, (DEPTH - 1) * N_CHAIN + count[0])

            rsqrt(link_end)
            dv.wait_ge(s_fing, 16)
            for tt in range(NT):
                dv.scalar_tensor_tensor(xn[:, tt, :], x[:, tt, :], rs[:, tt:tt + 1], fing, ALU.mult, ALU.mult)\
                  .then_inc(v_fin, 1)


_INS = ["x", "c", "norm1_g", "norm2_g", "w_ada", "b_ada", "w_in", "w_sc", "b_sc", "hf_w1", "hf_b1", "hf_w2", "hf_b2",
        "hf_w3", "hf_b3", "hf_w4", "hf_freq", "hy_bias", "w_br_h", "w_br_a", "w_out", "router_w", "router_bias",
        "moe_w1", "moe_w3", "moe_w2", "final_g"]


def kernel(**inputs):
    import concourse.bacc as _bacc
    from concourse.bass_utils import run_bass_kernel_spmd as _run

    nc = _bacc.Bacc("TRN2", target_bir_lowering=False, num_devices=1)
    arrays, t = {}, {}
    for name in _INS:
        a = np.ascontiguousarray(inputs[name])
        arrays[f"in_{name}_dram"] = a
        t[name] = nc.dram_tensor(f"in_{name}_dram", a.shape, mybir.dt.from_np(a.dtype), kind="ExternalInput").ap()
    for name, a in zip(("cst", "decay", "zpos"), constants()):
        arrays[f"in_{name}_dram"] = a
        t[name] = nc.dram_tensor(f"in_{name}_dram", a.shape, F32, kind="ExternalInput").ap()
    out = nc.dram_tensor("out_0_dram", (1, SEQ, D), F32, kind="ExternalOutput").ap()
    trunk_kernel(nc, t, out)
    r = _run(nc, [arrays], core_ids=[0])
    return r.results[0]["out_0_dram"]
```

```python
from contextlib import ExitStack

import numpy as np

import concourse.bass as bass
from concourse import mybir

F32 = mybir.dt.float32
I32 = mybir.dt.int32
ALU = mybir.AluOpType
ACT = mybir.ActivationFunctionType
AX = mybir.AxisListType

P = 128
D = 1024
SEQ = 256
DEPTH = 2
NT = SEQ // P
ND = D // P
HY = 768
NH_CH = HY // P
NSC = 3 * NH_CH
EMB = 33
FFN = 64
HD = 64
HALF = HD // 2
GROUPS = 3
HPG = 4
HEADS = GROUPS * HPG
GW = HPG * HD
RADIUS = 64
DILATION = (1, 4, 16)
NE = 16
NG = 4
EPG = NE // NG
FE = 512
NF = FE // P
EPS = 1e-6
NEG = -1e30
CAP = 64
EXTRA = SEQ // CAP - 1
PAIRS = NE // 2
W = 512
HW2 = HY // 2
SCALE = HD ** -0.5

N_ADA = 6 * D // W
IN_A = 9
N_EARLY = 4
N_HEAD = N_ADA + IN_A + 7 + 2
BPP = 6
N_BLOCKS = N_HEAD + BPP * PAIRS
RING = 6
PER_SLOT = N_BLOCKS // RING
assert N_BLOCKS % RING == 0 and N_HEAD % RING == 0

C_ID = 0
C_CT = C_ID + P
C_ST = C_CT + NT * SEQ
C_IC = C_ST + NT * SEQ
C_IS = C_IC + NT * SEQ
C_COS = C_IS + NT * SEQ
C_SIN = C_COS + SEQ
C_MASK = C_SIN + 2 * SEQ
C_TRI = C_MASK + (NT + 2) * SEQ
C_ONE = C_TRI + P
C_IOTA = C_ONE + P
C_DESC = C_IOTA + CAP
C_ALL = C_DESC + NE

R_N1 = 0
R_N2 = R_N1 + ND
R_WSC = R_N2 + ND
R_BSC = R_WSC + 3 * NSC
R_HYB = R_BSC + NSC
R_ALL = R_HYB + NH_CH

INV2PI = float(np.float32(1.0 / (2.0 * np.pi)))
MAGIC = 1.5 * 2.0 ** 23
N_START = 6
N_SMALL = 14
N_CHAIN = 129

TWOPI_HI = 6.28125
TWOPI_LO = float(2.0 * np.pi - 6.28125)
PI_SAFE = 3.1415925


def constants():
    f64 = np.float64
    tab = np.zeros((P, C_ALL), f64)
    tab[:, C_ID:C_ID + P] = np.eye(P)
    tok = np.arange(SEQ)
    fr = np.arange(SEQ)
    cos = np.cos(2 * np.pi * ((tok[:, None] * fr[None, :]) % (2 * SEQ)) / (2 * SEQ))
    sin = np.sin(2 * np.pi * ((tok[:, None] * fr[None, :]) % (2 * SEQ)) / (2 * SEQ))
    sin[:, 0] = (-1.0) ** tok
    wt = np.full(SEQ, 2.0)
    wt[0] = 1.0
    for t in range(NT):
        rows = slice(t * P, (t + 1) * P)
        tab[:, C_CT + t * SEQ:C_CT + (t + 1) * SEQ] = cos[rows]
        tab[:, C_ST + t * SEQ:C_ST + (t + 1) * SEQ] = sin[rows]
        tab[:, C_IC + t * SEQ:C_IC + (t + 1) * SEQ] = (cos * wt).T[rows] / (2 * SEQ)
        tab[:, C_IS + t * SEQ:C_IS + (t + 1) * SEQ] = (sin * wt).T[rows] / (2 * SEQ)
    f32 = np.float32
    inv = f32(10000.0) ** (-np.arange(HALF, dtype=f32) / f32(HALF))
    ang = (tok.astype(f32)[None, :] * inv[:, None]).astype(f64)
    tab[:, C_COS:C_COS + SEQ] = np.tile(np.cos(ang), (P // HALF, 1))
    tab[:, C_SIN:C_SIN + SEQ] = -np.tile(np.sin(ang), (P // HALF, 1))
    tab[:, C_SIN + SEQ:C_SIN + 2 * SEQ] = np.tile(np.sin(ang), (P // HALF, 1))
    for t in range(NT):
        q = t * P + np.arange(P)
        tab[:, C_MASK + t * SEQ:C_MASK + (t + 1) * SEQ] = np.where(np.abs(q[:, None] - tok[None, :]) <= RADIUS, 0, NEG)
    for n, dil in enumerate(DILATION[1:]):
        q = np.arange(P)
        c = C_MASK + (NT + n) * SEQ
        tab[:, c:c + SEQ] = np.where((q[:, None] - tok[None, :]) % dil == 0, 0, NEG)
    tab[:, C_TRI:C_TRI + P] = np.triu(np.ones((P, P)), 1)
    tab[:, C_ONE:C_ONE + P] = 1.0
    tab[:, C_IOTA:C_IOTA + CAP] = np.arange(CAP)
    tab[:, C_DESC:C_DESC + NE] = NE - np.arange(NE)
    t = np.linspace(0.0, 1.0, SEQ, dtype=f32).astype(f64)
    deltas = np.linspace(np.log(1e-2) / 1.5, np.log(1e-2) / 0.3, HY, dtype=f32).astype(f64)
    dec = np.exp(-t[:, None] * np.abs(deltas)[None, :])
    dec_b = dec.copy()
    dec_b[0] = 0.0
    decay = np.stack([dec.reshape(NT, P, HY), dec_b.reshape(NT, P, HY)]).transpose(2, 0, 1, 3)
    bands = (EMB - 1) // 2
    ww = (f32(2.0 * np.pi) * tok.astype(f32)[:, None] / f32(SEQ))
    ff = np.linspace(1e-4, bands - 1, bands, dtype=f32)[None, :]
    zz = np.concatenate([t[:, None], np.cos((ff * ww).astype(f64)), -np.sin((ff * ww).astype(f64))], axis=1)
    return (tab.astype(f32), np.ascontiguousarray(decay.astype(f32)), np.ascontiguousarray(zz.T.astype(f32)))


def trunk_kernel(nc, t, out):
    with ExitStack() as ctx:
        def sb(name, shape, dt=F32):
            return ctx.enter_context(nc.sbuf_tensor(name, shape, dt))

        def sem(name):
            return ctx.enter_context(nc.semaphore(name))

        ring = [sb(f"ring{r}", [P, 8 * W]) for r in range(RING)]
        cst = sb("cst", [P, C_ALL])
        x = sb("x", [P, NT, D])
        xn = sb("xn", [P, NT, D])
        hT = sb("hT", [P, ND, SEQ])
        g1b = sb("g1b", [P, D])
        g2b = sb("g2b", [P, D])
        Kr = sb("Kr", [P, 2, HY])
        Ks = sb("Ks", [P, 2, HY])
        KX = sb("KX", [P, HY])
        x0T = sb("x0T", [P, NH_CH, SEQ])
        zvT = sb("zvT", [P, NH_CH, SEQ])
        router = sb("router", [P, ND, NE])
        rbias = sb("rbias", [P, NE])
        cpad = sb("cpad", [P, ND, 32])
        vrow = sb("vrow", [P, P])
        brow = sb("brow", [6 * ND, P])
        hrow = sb("hrow", [4, FFN])
        vT = sb("vT", [P, R_ALL])
        bT = sb("bT", [P, 6 * ND])
        hvT = sb("hvT", [FFN, 4])
        modT = sb("modT", [P, 6 * ND])
        A1 = sb("A1", [P, ND])
        A2 = sb("A2", [P, ND])
        hw1 = sb("hw1", [EMB, FFN])
        hw2 = sb("hw2", [FFN, FFN])
        hw3 = sb("hw3", [FFN, FFN])
        ss = sb("ss", [P, NT])
        rs = sb("rs", [P, NT])
        eps = sb("eps", [P, 1])
        stat = sb("stat", [P, 12, 32])
        crow = stat[0:ND, 8:12, :].rearrange("k a b -> k (a b)")
        yatT = sb("yatT", [P, 2, SEQ])
        cnt_i = sb("cnt_i", [P, PAIRS], I32)
        AREA = 6656
        area = sb("area", [P, AREA])

        cut = [0]

        def region(size):
            a = area[:, cut[0]:cut[0] + size]
            cut[0] += size
            assert cut[0] <= AREA, cut[0]
            return a

        decay = region(2 * NT * HY).rearrange("p (b t c) -> p b t c", b=2, t=NT)
        kfb = [a[:, :, :].rearrange("p k n -> p (k n)").rearrange("p (t c) -> p t c", t=NT) for a in (x0T, zvT)]
        fu = region(SEQ)
        fk = region(SEQ)
        fh = region(SEQ)
        zpos = yatT[:, 0, :]
        hw4 = xn[:, :, :].rearrange("p t d -> p (t d)")[0:FFN, 0:2 * HY]
        cut[0] = 0
        qr = region(GROUPS * 2 * SEQ).rearrange("p (g x n) -> p g x n", g=GROUPS, x=2)
        kr = region(GROUPS * 2 * SEQ).rearrange("p (g x n) -> p g x n", g=GROUPS, x=2)
        vv = region(NT * HY).rearrange("p (t n) -> p t n", t=NT)
        qm = xn[:, :, :].rearrange("p t d -> p (t d)").rearrange("p (x h n) -> p x h n", x=2, h=HPG)
        sm_0 = region(2 * SEQ).rearrange("p (t n) -> p t n", t=NT)
        tmp = region(2 * SEQ)
        sm = [sm_0, tmp.rearrange("p (t n) -> p t n", t=NT)]
        acc = area[:, cut[0]:cut[0] + 2 * W].rearrange("p (b n) -> p b n", b=2)
        pT = region(2 * SEQ).rearrange("p (t n) -> p t n", t=NT)
        yat = region(NT * GW).rearrange("p (t n) -> p t n", t=NT)
        cut[0] = 0
        ztok = region(NT * HY).rearrange("p (t c) -> p t c", t=NT)
        Yr = region(2 * HY).rearrange("p (m c) -> p m c", m=2)
        Ys = region(2 * HY).rearrange("p (m c) -> p m c", m=2)
        ct = [region(HW2) for _ in range(4)]
        cut[0] = 0
        merged = region(NT * D).rearrange("p (t d) -> p t d", t=NT)
        mT = xn[:, :, :].rearrange("p t d -> p (t d)").rearrange("p (k n) -> p k n", k=ND)
        sg = region(2 * NT * W).rearrange("p (b t n) -> p b t n", b=2, t=NT)
        mtmp = region(W)
        cut[0] = 0
        yacc = region(NT * D).rearrange("p (t d) -> p t d", t=NT)
        hg = hT[:, :, 0:P]
        hg_x = hT[:, :, P:2 * P]
        sel = region(NT * P).rearrange("p (t s) -> p t s", t=NT)
        selg = region(NT * P).rearrange("p (t s) -> p t s", t=NT)
        selT = region(SEQ)
        sil = region(FE)
        act = region(FE)
        actT = region(FE).rearrange("p (f s) -> p f s", f=NF)
        yS = region(D)
        posc = region(NT * 2).rearrange("p (t j) -> p t j", t=NT)
        gatec = region(NT * 2).rearrange("p (t j) -> p t j", t=NT)
        rt_at = cut[0]
        rt = [region(NT * NE) for _ in range(13)]
        rb = [r.rearrange("p (t e) -> p t e", t=NT) for r in rt]
        g4 = [r.rearrange("p (t g e) -> p t g e", t=NT, g=NG) for r in rt]
        score, biased, pair, tA, tB, oh1, oh2, oh, tC, tD, gate_, pos_, tE = range(13)

        def row(i, tt):
            a = rt_at + (i * NT + tt) * NE
            return area[:, a:a + NE + 2]

        Krf = Kr[:, :, :].rearrange("p m c -> p (m c)")
        yS_x = Krf[:, 0:D]
        selT_x = Krf[:, D:D + SEQ]
        posc_x = Krf[:, D + SEQ:D + SEQ + 2 * NT].rearrange("p (t j) -> p t j", t=NT)
        gatec_x = Krf[:, D + SEQ + 2 * NT:D + SEQ + 4 * NT].rearrange("p (t j) -> p t j", t=NT)
        sel_x = KX[:, 0:NT * P].rearrange("p (t s) -> p t s", t=NT)
        selg_x = KX[:, NT * P:2 * NT * P].rearrange("p (t s) -> p t s", t=NT)
        buf_m = (sel, selg, selT, yS, posc, gatec, hg)
        buf_x = (sel_x, selg_x, selT_x, yS_x, posc_x, gatec_x, hg_x)
        fing = g1b[:, :]

        bank = [ctx.enter_context(nc.psum_tensor(f"bank{i}", [P, 512], F32)) for i in range(8)]

        ident = cst[:, C_ID:C_ID + P]
        ctab = cst[:, C_CT:C_CT + NT * SEQ].rearrange("p (t f) -> p t f", t=NT)
        stab = cst[:, C_ST:C_ST + NT * SEQ].rearrange("p (t f) -> p t f", t=NT)
        ictab = cst[:, C_IC:C_IC + NT * SEQ].rearrange("p (t f) -> p t f", t=NT)
        istab = cst[:, C_IS:C_IS + NT * SEQ].rearrange("p (t f) -> p t f", t=NT)
        rcos = cst[:, C_COS:C_COS + SEQ]
        rsin = cst[:, C_SIN:C_SIN + 2 * SEQ]
        tri = cst[:, C_TRI:C_TRI + P]
        ones = cst[:, C_ONE:C_ONE + P]
        iota = cst[:, C_IOTA:C_IOTA + CAP]
        desc = cst[:, C_DESC:C_DESC + NE]

        def mask(g, qt):
            c = C_MASK + (qt if g == 0 else NT + g - 1) * SEQ
            return cst[:, c:c + SEQ]

        slot_in = [sem(f"slot_in{r}") for r in range(RING)]
        slots_free = sem("slots_free")
        s_start = sem("s_start")
        s_small = sem("s_small")
        s_filter = sem("s_filter")
        s_gbias = sem("s_gbias")
        s_out = sem("s_out")
        s_fing = sem("s_fing")
        v_chain = sem("v_chain")
        v_ovf = sem("v_ovf")
        a_chain = sem("a_chain")
        p_c = sem("p_c")
        v_c = sem("v_c")
        a_c = sem("a_c")
        p_vec = sem("p_vec")
        v_vec = sem("v_vec")
        v_ada = sem("v_ada")
        p_mod = sem("p_mod")
        v_mod = sem("v_mod")
        v_A1 = sem("v_A1")
        v_A2 = sem("v_A2")
        p_fil = sem("p_fil")
        v_fu = sem("v_fu")
        a_fh = sem("a_fh")
        p_kt = sem("p_kt")
        v_kt = sem("v_kt")
        p_ks = sem("p_ks")
        a_ks = sem("a_ks")
        v_kx = sem("v_kx")
        a_sq = sem("a_sq")
        v_xn = sem("v_xn")
        p_tr = sem("p_tr")
        v_hT = sem("v_hT")
        p_u = sem("p_u")
        a_u = sem("a_u")
        v_u = sem("v_u")
        p_qk = sem("p_qk")
        v_qk = sem("v_qk")
        p_v = sem("p_v")
        a_v = sem("a_v")
        g_qm = sem("g_qm")
        v_qm = sem("v_qm")
        p_s = sem("p_s")
        v_s = sem("v_s")
        a_p = sem("a_p")
        p_pt = sem("p_pt")
        a_pt = sem("a_pt")
        p_o = sem("p_o")
        v_md = sem("v_md")
        a_me = sem("a_me")
        v_yat = sem("v_yat")
        p_yat = sem("p_yat")
        a_yat = sem("a_yat")
        p_zt = sem("p_zt")
        a_zt = sem("a_zt")
        p_z = sem("p_z")
        v_z = sem("v_z")
        p_y = sem("p_y")
        v_y = sem("v_y")
        p_gate = sem("p_gate")
        a_gate = sem("a_gate")
        p_br = sem("p_br")
        v_br = sem("v_br")
        p_mt = sem("p_mt")
        a_mt = sem("a_mt")
        p_wo = sem("p_wo")
        v_wo = sem("v_wo")
        p_lg = sem("p_lg")
        a_lg = sem("a_lg")
        v_oh = sem("v_oh")
        p_pos = sem("p_pos")
        v_rt = sem("v_rt")
        v_layer = sem("v_layer")
        v_fin = sem("v_fin")

        def block_sems(tag):
            return {n: sem(f"{n}_{tag}") for n in (
                "v_pos", "v_sel", "p_selT", "p_hg", "a_selT", "a_hg", "v_hg", "p_up", "a_sil", "v_act", "p_actT", "a_actT",
                "p_down", "a_yS", "v_yS", "p_sc", "v_acc")}

        def skip(eng, signals, at, times):
            for name, k in signals.items():
                at.wait_before(eng, name)
                eng.sem_inc(at.s[name], times * k)

        def first_credit(eng, signals):
            for sems in (main, ovf):
                for name in signals:
                    eng.sem_inc(sems[name], CREDIT)

        CREDIT = 4
        main = block_sems("m")
        ovf = block_sems("x")
        PE_SIGNALS = {"p_selT": 1, "p_hg": 2, "p_up": 2, "p_actT": 1, "p_down": 2, "p_sc": 4}
        ACT_SIGNALS = {"a_selT": 1, "a_hg": 1, "a_sil": 1, "a_actT": 1, "a_yS": 1}
        DVE_SIGNALS = {"v_pos": 1, "v_sel": 1, "v_hg": 1, "v_act": 1, "v_yS": 1, "v_acc": 4}
        SIGNALS = {**PE_SIGNALS, **ACT_SIGNALS, **DVE_SIGNALS}

        class At:
            def __init__(self, sems, n):
                self.s, self.n = sems, n

            def wait(self, eng, name, k=None):
                k = SIGNALS[name] if k is None else k
                eng.wait_ge(self.s[name], self.n * SIGNALS[name] + (k + CREDIT))

            def wait_before(self, eng, name):
                eng.wait_ge(self.s[name], self.n * SIGNALS[name] + CREDIT)

        stream = [("ada", b) for b in range(N_EARLY)]
        for c in range(NSC):
            if c % 4 == 3:
                stream.append(("in", c // 4))
            if c % 2 and c // 2 < N_ADA - N_EARLY:
                stream.append(("ada", N_EARLY + c // 2))
        stream += [("in", b) for b in range(NSC // 4, IN_A)]
        stream += [("in", 9), ("brh", 0), ("in", 10), ("brh", 1), ("in", 11), ("in", 12), ("bra", 0), ("out", 0), ("out", 1)]
        assert len(stream) == N_HEAD
        at_ = {key: n for n, key in enumerate(stream)}

        s_settled = sem("s_settled")

        def settle(eng):
            eng.sem_inc(s_settled, 1)

        block = ctx.enter_context(nc.Block())

        @block.sync
        def _(sp):
            sp.sem_inc(slots_free, RING)
            sp.wait_ge(s_start, 16 * N_START)
            sp.wait_ge(s_small, 16 * N_SMALL)
            with sp.Fori(0, DEPTH) as L:
                def load(n, dst, src):
                    sp.wait_ge(slots_free, L * N_BLOCKS + (n + 1))
                    sp.dma_start(dst, src).then_inc(slot_in[n % RING], 16)

                for n, (kind, b) in enumerate(stream):
                    if n == N_EARLY:
                        sp.wait_ge(s_filter, (L + 1) * 32)
                        sp.sem_inc(s_settled, 1)
                    if kind == "bra":
                        load(n, ring[n % RING][:, 0:2 * D].rearrange("p (k f) -> p k f", f=D),
                             t["w_br_a"][L, :, :].rearrange("(k p) f -> p k f", p=P))
                    elif kind == "brh":
                        load(n, ring[n % RING][:, 0:NH_CH * W].rearrange("p (k f) -> p k f", f=W),
                             t["w_br_h"][L, :, b * W:(b + 1) * W].rearrange("(k p) f -> p k f", p=P))
                    else:
                        src = {"ada": t["w_ada"], "in": t["w_in"], "out": t["w_out"]}[kind]
                        load(n, ring[n % RING][:, :].rearrange("p (k f) -> p k f", f=W),
                             src[L, :, b * W:(b + 1) * W].rearrange("(k p) f -> p k f", p=P))
                with sp.Fori(0, PAIRS) as pr:
                    for j in range(BPP):
                        name = ("moe_w1", "moe_w3", "moe_w2")[j // 2]
                        f = FE if j < 4 else D
                        sp.wait_ge(slots_free, L * N_BLOCKS + pr * BPP + (N_HEAD + j + 1))
                        sp.dma_start(ring[j][:, :].rearrange("p (k f) -> p k f", f=f),
                                     t[name][L, pr * 2 + j % 2, :, :].rearrange("(k p) f -> p k f", p=P))\
                          .then_inc(slot_in[j], 16)

        @block.gpsimd
        def _(pool):
            with pool.Fori(0, DEPTH) as L:
                loads = [
                    (vrow[R_N1:R_N1 + ND, :], t["norm1_g"][L, :].rearrange("(k p) -> k p", p=P)),
                    (vrow[R_N2:R_N2 + ND, :], t["norm2_g"][L, :].rearrange("(k p) -> k p", p=P)),
                    (vrow[R_WSC:R_BSC, :], t["w_sc"][L, :, :].rearrange("j (k p) -> (j k) p", p=P)),
                    (vrow[R_BSC:R_HYB, :], t["b_sc"][L, :].rearrange("(k p) -> k p", p=P)),
                    (vrow[R_HYB:R_ALL, :], t["hy_bias"][L, :].rearrange("(k p) -> k p", p=P)),
                    (brow[:, :], t["b_ada"][L, :].rearrange("(k p) -> k p", p=P)),
                    (hrow[0:1, :], t["hf_b1"][L, :].rearrange("(a n) -> a n", a=1)),
                    (hrow[1:2, :], t["hf_b2"][L, :].rearrange("(a n) -> a n", a=1)),
                    (hrow[2:3, :], t["hf_b3"][L, :].rearrange("(a n) -> a n", a=1)),
                    (hrow[3:4, :], t["hf_freq"][L, :].rearrange("(a n) -> a n", a=1)),
                    (hw1[:, :], t["hf_w1"][L, :, :]),
                    (hw2[:, :], t["hf_w2"][L, :, :]),
                    (hw3[:, :], t["hf_w3"][L, :, :]),
                    (zpos[0:EMB, :], t["zpos"]),
                ]
                assert len(loads) == N_SMALL
                for dst, src in loads:
                    pool.dma_start(dst, src).then_inc(s_small, 16)
                pool.wait_ge(v_layer, L + 1)
                settle(pool)
                pool.dma_start(decay, t["decay"]).then_inc(s_filter, 16)
                pool.dma_start(hw4, t["hf_w4"][L, :, :]).then_inc(s_filter, 16)
                for n, g in ((2, g1b), (5, g2b)):
                    pool.dma_start(g[:, :], t["b_ada"][L, n * D:(n + 1) * D].rearrange("(a n) -> a n", a=1)
                                   .to_broadcast([P, D])).then_inc(s_gbias, 16)
                pool.wait_ge(a_ks, (L + 1) * 8)
                pool.wait_ge(v_kx, (L + 1) * 2)
                pool.wait_ge(p_tr, L * 8 + 4)
                settle(pool)
                pool.memset(qm, 0.0).then_inc(g_qm, 1)
                pool.wait_ge(p_br, (L + 1) * 8)
            pool.wait_ge(s_out, 16 * NT)

        @block.tensor
        def _(pe):
            def mm(dst, lhsT, rhs, start, stop):
                return pe.matmul(dst, lhsT, rhs, start=start, stop=stop, skip_group_check=True)

            first_credit(pe, PE_SIGNALS)
            pe.wait_ge(s_start, 16 * N_START)
            pe.transpose(bank[0][:, 0:ND], crow, ident[0:ND, 0:ND]).then_inc(p_c, 1)
            pe.wait_ge(v_c, 2)

            def free_after(done, value, n=1):
                pe.wait_ge(done, value)
                pe.sem_inc(slots_free, n)

            with pe.Fori(0, DEPTH) as L:
                def landed(n):
                    pe.wait_ge(slot_in[n % RING], (L * PER_SLOT + (n // RING + 1)) * 16)
                    return ring[n % RING]

                def block_of(kind, b):
                    return landed(at_[kind, b])[:, :].rearrange("p (k f) -> p k f", f=W)

                pe.wait_ge(s_small, (L + 1) * (16 * N_SMALL))
                pe.wait_ge(v_layer, L + 1)
                pe.transpose(bank[6][:, 0:R_ALL], vrow[0:R_ALL, :], ident[0:R_ALL, 0:R_ALL])
                pe.transpose(bank[6][:, P:P + 6 * ND], brow[:, :], ident[0:6 * ND, 0:6 * ND])
                pe.transpose(bank[6][0:FFN, 2 * P:2 * P + 4], hrow[:, :], ident[0:4, 0:4]).then_inc(p_vec, 1)

                def ada_post(n):
                    pe.wait_ge(v_ada, L * N_ADA + n + 1)
                    if n // 2 in (2, 5):
                        q = (n // 2 == 5) * 2 + n % 2
                        if q >= 1:
                            pe.wait_ge(v_mod, L * 4 + q)
                        mm(bank[7][:, :], ones, acc[:, n % 2, :], True, True).then_inc(p_mod, 1)
                    else:
                        for j in range(4):
                            last = mm(bank[6][:, n * 4 + j:n * 4 + j + 1], acc[:, n % 2, j * P:(j + 1) * P],
                                      ones[:, 0:1], True, True)
                        last.then_inc(p_mod, 1)

                def ada(n):
                    w = block_of("ada", n)
                    if n >= 2:
                        pe.wait_ge(v_ada, L * N_ADA + n - 1)
                    for h in range(2):
                        for j in range(4):
                            k = h * 4 + j
                            last = mm(bank[4 + n % 2][32 * j:32 * j + 32, :], cpad[:, k, :], w[:, k, :], h == 0, h == 1)
                    last.then_inc(slots_free, 1)

                pe.wait_ge(v_vec, (L + 1) * 3)
                settle(pe)
                mm(bank[7][0:FFN, 0:SEQ], hw1[:, :], zpos[0:EMB, :], True, True).then_inc(p_fil, 1)
                ada(0)
                ada(1)
                for s, w in ((1, hw2), (2, hw3)):
                    pe.wait_ge(a_fh, L * 3 + s)
                    settle(pe)
                    mm(bank[7][0:FFN, 0:SEQ], w[:, :], fh[0:FFN, :], True, True).then_inc(p_fil, 1)
                    ada_post(2 * s - 2)
                    if s == 1:
                        ada(2)
                        ada_post(1)
                        ada(3)
                    else:
                        ada_post(3)
                pe.wait_ge(a_fh, (L + 1) * 3)
                pe.wait_ge(s_filter, (L + 1) * 32)
                u = 0
                for b in range(2):
                    for lt in range(NT):
                        for n in range(2):
                            if u >= 4:
                                pe.wait_ge(v_kt, L * 10 + u - 3)
                            mm(bank[u % 4][:, 0:HW2], fh[0:FFN, lt * P:(lt + 1) * P],
                               hw4[:, b * HY + n * HW2:b * HY + (n + 1) * HW2], True, True).then_inc(p_kt, 1)
                            u += 1
                pe.wait_ge(v_kt, (L + 1) * 10)
                u = 0
                for b, tab in ((0, ctab), (1, stab)):
                    for m in range(2):
                        for n in range(2):
                            if u >= 4:
                                pe.wait_ge(a_ks, L * 8 + u - 3)
                            for lt in range(NT):
                                last = mm(bank[u % 4][:, 0:HW2], tab[:, lt, m * P:(m + 1) * P],
                                          decay[:, b, lt, n * HW2:(n + 1) * HW2], lt == 0, lt == NT - 1)
                            last.then_inc(p_ks, 1)
                            u += 1
                for n in range(2):
                    for lt in range(NT):
                        last = mm(bank[4 + n][0:1, 0:HW2], stab[:, lt, 0:1],
                                  decay[:, 0, lt, n * HW2:(n + 1) * HW2], lt == 0, lt == NT - 1)
                last.then_inc(p_ks, 1)

                def transposes_to_h(q):
                    pe.wait_ge(v_xn, L * 2 + q + 1)
                    for k in range(ND):
                        for tt in range(NT):
                            last = pe.transpose(bank[k // 2][:, (k % 2) * SEQ + tt * P:(k % 2) * SEQ + (tt + 1) * P],
                                                xn[:, tt, k * P:(k + 1) * P], ident)
                        if k % 2:
                            last.then_inc(p_tr, 1)

                pe.wait_ge(a_ks, (L + 1) * 8)
                transposes_to_h(0)

                for c in range(NSC):
                    w = block_of("in", c // 4)
                    if c >= 4:
                        pe.wait_ge(v_u, L * NSC + c - 3)
                    for k in range(ND):
                        if c == 0 and k % 2 == 0:
                            pe.wait_ge(v_hT, L * 8 + k // 2 + 1)
                        last = mm(bank[c % 4][:, 0:SEQ], w[:, k, (c % 4) * P:(c % 4 + 1) * P], hT[:, k, :],
                                  k == 0, k == ND - 1)
                    last.then_inc(p_u, 1)
                    if c % 4 == 3:
                        free_after(p_u, L * NSC + c + 1)
                    if c % 2:
                        n = N_EARLY + c // 2
                        if n == N_EARLY:
                            pe.wait_ge(v_kx, (L + 1) * 2)
                        if n < N_ADA:
                            ada(n)
                        if N_EARLY < n <= N_ADA:
                            ada_post(n - 1)
                for g in range(2 * GROUPS):
                    col = NSC * P + g * GW
                    b, o = col // W, col % W
                    w = block_of("in", b)
                    if g >= 2:
                        pe.wait_ge(v_qk, L * 6 + g - 1)
                    for xx in range(2):
                        for k in range(ND):
                            for hh in range(HPG):
                                a = o + hh * HD + xx * HALF
                                last = mm(bank[4 + g % 2][hh * HALF:(hh + 1) * HALF, xx * SEQ:(xx + 1) * SEQ],
                                          w[:, k, a:a + HALF], hT[:, k, :], k == 0, k == ND - 1)
                    last.then_inc(p_qk, 1)
                    if o + GW == W:
                        free_after(p_qk, L * 6 + g + 1)
                pe.wait_ge(v_mod, (L + 1) * 4)
                pe.wait_ge(v_A2, L + 1)
                for tt in range(NT):
                    for half in range(2):
                        b, o, n = (7, GW, GW) if half == 0 else (8, 0, W)
                        w = block_of("in", b)
                        for k in range(ND):
                            last = mm(bank[6 + half][:, 0:n], hT[:, k, tt * P:(tt + 1) * P], w[:, k, o:o + n],
                                      k == 0, k == ND - 1)
                        last.then_inc(p_v, 1)
                    if tt == 0:
                        pe.wait_ge(a_v, L * 4 + 2)
                free_after(p_v, L * 4 + 4, 2)

                pe.wait_ge(v_u, (L + 1) * NSC)
                pe.wait_ge(v_qk, (L + 1) * 6)
                pe.wait_ge(a_v, (L + 1) * 4)

                def scores(h):
                    g = h // HPG
                    pe.wait_ge(v_qm, L * GROUPS + g + 1)
                    if h >= 2:
                        pe.wait_ge(v_s, L * HEADS + h - 1)
                    for qt in range(NT):
                        for xx in range(2):
                            last = mm(bank[h % 2][:, qt * SEQ:(qt + 1) * SEQ], qm[:, xx, h % HPG, qt * P:(qt + 1) * P],
                                      kr[:, g, xx, :], xx == 0, xx == 1)
                    last.then_inc(p_s, 1)

                def attend(h):
                    pe.wait_ge(a_p, L * HEADS + h + 1)
                    if h >= 2:
                        pe.wait_ge(a_pt, L * HEADS + h - 1)
                    for qt in range(NT):
                        for kt in range(NT):
                            last = pe.transpose(bank[2 + h % 2][:, kt * SEQ + qt * P:kt * SEQ + (qt + 1) * P],
                                                sm[h % 2][:, qt, kt * P:(kt + 1) * P], ident)
                    last.then_inc(p_pt, 1)

                def values(h):
                    pe.wait_ge(a_pt, L * HEADS + h + 1)
                    for qt in range(NT):
                        for kt in range(NT):
                            last = mm(bank[4 + 2 * qt + h // 8][:, (h % 8) * HD:(h % 8 + 1) * HD],
                                      pT[:, kt, qt * P:(qt + 1) * P], vv[:, kt, h * HD:(h + 1) * HD],
                                      kt == 0, kt == NT - 1)
                    last.then_inc(p_o, 1)

                scores(0)
                for h in range(HEADS):
                    if h + 1 < HEADS:
                        scores(h + 1)
                    if h:
                        values(h - 1)
                    attend(h)
                values(HEADS - 1)
                pe.wait_ge(v_yat, L + 1)
                for c in range(2):
                    for tt in range(NT):
                        last = pe.transpose(bank[0][:, c * SEQ + tt * P:c * SEQ + (tt + 1) * P],
                                            yat[:, tt, c * P:(c + 1) * P], ident)
                last.then_inc(p_yat, 1)

                for tt in range(NT):
                    for half in range(2):
                        for j in range(3):
                            c = half * 3 + j
                            last = pe.transpose(bank[1 + tt * 2 + half][:, j * P:(j + 1) * P],
                                                zvT[:, c, tt * P:(tt + 1) * P], ident)
                        last.then_inc(p_zt, 1)
                pe.wait_ge(a_zt, (L + 1) * 4)
                u = 0
                for m in range(2):
                    for n in range(2):
                        if u >= 2:
                            pe.wait_ge(v_z, L * 4 + u - 1)
                        if u == 0:
                            pe.wait_ge(a_yat, L + 1)
                        for s, tab in enumerate((ctab, stab)):
                            for tt in range(NT):
                                last = mm(bank[2 * (u % 2) + s][:, 0:HW2], tab[:, tt, m * P:(m + 1) * P],
                                          ztok[:, tt, n * HW2:(n + 1) * HW2], tt == 0, tt == NT - 1)
                        last.then_inc(p_z, 1)
                        u += 1
                pe.wait_ge(v_z, (L + 1) * 4)
                for c in range(NH_CH):
                    if c >= 4:
                        pe.wait_ge(v_y, L * NH_CH + c - 3)
                    q = 0
                    for spec, tab in ((Yr, ictab), (Ys, istab)):
                        for m in range(2):
                            last = mm(bank[4 + c % 4][:, 0:SEQ], spec[:, m, c * P:(c + 1) * P], tab[:, m, :],
                                      q == 0, q == 3)
                            q += 1
                    last.then_inc(p_y, 1)

                def gate(q):
                    w = block_of("in", IN_A + q)
                    if q >= 1:
                        pe.wait_ge(a_gate, L * 8 + 2 * q)
                    for tt in range(NT):
                        for k in range(ND):
                            last = mm(bank[tt][:, :], hT[:, k, tt * P:(tt + 1) * P], w[:, k, :], k == 0, k == ND - 1)
                        last.then_inc(p_gate, 1)
                    free_after(p_gate, L * 8 + 2 * q + 2)

                def branch(q, w, src, ks, o):
                    if q >= 1:
                        pe.wait_ge(v_br, L * 8 + 2 * q)
                    for tt in range(NT):
                        for k in range(ks):
                            last = mm(bank[2 + tt][:, :], src[:, k, tt * P:(tt + 1) * P], w[:, k, o:o + W],
                                      k == 0, k == ks - 1)
                        last.then_inc(p_br, 1)

                pe.wait_ge(v_y, (L + 1) * NH_CH)
                for q in range(2):
                    gate(q)
                    wv = landed(at_["brh", q])[:, 0:NH_CH * W].rearrange("p (k f) -> p k f", f=W)
                    branch(q, wv, x0T, NH_CH, 0)
                    free_after(p_br, L * 8 + 2 * q + 2)
                gate(2)
                gate(3)
                wv = landed(at_["bra", 0])[:, 0:2 * D].rearrange("p (k f) -> p k f", f=D)
                branch(2, wv, yatT, 2, 0)
                branch(3, wv, yatT, 2, W)
                free_after(p_br, L * 8 + 8)
                pe.wait_ge(v_br, (L + 1) * 8)
                for k in range(ND):
                    for tt in range(NT):
                        last = pe.transpose(bank[4 + k // 2][:, (k % 2) * SEQ + tt * P:(k % 2) * SEQ + (tt + 1) * P],
                                            merged[:, tt, k * P:(k + 1) * P], ident)
                    if k % 2:
                        last.then_inc(p_mt, 1)
                pe.wait_ge(a_mt, (L + 1) * 4)
                for n in range(2):
                    w = block_of("out", n)
                    for tt in range(NT):
                        for k in range(ND):
                            last = mm(bank[2 * n + tt][:, :], mT[:, k, tt * P:(tt + 1) * P], w[:, k, :],
                                      k == 0, k == ND - 1)
                        last.then_inc(p_wo, 1)
                    free_after(p_wo, L * 4 + 2 * n + 2)

                pe.wait_ge(v_wo, (L + 1) * 4)
                transposes_to_h(1)
                pe.wait_ge(v_hT, (L + 1) * 8)
                for tt in range(NT):
                    for k in range(ND):
                        last = mm(bank[4][:, tt * NE:(tt + 1) * NE], hT[:, k, tt * P:(tt + 1) * P], router[:, k, :],
                                  k == 0, k == ND - 1)
                last.then_inc(p_lg, 1)
                pe.wait_ge(v_oh, L + 1)
                mm(bank[5][:, 0:NE], tri, rb[oh][:, 0, :], True, True)
                mm(bank[5][:, NE:2 * NE], ones, rb[oh][:, 0, :], True, False)
                mm(bank[5][:, NE:2 * NE], tri, rb[oh][:, 1, :], False, True)
                mm(bank[5][:, 2 * NE:3 * NE], ones, rb[oh][:, 0, :], True, False)
                mm(bank[5][:, 2 * NE:3 * NE], ones, rb[oh][:, 1, :], False, True).then_inc(p_pos, 1)
                pe.wait_ge(v_rt, L + 1)
                settle(pe)

                def gather(at, buf):
                    at.wait(pe, "v_sel")
                    for k in range(ND):
                        for tt in range(NT):
                            last = mm(bank[2 + k // 4][:, (k % 4) * P:(k % 4 + 1) * P], xn[:, tt, k * P:(k + 1) * P],
                                      buf[0][:, tt, :], tt == 0, tt == NT - 1)
                        if k % 4 == 3:
                            last.then_inc(at.s["p_hg"], 1)

                def up(at, buf, arrived, last_use):
                    at.wait(pe, "a_hg")
                    for which in range(2):
                        arrived(2 * which)
                        arrived(2 * which + 1)
                        for k in range(ND):
                            if which == 0 and k == 4:
                                at.wait(pe, "v_hg")
                            for e in range(2):
                                w = ring[2 * which + e][:, :].rearrange("p (k f) -> p k f", f=FE)
                                last = mm(bank[which][CAP * e:CAP * (e + 1), :], buf[6][:, k, CAP * e:CAP * (e + 1)],
                                          w[:, k, :], k == 0, k == ND - 1)
                        last.then_inc(at.s["p_up"], 1)
                        if which == 0:
                            at.wait(pe, "p_up", 1)
                            settle(pe)
                            with pe.If(last_use):
                                pe.sem_inc(slots_free, 2)

                def turn(at, buf):
                    for tt in range(NT):
                        last = pe.transpose(bank[4][:, tt * P:(tt + 1) * P], buf[1][:, tt, :], ident)
                    last.then_inc(at.s["p_selT"], 1)
                    at.wait(pe, "v_act")
                    for f in range(NF):
                        last = pe.transpose(bank[5][:, f * P:(f + 1) * P], act[:, f * P:(f + 1) * P], ident)
                    last.then_inc(at.s["p_actT"], 1)

                def down(at, arrived):
                    at.wait(pe, "a_actT")
                    arrived(4)
                    arrived(5)
                    for n in range(2):
                        for f in range(NF):
                            for e in range(2):
                                w = ring[4 + e][:, :].rearrange("p (k f) -> p k f", f=D)
                                last = mm(bank[6 + n][CAP * e:CAP * (e + 1), :], actT[:, f, CAP * e:CAP * (e + 1)],
                                          w[:, f, n * W:(n + 1) * W], f == 0, f == NF - 1)
                        last.then_inc(at.s["p_down"], 1)

                def scatter(at, buf):
                    at.wait(pe, "a_yS")
                    at.wait(pe, "v_yS")
                    at.wait(pe, "a_selT")
                    for tt in (1, 0):
                        for n in range(2):
                            mm(bank[2 + 2 * tt + n][:, :], buf[2][:, tt * P:(tt + 1) * P],
                               buf[3][:, n * W:(n + 1) * W], True, True).then_inc(at.s["p_sc"], 1)

                gather(At(main, L * PAIRS), buf_m)
                with pe.Fori(0, PAIRS) as pr:
                    n = pe.value_load(cnt_i[0:1, bass.ds(pr, 1)], min_val=0, max_val=SEQ)
                    run = L * PAIRS + pr
                    at, before, after = At(main, run), At(main, run - 1), At(main, run + 1)

                    def arrived(j):
                        pe.wait_ge(slot_in[j], (L * PER_SLOT + pr + (N_HEAD // RING + 1)) * 16)

                    up(at, buf_m, arrived, n <= CAP)
                    with pe.If(pr > 0):
                        At(ovf, run * EXTRA).wait_before(pe, "v_acc")
                        scatter(before, buf_m)
                        before.wait(pe, "v_acc", 2)
                        settle(pe)
                    turn(at, buf_m)
                    with pe.If(n <= CAP):
                        pe.sem_inc(slots_free, 2)
                    down(at, arrived)
                    with pe.If(pr > 0):
                        before.wait(pe, "v_acc")
                        settle(pe)
                    with pe.If(pr < PAIRS - 1):
                        gather(after, buf_m)
                    with pe.If(n <= CAP):
                        skip(pe, PE_SIGNALS, At(ovf, run * EXTRA), EXTRA)
                    with pe.Else():
                        with pe.If(pr < PAIRS - 1):
                            after.wait(pe, "a_hg")
                            after.wait(pe, "v_hg")
                            settle(pe)
                        with pe.Fori(0, EXTRA) as b:
                            ob = At(ovf, run * EXTRA + b)
                            with pe.If(n > b * CAP + CAP):
                                ob.wait_before(pe, "v_acc")
                                gather(ob, buf_x)
                                up(ob, buf_x, arrived, n <= b * CAP + 2 * CAP)
                                turn(ob, buf_x)
                                with pe.If(n <= b * CAP + 2 * CAP):
                                    pe.sem_inc(slots_free, 2)
                                at.wait(pe, "a_yS")
                                at.wait(pe, "v_yS")
                                settle(pe)
                                down(ob, arrived)
                                scatter(ob, buf_x)
                                ob.wait(pe, "p_sc")
                                settle(pe)
                            with pe.Else():
                                skip(pe, PE_SIGNALS, ob, 1)
                    at.wait(pe, "p_down")
                    pe.sem_inc(slots_free, 2)
                At(ovf, (L + 1) * (PAIRS * EXTRA)).wait_before(pe, "v_acc")
                scatter(At(main, L * PAIRS + (PAIRS - 1)), buf_m)

        @block.scalar
        def _(sc):
            starts = [
                (cst[:, :], t["cst"]),
                (crow, t["c"][0, :].rearrange("(k p) -> k p", p=P)),
                (router[:, :, :], t["router_w"].rearrange("(k p) e -> p k e", p=P)),
                (rbias[:, :], t["router_bias"].rearrange("(a n) -> a n", a=1).to_broadcast([P, NE])),
                (x[:, 0, :], t["x"][0, 0:P, :]),
                (x[:, 1, :], t["x"][0, P:2 * P, :]),
            ]
            assert len(starts) == N_START
            for dst, src in starts:
                sc.dma_start(dst, src).then_inc(s_start, 16)
            first_credit(sc, ACT_SIGNALS)
            sc.wait_ge(p_c, 1)
            sc.activation(stat[:, 0, 0:ND], bank[0][:, 0:ND], ACT.Sigmoid).then_inc(a_c, 1)
            sc.wait_ge(s_start, 16 * N_START)

            with sc.Fori(0, DEPTH) as L:
                for s in range(3):
                    sc.wait_ge(v_fu, L * 3 + s + 1)
                    sc.activation(fh[0:FFN, :], fu[0:FFN, :], ACT.Sin).then_inc(a_fh, 1)
                def squares(q):
                    for tt in range(NT):
                        last = sc.activation(xn[:, tt, :], x[:, tt, :], ACT.Square, scale=D ** -0.5,
                                             accum_out=ss[:, tt:tt + 1])
                    last.then_inc(a_chain, 1)
                    sc.wait_ge(a_chain, L * 2 + q + 1)
                    sc.activation(rs[:, :], ss[:, :], ACT.Sqrt, bias=eps[:, :]).then_inc(a_sq, 1)

                sc.wait_ge(p_kt, (L + 1) * 8)
                sc.wait_ge(v_layer, L + 1)
                squares(0)
                u = 0
                for dst in (Kr, Ks):
                    for m in range(2):
                        for n in range(2):
                            sc.wait_ge(p_ks, L * 9 + u + 1)
                            sc.activation(dst[:, m, n * HW2:(n + 1) * HW2], bank[u % 4][:, 0:HW2], ACT.Copy)\
                              .then_inc(a_ks, 1)
                            u += 1
                for c in range(NSC):
                    sc.wait_ge(p_u, L * NSC + c + 1)
                    if c >= 2 * NH_CH + 1:
                        sc.wait_ge(v_u, L * NSC + c)
                    dst = x0T[:, c, :] if c < NH_CH else zvT[:, c - NH_CH, :] if c < 2 * NH_CH else tmp[:, 0:SEQ]
                    sc.activation(dst, bank[c % 4][:, 0:SEQ], ACT.Identity,
                                  bias=vT[:, R_BSC + c:R_BSC + c + 1],
                                  scale=vT[:, R_WSC + NSC + c:R_WSC + NSC + c + 1]).then_inc(a_u, 1)
                for tt in range(NT):
                    for half in range(2):
                        sc.wait_ge(p_v, L * 4 + 2 * tt + half + 1)
                        o, n = (0, GW) if half == 0 else (GW, W)
                        sc.activation(vv[:, tt, o:o + n], bank[6 + half][:, 0:n], ACT.Copy).then_inc(a_v, 1)
                for h in range(HEADS):
                    sc.wait_ge(v_s, L * HEADS + h + 1)
                    for qt in range(NT):
                        last = sc.activation(sm[h % 2][:, qt, :], sm[h % 2][:, qt, :], ACT.Exp,
                                             bias=stat[:, 2, h * NT + qt:h * NT + qt + 1], scale=SCALE,
                                             accum_out=stat[:, 1, h * NT + qt:h * NT + qt + 1])
                    last.then_inc(a_p, 1)
                    sc.wait_ge(p_pt, L * HEADS + h + 1)
                    if h >= 1:
                        sc.wait_ge(p_o, L * HEADS + h)
                    sc.activation(pT[:, :, :].rearrange("p t n -> p (t n)"), bank[2 + h % 2][:, :], ACT.Copy)\
                      .then_inc(a_pt, 1)
                sc.wait_ge(v_md, L + 1)
                sc.activation(stat[:, 4, 0:HEADS * NT], stat[:, 3, 0:HEADS * NT], ACT.Exp, scale=SCALE).then_inc(a_me, 1)
                sc.wait_ge(p_yat, L + 1)
                sc.activation(yatT[:, :, :].rearrange("p c n -> p (c n)"), bank[0][:, :], ACT.Copy).then_inc(a_yat, 1)
                for tt in range(NT):
                    for half in range(2):
                        sc.wait_ge(p_zt, L * 4 + 2 * tt + half + 1)
                        sc.activation(ztok[:, tt, half * HW2:(half + 1) * HW2],
                                      bank[1 + tt * 2 + half][:, 0:HW2], ACT.Copy).then_inc(a_zt, 1)
                for q in range(4):
                    if q >= 2:
                        sc.wait_ge(v_br, L * 8 + 2 * (q - 1))
                    for tt in range(NT):
                        sc.wait_ge(p_gate, L * 8 + 2 * q + tt + 1)
                        sc.activation(sg[:, q % 2, tt, :], bank[tt][:, :], ACT.Sigmoid).then_inc(a_gate, 1)
                for j in range(4):
                    sc.wait_ge(p_mt, L * 4 + j + 1)
                    sc.activation(mT[:, 2 * j:2 * j + 2, :].rearrange("p k n -> p (k n)"), bank[4 + j][:, :], ACT.Copy)\
                      .then_inc(a_mt, 1)
                sc.wait_ge(v_wo, (L + 1) * 4)
                squares(1)
                sc.wait_ge(p_lg, L + 1)
                sc.activation(rt[score], bank[4][:, 0:NT * NE], ACT.Sigmoid).then_inc(a_lg, 1)

                def rows_to_h(at, buf):
                    at.wait(sc, "p_hg", 1)
                    for k in range(4):
                        last = sc.activation(buf[6][:, k, :], bank[2][:, k * P:(k + 1) * P], ACT.Identity,
                                             bias=modT[:, 3 * ND + k:3 * ND + k + 1], scale=A2[:, k:k + 1])
                    last.then_inc(at.s["a_hg"], 1)

                def middle(at, buf):
                    at.wait(sc, "p_up", 1)
                    sc.activation(sil, bank[0][:, :], ACT.Silu).then_inc(at.s["a_sil"], 1)
                    at.wait(sc, "p_selT")
                    sc.activation(buf[2], bank[4][:, 0:SEQ], ACT.Copy).then_inc(at.s["a_selT"], 1)
                    at.wait(sc, "p_actT")
                    sc.activation(actT[:, :, :].rearrange("p f s -> p (f s)"), bank[5][:, :], ACT.Copy)\
                      .then_inc(at.s["a_actT"], 1)
                    at.wait(sc, "p_down", 1)
                    sc.activation(buf[3][:, 0:W], bank[6][:, :], ACT.Copy).then_inc(at.s["a_yS"], 1)

                sc.wait_ge(v_rt, L + 1)
                rows_to_h(At(main, L * PAIRS), buf_m)
                with sc.Fori(0, PAIRS) as pr:
                    n = sc.value_load(cnt_i[0:1, bass.ds(pr, 1)], min_val=0, max_val=SEQ)
                    run = L * PAIRS + pr
                    at = At(main, run)
                    middle(at, buf_m)
                    with sc.If(pr < PAIRS - 1):
                        rows_to_h(At(main, run + 1), buf_m)
                    with sc.If(n <= CAP):
                        skip(sc, ACT_SIGNALS, At(ovf, run * EXTRA), EXTRA)
                    with sc.Else():
                        with sc.Fori(0, EXTRA) as b:
                            ob = At(ovf, run * EXTRA + b)
                            with sc.If(n > b * CAP + CAP):
                                rows_to_h(ob, buf_x)
                                middle(ob, buf_x)
                                ob.wait(sc, "p_sc")
                                settle(sc)
                            with sc.Else():
                                skip(sc, ACT_SIGNALS, ob, 1)
            sc.wait_ge(v_layer, DEPTH + 1)
            sc.dma_start(fing, t["final_g"].rearrange("(a n) -> a n", a=1).to_broadcast([P, D])).then_inc(s_fing, 16)
            sc.wait_ge(v_layer, DEPTH + 1)
            for tt in range(NT):
                last = sc.activation(xn[:, tt, :], x[:, tt, :], ACT.Square, scale=D ** -0.5,
                                     accum_out=ss[:, tt:tt + 1])
            last.then_inc(a_chain, 1)
            sc.wait_ge(a_chain, 2 * DEPTH + 1)
            sc.activation(rs[:, :], ss[:, :], ACT.Sqrt, bias=eps[:, :]).then_inc(a_sq, 1)
            for tt in range(NT):
                sc.wait_ge(v_fin, tt + 1)
                sc.dma_start(out[0, tt * P:(tt + 1) * P, :], xn[:, tt, :]).then_inc(s_out, 16)
            sc.wait_ge(s_out, 16 * NT)

        @block.vector
        def _(dv):
            first_credit(dv, DVE_SIGNALS)
            dv.sem_inc(v_layer, 1)
            dv.memset(eps[:, :], EPS)
            dv.memset(cpad[:, :, :], 0.0).then_inc(v_c, 1)
            dv.wait_ge(a_c, 1)
            dv.wait_ge(v_c, 1)
            dv.tensor_tensor(cpad[:, :, 0:1].rearrange("p k a -> p (k a)"), bank[0][:, 0:ND], stat[:, 0, 0:ND], ALU.mult)\
              .then_inc(v_c, 1)
            dv.wait_ge(s_start, 16 * N_START)

            count = [0]

            def rsqrt(link):
                link(dv.reciprocal(rs[:, :], rs[:, :]))
                link(dv.tensor_scalar(ss[:, :], ss[:, :], EPS, -0.5, ALU.add, ALU.mult))
                link(dv.tensor_tensor(ss[:, :], ss[:, :], rs[:, :], ALU.mult))
                link(dv.tensor_tensor(ss[:, :], ss[:, :], rs[:, :], ALU.mult))
                link(dv.scalar_tensor_tensor(rs[:, :], ss[:, :], 1.5, rs[:, :], ALU.add, ALU.mult))

            with dv.Fori(0, DEPTH) as L:
                def link(ins):
                    count[0] += 1
                    ins.then_inc(v_chain, 1)
                    dv.wait_ge(v_chain, L * N_CHAIN + count[0])

                dv.wait_ge(p_vec, L + 1)
                dv.tensor_copy(vT[:, :], bank[6][:, 0:R_ALL]).then_inc(v_vec, 1)
                dv.tensor_copy(bT[:, :], bank[6][:, P:P + 6 * ND]).then_inc(v_vec, 1)
                dv.tensor_copy(hvT[:, :], bank[6][0:FFN, 2 * P:2 * P + 4]).then_inc(v_vec, 1)
                dv.wait_ge(v_vec, (L + 1) * 3)
                def ada_copy(n):
                    dv.wait_ge(slots_free, L * N_BLOCKS + (RING + at_["ada", n] + 1))
                    if n >= 2:
                        dv.wait_ge(p_mod, L * N_ADA + n - 1)
                    dv.tensor_copy(acc[:, n % 2, :], bank[4 + n % 2][:, :]).then_inc(v_ada, 1)

                def ada_gate(n):
                    if n // 2 in (2, 5):
                        g = g1b if n // 2 == 2 else g2b
                        cols = slice((n % 2) * W, (n % 2 + 1) * W)
                        dv.wait_ge(s_gbias, (L + 1) * 32)
                        dv.wait_ge(p_mod, L * N_ADA + n + 1)
                        dv.tensor_tensor(g[:, cols], bank[7][:, :], g[:, cols], ALU.add).then_inc(v_mod, 1)

                u_, k_ = fu[0:FFN, :], fk[0:FFN, :]
                for s in range(3):
                    dv.wait_ge(p_fil, L * 3 + s + 1)
                    if s >= 1:
                        dv.wait_ge(a_fh, L * 3 + s)
                    link(dv.tensor_scalar(u_, bank[7][0:FFN, 0:SEQ], hvT[:, s:s + 1], hvT[:, 3:4], ALU.add, ALU.mult))
                    link(dv.tensor_scalar(k_, u_, INV2PI, MAGIC, ALU.mult, ALU.add))
                    link(dv.tensor_scalar(k_, k_, MAGIC, None, ALU.subtract))
                    link(dv.scalar_tensor_tensor(u_, k_, -TWOPI_HI, u_, ALU.mult, ALU.add))
                    link(dv.scalar_tensor_tensor(u_, k_, -TWOPI_LO, u_, ALU.mult, ALU.add))
                    dv.tensor_scalar(u_, u_, PI_SAFE, -PI_SAFE, ALU.min, ALU.max).then_inc(v_fu, 1)
                    if s < 2:
                        ada_copy(2 * s)
                        ada_copy(2 * s + 1)
                dv.wait_ge(p_mod, L * N_ADA + N_EARLY)
                cols = slice(0, 2 * ND)
                link(dv.tensor_tensor(modT[:, cols], bank[6][:, cols], bT[:, cols], ALU.add))
                dv.scalar_tensor_tensor(A1[:, :], modT[:, ND:2 * ND], 1.0, vT[:, R_N1:R_N1 + ND], ALU.add, ALU.mult)\
                  .then_inc(v_A1, 1)
                dv.wait_ge(v_A1, L + 1)
                dv.wait_ge(s_filter, (L + 1) * 32)
                u = 0
                for b in range(2):
                    for lt in range(NT):
                        for n in range(2):
                            dv.wait_ge(p_kt, L * 8 + u + 1)
                            cols = slice(n * HW2, (n + 1) * HW2)
                            dv.tensor_tensor(kfb[b][:, lt, cols], bank[u % 4][:, 0:HW2], decay[:, b, lt, cols], ALU.mult)\
                              .then_inc(v_kt, 1)
                            u += 1
                dv.wait_ge(v_kt, L * 10 + 8)
                dv.tensor_tensor(decay[:, 0, :, :], kfb[0], kfb[1], ALU.add).then_inc(v_kt, 1)
                dv.tensor_tensor(decay[:, 1, :, :], kfb[0], kfb[1], ALU.subtract).then_inc(v_kt, 1)
                def norm(q, nsq):
                    dv.wait_ge(a_sq, nsq)
                    rsqrt(link)
                    for tt in range(NT):
                        last = dv.tensor_scalar(xn[:, tt, :], x[:, tt, :], rs[:, tt:tt + 1], None, ALU.mult)
                    return last

                def to_h(q, A, shift):
                    for j in range(4):
                        dv.wait_ge(p_tr, L * 8 + 4 * q + j + 1)
                        for k in (2 * j, 2 * j + 1):
                            last = dv.tensor_scalar(hT[:, k, :], bank[j][:, (k % 2) * SEQ:(k % 2 + 1) * SEQ],
                                                    A[:, k:k + 1], modT[:, shift + k:shift + k + 1], ALU.mult, ALU.add)
                        last.then_inc(v_hT, 1)

                norm(0, L * 2 + 1).then_inc(v_xn, 1)
                dv.wait_ge(a_ks, (L + 1) * 8)
                dv.wait_ge(p_ks, (L + 1) * 9)
                link(dv.tensor_copy(KX[:, :], Kr[:, 0, :]))
                for n in range(2):
                    last = dv.tensor_copy(KX[0:1, n * HW2:(n + 1) * HW2], bank[4 + n][0:1, 0:HW2])
                last.then_inc(v_kx, 1)
                dv.memset(Ks[0:1, 0, :], 0.0).then_inc(v_kx, 1)
                to_h(0, A1, 0)

                for c in range(NSC):
                    dv.wait_ge(a_u, L * NSC + c + 1)
                    dst = x0T[:, c, :] if c < NH_CH else zvT[:, c - NH_CH, :] if c < 2 * NH_CH else tmp[:, 0:SEQ]
                    src = bank[c % 4]
                    link(dv.scalar_tensor_tensor(dst[:, 1:SEQ], src[:, 0:SEQ - 1], vT[:, R_WSC + c:R_WSC + c + 1],
                                                 dst[:, 1:SEQ], ALU.mult, ALU.add))
                    w2c = R_WSC + 2 * NSC + c
                    last = dv.scalar_tensor_tensor(dst[:, 0:SEQ - 1], src[:, 1:SEQ], vT[:, w2c:w2c + 1],
                                                   dst[:, 0:SEQ - 1], ALU.mult, ALU.add)
                    if c >= 2 * NH_CH:
                        link(last)
                        z = zvT[:, c - 2 * NH_CH, :]
                        last = dv.tensor_tensor(z, z, dst, ALU.mult)
                    last.then_inc(v_u, 1)
                    if c % 2:
                        n = N_EARLY + c // 2
                        if n < N_ADA:
                            ada_copy(n)
                        if N_EARLY < n <= N_ADA:
                            ada_gate(n - 1)
                dv.wait_ge(p_mod, (L + 1) * N_ADA)
                cols = slice(3 * ND, 5 * ND)
                link(dv.tensor_tensor(modT[:, cols], bank[6][:, cols], bT[:, cols], ALU.add))
                dv.scalar_tensor_tensor(A2[:, :], modT[:, 4 * ND:5 * ND], 1.0, vT[:, R_N2:R_N2 + ND],
                                        ALU.add, ALU.mult).then_inc(v_A2, 1)
                dv.wait_ge(v_A2, L + 1)
                dv.wait_ge(v_u, (L + 1) * NSC)
                for g in range(2 * GROUPS):
                    dv.wait_ge(p_qk, L * 6 + g + 1)
                    dst = (qr if g < GROUPS else kr)[:, g % GROUPS, :, :]
                    src = bank[4 + g % 2]
                    tv = tmp.rearrange("p (x n) -> p x n", x=2)
                    for xx in range(2):
                        dv.tensor_tensor(dst[:, xx, :], src[:, xx * SEQ:(xx + 1) * SEQ], rcos, ALU.mult)
                    for xx in range(2):
                        last = dv.tensor_tensor(tv[:, xx, :], src[:, (1 - xx) * SEQ:(2 - xx) * SEQ],
                                                rsin[:, xx * SEQ:(xx + 1) * SEQ], ALU.mult)
                    link(last)
                    dv.tensor_tensor(dst, dst, tv, ALU.add).then_inc(v_qk, 1)
                    dv.wait_ge(v_qk, L * 6 + g + 1)
                dv.wait_ge(g_qm, L + 1)
                for h in range(HEADS):
                    g = h // HPG
                    if h % HPG == 0:
                        if h:
                            dv.wait_ge(p_s, L * HEADS + h)
                        for hh in range(HPG):
                            rows = slice(hh * HALF, (hh + 1) * HALF)
                            last = dv.tensor_copy(qm[rows, :, hh, :], qr[rows, g, :, :])
                        last.then_inc(v_qm, 1)
                    dv.wait_ge(p_s, L * HEADS + h + 1)
                    if h >= 2:
                        dv.wait_ge(p_pt, L * HEADS + h - 1)
                    settle(dv)
                    for qt in range(NT):
                        last = dv.tensor_tensor_reduce(out=sm[h % 2][:, qt, :], in0=bank[h % 2][:, qt * SEQ:(qt + 1) * SEQ],
                                                       in1=mask(g, qt), scale=1.0, scalar=-3e38, op0=ALU.add, op1=ALU.max,
                                                       accum_out=stat[:, 0, h * NT + qt:h * NT + qt + 1])
                    link(last)
                    dv.tensor_scalar(stat[:, 2, h * NT:(h + 1) * NT], stat[:, 0, h * NT:(h + 1) * NT], -SCALE, None,
                                     ALU.mult).then_inc(v_s, 1)
                n8 = HPG * NT
                m_ = stat[:, 0, 0:GROUPS * n8].rearrange("p (g a) -> p g a", g=GROUPS)
                d_ = stat[:, 3, 0:GROUPS * n8].rearrange("p (g a) -> p g a", g=GROUPS)
                e_ = stat[:, 4, 0:GROUPS * n8].rearrange("p (g a) -> p g a", g=GROUPS)
                s_ = stat[:, 1, 0:GROUPS * n8].rearrange("p (g a) -> p g a", g=GROUPS)
                w_ = stat[:, 5, 0:GROUPS * n8].rearrange("p (g a) -> p g a", g=GROUPS)
                M_ = stat[:, 6, 0:n8]
                dv.wait_ge(v_s, (L + 1) * HEADS)
                link(dv.tensor_tensor(M_, m_[:, 0, :], m_[:, 1, :], ALU.max))
                link(dv.tensor_tensor(M_, M_, m_[:, 2, :], ALU.max))
                for g in range(GROUPS):
                    last = dv.tensor_tensor(d_[:, g, :], m_[:, g, :], M_, ALU.subtract)
                last.then_inc(v_md, 1)
                dv.wait_ge(a_me, L + 1)
                dv.wait_ge(a_p, (L + 1) * HEADS)
                link(dv.tensor_scalar(stat[:, 1, 0:GROUPS * n8], stat[:, 1, 0:GROUPS * n8], 1e-30, None, ALU.max))
                link(dv.tensor_tensor(stat[:, 5, 0:GROUPS * n8], stat[:, 4, 0:GROUPS * n8],
                                      stat[:, 1, 0:GROUPS * n8], ALU.mult))
                link(dv.tensor_tensor(M_, w_[:, 0, :], w_[:, 1, :], ALU.add))
                link(dv.tensor_tensor(M_, M_, w_[:, 2, :], ALU.add))
                link(dv.reciprocal(M_, M_))
                for g in range(GROUPS):
                    last = dv.tensor_tensor(w_[:, g, :], e_[:, g, :], M_, ALU.mult)
                link(last)
                dv.wait_ge(p_o, (L + 1) * HEADS)
                for qt in range(NT):
                    for g in range(GROUPS):
                        for hh in range(HPG):
                            h = g * HPG + hh
                            o = bank[4 + 2 * qt + h // 8][:, (h % 8) * HD:(h % 8 + 1) * HD]
                            dst = yat[:, qt, hh * HD:(hh + 1) * HD]
                            wq = w_[:, g, hh * NT + qt:hh * NT + qt + 1]
                            if g == 0:
                                last = dv.tensor_scalar(dst, o, wq, None, ALU.mult)
                            else:
                                last = dv.scalar_tensor_tensor(dst, o, wq, dst, ALU.mult, ALU.add)
                        if g < GROUPS - 1:
                            link(last)
                last.then_inc(v_yat, 1)
                u = 0
                for m in range(2):
                    for n in range(2):
                        dv.wait_ge(p_z, L * 4 + u + 1)
                        if u:
                            dv.wait_ge(v_z, L * 4 + u)
                        cols = slice(n * HW2, (n + 1) * HW2)
                        zr, zs = bank[2 * (u % 2)][:, 0:HW2], bank[2 * (u % 2) + 1][:, 0:HW2]
                        kx = KX[:, cols] if m == 0 else Kr[:, 1, cols]
                        dv.tensor_tensor(ct[0], zr, Kr[:, m, cols], ALU.mult)
                        dv.tensor_tensor(ct[1], zs, Ks[:, m, cols], ALU.mult)
                        dv.tensor_tensor(ct[2], zr, Ks[:, m, cols], ALU.mult)
                        link(dv.tensor_tensor(ct[3], zs, kx, ALU.mult))
                        dv.tensor_tensor(Yr[:, m, cols], ct[0], ct[1], ALU.subtract)
                        dv.tensor_tensor(Ys[:, m, cols], ct[2], ct[3], ALU.add).then_inc(v_z, 1)
                        u += 1
                for c in range(NH_CH):
                    dv.wait_ge(p_y, L * NH_CH + c + 1)
                    link(dv.scalar_tensor_tensor(zvT[:, c, :], zvT[:, c, :], vT[:, R_HYB + c:R_HYB + c + 1],
                                                 bank[4 + c % 4][:, 0:SEQ], ALU.mult, ALU.add))
                    dv.tensor_tensor(x0T[:, c, :], x0T[:, c, :], zvT[:, c, :], ALU.mult).then_inc(v_y, 1)
                for q in range(4):
                    for tt in range(NT):
                        dv.wait_ge(a_gate, L * 8 + 2 * q + tt + 1)
                        dv.wait_ge(p_br, L * 8 + 2 * q + tt + 1)
                        cols = slice((q % 2) * W, (q % 2 + 1) * W)
                        if q < 2:
                            dv.tensor_tensor(merged[:, tt, cols], bank[2 + tt][:, :], sg[:, q % 2, tt, :], ALU.mult)\
                              .then_inc(v_br, 1)
                        else:
                            link(dv.tensor_tensor(mtmp, bank[2 + tt][:, :], sg[:, q % 2, tt, :], ALU.mult))
                            dv.tensor_tensor(merged[:, tt, cols], merged[:, tt, cols], mtmp, ALU.add).then_inc(v_br, 1)
                            dv.wait_ge(v_br, L * 8 + 2 * q + tt + 1)
                for n in range(2):
                    for tt in range(NT):
                        dv.wait_ge(p_wo, L * 4 + 2 * n + tt + 1)
                        cols = slice(n * W, (n + 1) * W)
                        link(dv.tensor_tensor(mtmp, bank[2 * n + tt][:, :], g1b[:, cols], ALU.mult))
                        link_last = dv.tensor_tensor(x[:, tt, cols], x[:, tt, cols], mtmp, ALU.add)
                        link_last.then_inc(v_wo, 1)
                        dv.wait_ge(v_wo, L * 4 + 2 * n + tt + 1)
                norm(1, L * 2 + 2).then_inc(v_xn, 1)
                to_h(1, A2, 3 * ND)
                link(dv.memset(yacc, 0.0))
                dv.wait_ge(a_lg, L + 1)
                for tt in range(NT):
                    last = dv.tensor_tensor(rb[biased][:, tt, :], rb[score][:, tt, :], rbias[:, :], ALU.add)
                link(last)
                b4, p4, q4 = g4[biased], g4[pair], g4[tA]
                for tt in range(NT):
                    dv.tensor_tensor(p4[:, tt, :, 0:3], b4[:, tt, :, 0:3], b4[:, tt, :, 1:4], ALU.add)
                    dv.tensor_tensor(p4[:, tt, :, 3:4], b4[:, tt, :, 0:1], b4[:, tt, :, 3:4], ALU.add)
                    last = dv.tensor_tensor(q4[:, tt, :, 0:2], b4[:, tt, :, 0:2], b4[:, tt, :, 2:4], ALU.add)
                link(last)
                gs = rt[tB][:, 0:NT * NG]
                gs2 = rt[tB][:, NT * NG:2 * NT * NG]
                dv.tensor_reduce(gs, rt[pair].rearrange("p (a e) -> p a e", e=EPG), AX.X, ALU.max)
                link(dv.tensor_reduce(gs2, rt[tA].rearrange("p (a e) -> p a e", e=EPG)[:, :, 0:2], AX.X, ALU.max))
                link(dv.tensor_tensor(gs, gs, gs2, ALU.max))

                def first_max(dst, src, width, mx, key):
                    link(dv.tensor_reduce(mx, src, AX.X, ALU.max))
                    for tt in range(NT):
                        last = dv.scalar_tensor_tensor(key[:, tt, :], src[:, tt, :], mx[:, tt:tt + 1],
                                                       desc[:, 0:width], ALU.is_equal, ALU.mult)
                    link(last)
                    link(dv.tensor_reduce(mx, key, AX.X, ALU.max))
                    for tt in range(NT):
                        last = dv.tensor_scalar(dst[:, tt, :], key[:, tt, :], mx[:, tt:tt + 1], None, ALU.is_equal)
                    link(last)

                mx = stat[:, 7, 0:NT]
                gsv = gs.rearrange("p (t g) -> p t g", t=NT)
                gk = rt[tC][:, 0:NT * NG].rearrange("p (t g) -> p t g", t=NT)
                gm = rt[tC][:, NT * NG:2 * NT * NG]
                first_max(gm.rearrange("p (t g) -> p t g", t=NT), gsv, NG, mx, gk)
                gmv = gm.rearrange("p (t g) -> p t g", t=NT)
                for e in range(EPG):
                    dv.tensor_tensor(g4[tA][:, :, :, e], g4[biased][:, :, :, e], gmv, ALU.mult)
                    last = dv.tensor_scalar(g4[pair][:, :, :, e], gmv, 1.0, -NEG, ALU.subtract, ALU.mult)
                link(last)
                link(dv.tensor_tensor(rt[tA], rt[tA], rt[pair], ALU.add))
                first_max(rb[oh1], rb[tA], NE, mx, rb[tD])
                link(dv.scalar_tensor_tensor(rt[tA], rt[oh1], 3.0 * NEG, rt[tA], ALU.mult, ALU.add))
                first_max(rb[oh2], rb[tA], NE, mx, rb[tD])
                dv.tensor_tensor(rt[oh], rt[oh1], rt[oh2], ALU.add).then_inc(v_oh, 1)
                dv.wait_ge(v_oh, L + 1)
                link(dv.tensor_tensor(rt[gate_], rt[oh], rt[score], ALU.mult))
                link(dv.tensor_reduce(mx, rb[gate_], AX.X, ALU.add))
                link(dv.reciprocal(mx, mx))
                for tt in range(NT):
                    last = dv.tensor_scalar(rb[gate_][:, tt, :], rb[gate_][:, tt, :], mx[:, tt:tt + 1], None, ALU.mult)
                link(last)
                dv.wait_ge(p_pos, L + 1)
                link(dv.scalar_tensor_tensor(rt[pos_], bank[5][:, 0:NT * NE], 1.0, rt[oh], ALU.add, ALU.mult))
                link(dv.tensor_scalar(rt[pos_], rt[pos_], 1.0, None, ALU.subtract))
                link(dv.tensor_copy(rt[tE][:, 0:NE], bank[5][:, 2 * NE:3 * NE]))
                dv.tensor_reduce(cnt_i[:, :], rt[tE][:, 0:NE].rearrange("p (a e) -> p a e", e=2), AX.X, ALU.max)\
                  .then_inc(v_rt, 1)
                dv.wait_ge(v_rt, L + 1)
                settle(dv)

                def select(at, buf, col):
                    for tt in range(NT):
                        dv.tensor_copy(buf[4][:, tt, :], row(pos_, tt)[:, bass.ds(col, 2)])
                        last = dv.tensor_copy(buf[5][:, tt, :], row(gate_, tt)[:, bass.ds(col, 2)])
                    last.then_inc(at.s["v_pos"], 1)
                    at.wait(dv, "v_pos")
                    for tt in range(NT):
                        for j in range(2):
                            cols = slice(j * CAP, (j + 1) * CAP)
                            dv.tensor_scalar(buf[0][:, tt, cols], iota, buf[4][:, tt, j:j + 1], None, ALU.is_equal)
                            last = dv.tensor_scalar(buf[1][:, tt, cols], iota, buf[4][:, tt, j:j + 1],
                                                    buf[5][:, tt, j:j + 1], ALU.is_equal, ALU.mult)
                    last.then_inc(at.s["v_sel"], 1)

                def rows_to_h(at, buf):
                    at.wait(dv, "p_hg")
                    for kk in range(4, ND):
                        last = dv.tensor_scalar(buf[6][:, kk, :], bank[3][:, (kk - 4) * P:(kk - 3) * P], A2[:, kk:kk + 1],
                                                modT[:, 3 * ND + kk:3 * ND + kk + 1], ALU.mult, ALU.add)
                    last.then_inc(at.s["v_hg"], 1)

                def gated(at):
                    at.wait(dv, "p_up")
                    at.wait(dv, "a_sil")
                    dv.tensor_tensor(act, bank[1][:, :], sil, ALU.mult).then_inc(at.s["v_act"], 1)

                def rows_out(at, buf):
                    at.wait(dv, "p_down")
                    dv.tensor_copy(buf[3][:, W:2 * W], bank[7][:, :]).then_inc(at.s["v_yS"], 1)

                def accumulate(at):
                    k = 0
                    for tt in (1, 0):
                        for n in range(2):
                            k += 1
                            cols = slice(n * W, (n + 1) * W)
                            at.wait(dv, "p_sc", k)
                            last = dv.tensor_tensor(yacc[:, tt, cols], yacc[:, tt, cols], bank[2 + 2 * tt + n][:, :],
                                                    ALU.add)
                            last.then_inc(at.s["v_acc"], 1)
                    at.wait(dv, "v_acc")
                    settle(dv)

                select(At(main, L * PAIRS), buf_m, 0)
                rows_to_h(At(main, L * PAIRS), buf_m)
                with dv.Fori(0, PAIRS) as pr:
                    n = dv.value_load(cnt_i[0:1, bass.ds(pr, 1)], min_val=0, max_val=SEQ)
                    run = L * PAIRS + pr
                    at = At(main, run)
                    gated(at)
                    with dv.If(pr > 0):
                        accumulate(At(main, run - 1))
                    with dv.If(pr < PAIRS - 1):
                        at.wait(dv, "p_selT")
                        settle(dv)
                        select(At(main, run + 1), buf_m, pr * 2 + 2)
                    with dv.If(n > CAP):
                        dv.tensor_scalar(rt[pos_], rt[pos_], float(CAP), None, ALU.subtract).then_inc(v_ovf, 1)
                        dv.wait_ge(v_ovf, run * (EXTRA + 1) + 1)
                        settle(dv)
                        select(At(ovf, run * EXTRA), buf_x, pr * 2)
                    rows_out(at, buf_m)
                    with dv.If(pr < PAIRS - 1):
                        rows_to_h(At(main, run + 1), buf_m)
                    with dv.If(n <= CAP):
                        skip(dv, DVE_SIGNALS, At(ovf, run * EXTRA), EXTRA)
                        dv.sem_inc(v_ovf, EXTRA + 1)
                    with dv.Else():
                        with dv.Fori(0, EXTRA) as b:
                            ob = At(ovf, run * EXTRA + b)
                            with dv.If(b > 0):
                                dv.tensor_scalar(rt[pos_], rt[pos_], float(CAP), None, ALU.subtract).then_inc(v_ovf, 1)
                                dv.wait_ge(v_ovf, run * (EXTRA + 1) + b + 1)
                                settle(dv)
                            with dv.If(n > b * CAP + CAP):
                                with dv.If(b > 0):
                                    select(ob, buf_x, pr * 2)
                                rows_to_h(ob, buf_x)
                                gated(ob)
                                rows_out(ob, buf_x)
                                accumulate(ob)
                            with dv.Else():
                                skip(dv, DVE_SIGNALS, ob, 1)
                        dv.tensor_scalar(rt[pos_], rt[pos_], float(CAP * EXTRA), None, ALU.add).then_inc(v_ovf, 1)
                        dv.wait_ge(v_ovf, (run + 1) * (EXTRA + 1))
                        settle(dv)
                accumulate(At(main, L * PAIRS + (PAIRS - 1)))
                for tt in range(NT):
                    link(dv.tensor_tensor(yacc[:, tt, :], yacc[:, tt, :], g2b[:, :], ALU.mult))
                    last = dv.tensor_tensor(x[:, tt, :], x[:, tt, :], yacc[:, tt, :], ALU.add)
                last.then_inc(v_layer, 1)
                assert count[0] == N_CHAIN, count[0]
            L = DEPTH
            dv.wait_ge(a_sq, 2 * DEPTH + 1)

            def link_end(ins):
                count[0] += 1
                ins.then_inc(v_chain, 1)
                dv.wait_ge(v_chain, (DEPTH - 1) * N_CHAIN + count[0])

            rsqrt(link_end)
            dv.wait_ge(s_fing, 16)
            for tt in range(NT):
                dv.scalar_tensor_tensor(xn[:, tt, :], x[:, tt, :], rs[:, tt:tt + 1], fing, ALU.mult, ALU.mult)\
                  .then_inc(v_fin, 1)


_INS = ["x", "c", "norm1_g", "norm2_g", "w_ada", "b_ada", "w_in", "w_sc", "b_sc", "hf_w1", "hf_b1", "hf_w2", "hf_b2",
        "hf_w3", "hf_b3", "hf_w4", "hf_freq", "hy_bias", "w_br_h", "w_br_a", "w_out", "router_w", "router_bias",
        "moe_w1", "moe_w3", "moe_w2", "final_g"]


def kernel(**inputs):
    import concourse.bacc as _bacc
    from concourse.bass_utils import run_bass_kernel_spmd as _run

    nc = _bacc.Bacc("TRN2", target_bir_lowering=False, num_devices=1)
    arrays, t = {}, {}
    for name in _INS:
        a = np.ascontiguousarray(inputs[name])
        arrays[f"in_{name}_dram"] = a
        t[name] = nc.dram_tensor(f"in_{name}_dram", a.shape, mybir.dt.from_np(a.dtype), kind="ExternalInput").ap()
    for name, a in zip(("cst", "decay", "zpos"), constants()):
        arrays[f"in_{name}_dram"] = a
        t[name] = nc.dram_tensor(f"in_{name}_dram", a.shape, F32, kind="ExternalInput").ap()
    out = nc.dram_tensor("out_0_dram", (1, SEQ, D), F32, kind="ExternalOutput").ap()
    trunk_kernel(nc, t, out)
    r = _run(nc, [arrays], core_ids=[0])
    return r.results[0]["out_0_dram"]
```

```python
from contextlib import ExitStack

import numpy as np

import concourse.bass as bass
from concourse import mybir

F32 = mybir.dt.float32
I32 = mybir.dt.int32
ALU = mybir.AluOpType
ACT = mybir.ActivationFunctionType
AX = mybir.AxisListType

P = 128
D = 1024
SEQ = 256
DEPTH = 2
NT = SEQ // P
ND = D // P
HY = 768
NH_CH = HY // P
NSC = 3 * NH_CH
EMB = 33
FFN = 64
HD = 64
HALF = HD // 2
GROUPS = 3
HPG = 4
HEADS = GROUPS * HPG
GW = HPG * HD
RADIUS = 64
DILATION = (1, 4, 16)
NE = 16
NG = 4
EPG = NE // NG
FE = 512
NF = FE // P
EPS = 1e-6
NEG = -1e30
CAP = 64
FEW = 32
EXTRA = SEQ // CAP - 1
PAIRS = NE // 2
W = 512
HW2 = HY // 2
SCALE = HD ** -0.5

N_ADA = 6 * D // W
IN_A = 9
C_SPEC = 5
C_NYQ = C_SPEC + 4
N_EARLY = 4
N_HEAD = N_ADA + IN_A + 7 + 2
BPP = 6
N_BLOCKS = N_HEAD + BPP * PAIRS
RING = 6
PER_SLOT = N_BLOCKS // RING
assert N_BLOCKS % RING == 0 and N_HEAD % RING == 0

C_ID = 0
C_CT = C_ID + P
C_ST = C_CT + NT * SEQ
C_IC = C_ST + NT * SEQ
C_IS = C_IC + NT * SEQ
C_COS = C_IS + NT * SEQ
C_SIN = C_COS + SEQ
C_MASK = C_SIN + 2 * SEQ
C_TRI = C_MASK + (NT + 2) * SEQ
C_ONE = C_TRI + P
C_IOTA = C_ONE + P
C_DESC = C_IOTA + CAP
C_FOLD = C_DESC + NE
C_ALL = C_FOLD + FEW

R_N1 = 0
R_N2 = R_N1 + ND
R_WSC = R_N2 + ND
R_BSC = R_WSC + 3 * NSC
R_HYB = R_BSC + NSC
R_ALL = R_HYB + NH_CH

INV2PI = float(np.float32(1.0 / (2.0 * np.pi)))
MAGIC = 1.5 * 2.0 ** 23
N_START = 6
N_SMALL = 14
N_CHAIN = 129

TWOPI_HI = 6.28125
TWOPI_LO = float(2.0 * np.pi - 6.28125)
PI_SAFE = 3.1415925


def constants():
    f64 = np.float64
    tab = np.zeros((P, C_ALL), f64)
    tab[:, C_ID:C_ID + P] = np.eye(P)
    tok = np.arange(SEQ)
    fr = np.arange(SEQ)
    cos = np.cos(2 * np.pi * ((tok[:, None] * fr[None, :]) % (2 * SEQ)) / (2 * SEQ))
    sin = np.sin(2 * np.pi * ((tok[:, None] * fr[None, :]) % (2 * SEQ)) / (2 * SEQ))
    sin[:, 0] = (-1.0) ** tok
    wt = np.full(SEQ, 2.0)
    wt[0] = 1.0
    for t in range(NT):
        rows = slice(t * P, (t + 1) * P)
        tab[:, C_CT + t * SEQ:C_CT + (t + 1) * SEQ] = cos[rows]
        tab[:, C_ST + t * SEQ:C_ST + (t + 1) * SEQ] = sin[rows]
        tab[:, C_IC + t * SEQ:C_IC + (t + 1) * SEQ] = (cos * wt).T[rows] / (2 * SEQ)
        tab[:, C_IS + t * SEQ:C_IS + (t + 1) * SEQ] = (sin * wt).T[rows] / (2 * SEQ)
    f32 = np.float32
    inv = f32(10000.0) ** (-np.arange(HALF, dtype=f32) / f32(HALF))
    ang = (tok.astype(f32)[None, :] * inv[:, None]).astype(f64)
    tab[:, C_COS:C_COS + SEQ] = np.tile(np.cos(ang), (P // HALF, 1))
    tab[:, C_SIN:C_SIN + SEQ] = -np.tile(np.sin(ang), (P // HALF, 1))
    tab[:, C_SIN + SEQ:C_SIN + 2 * SEQ] = np.tile(np.sin(ang), (P // HALF, 1))
    for t in range(NT):
        q = t * P + np.arange(P)
        tab[:, C_MASK + t * SEQ:C_MASK + (t + 1) * SEQ] = np.where(np.abs(q[:, None] - tok[None, :]) <= RADIUS, 0, NEG)
    for n, dil in enumerate(DILATION[1:]):
        q = np.arange(P)
        c = C_MASK + (NT + n) * SEQ
        tab[:, c:c + SEQ] = np.where((q[:, None] - tok[None, :]) % dil == 0, 0, NEG)
    tab[:, C_TRI:C_TRI + P] = np.triu(np.ones((P, P)), 1)
    tab[:, C_ONE:C_ONE + P] = 1.0
    tab[:, C_IOTA:C_IOTA + CAP] = np.arange(CAP)
    tab[:, C_DESC:C_DESC + NE] = NE - np.arange(NE)
    tab[:, C_FOLD:C_FOLD + FEW] = np.tile(np.eye(FEW), (P // FEW, 1))
    t = np.linspace(0.0, 1.0, SEQ, dtype=f32).astype(f64)
    deltas = np.linspace(np.log(1e-2) / 1.5, np.log(1e-2) / 0.3, HY, dtype=f32).astype(f64)
    dec = np.exp(-t[:, None] * np.abs(deltas)[None, :])
    dec_b = dec.copy()
    dec_b[0] = 0.0
    decay = np.stack([dec.reshape(NT, P, HY), dec_b.reshape(NT, P, HY)]).transpose(2, 0, 1, 3)
    bands = (EMB - 1) // 2
    ww = (f32(2.0 * np.pi) * tok.astype(f32)[:, None] / f32(SEQ))
    ff = np.linspace(1e-4, bands - 1, bands, dtype=f32)[None, :]
    zz = np.concatenate([t[:, None], np.cos((ff * ww).astype(f64)), -np.sin((ff * ww).astype(f64))], axis=1)
    return (tab.astype(f32), np.ascontiguousarray(decay.astype(f32)), np.ascontiguousarray(zz.T.astype(f32)))


def trunk_kernel(nc, t, out):
    with ExitStack() as ctx:
        def sb(name, shape, dt=F32):
            return ctx.enter_context(nc.sbuf_tensor(name, shape, dt))

        def sem(name):
            return ctx.enter_context(nc.semaphore(name))

        ring = [sb(f"ring{r}", [P, 8 * W]) for r in range(RING)]
        cst = sb("cst", [P, C_ALL])
        x = sb("x", [P, NT, D])
        xn = sb("xn", [P, NT, D])
        hT = sb("hT", [P, ND, SEQ])
        g1b = sb("g1b", [P, D])
        g2b = sb("g2b", [P, D])
        Kr = sb("Kr", [P, 2, HY])
        Ks = sb("Ks", [P, 2, HY])
        KX = sb("KX", [P, HY])
        x0T = sb("x0T", [P, NH_CH, SEQ])
        zvT = sb("zvT", [P, NH_CH, SEQ])
        router = sb("router", [P, ND, NE])
        rbias = sb("rbias", [P, NE])
        cpad = sb("cpad", [P, ND, 32])
        vrow = sb("vrow", [P, P])
        brow = sb("brow", [6 * ND, P])
        hrow = sb("hrow", [4, FFN])
        vT = sb("vT", [P, R_ALL])
        bT = sb("bT", [P, 6 * ND])
        hvT = sb("hvT", [FFN, 4])
        modT = sb("modT", [P, 6 * ND])
        A1 = sb("A1", [P, ND])
        A2 = sb("A2", [P, ND])
        hw1 = sb("hw1", [EMB, FFN])
        hw2 = sb("hw2", [FFN, FFN])
        hw3 = sb("hw3", [FFN, FFN])
        ss = sb("ss", [P, NT])
        rs = sb("rs", [P, NT])
        eps = sb("eps", [P, 1])
        stat = sb("stat", [P, 12, 32])
        crow = stat[0:ND, 8:12, :].rearrange("k a b -> k (a b)")
        yatT = sb("yatT", [P, 2, SEQ])
        cnt_i = sb("cnt_i", [P, PAIRS], I32)
        side_i = sb("side_i", [P, PAIRS], I32)
        AREA = 6656
        area = sb("area", [P, AREA])

        cut = [0]

        def region(size):
            a = area[:, cut[0]:cut[0] + size]
            cut[0] += size
            assert cut[0] <= AREA, cut[0]
            return a

        decay = region(2 * NT * HY).rearrange("p (b t c) -> p b t c", b=2, t=NT)
        fu = region(SEQ)
        fk = region(SEQ)
        fh = region(SEQ)
        zpos = yatT[:, 0, :]
        hw4 = region(2 * HY)[0:FFN, :]
        cut[0] = 0
        qr = region(GROUPS * 2 * SEQ).rearrange("p (g x n) -> p g x n", g=GROUPS, x=2)
        kr = region(GROUPS * 2 * SEQ).rearrange("p (g x n) -> p g x n", g=GROUPS, x=2)
        vv = region(NT * HY).rearrange("p (t n) -> p t n", t=NT)
        qm = xn[:, :, :].rearrange("p t d -> p (t d)").rearrange("p (x h n) -> p x h n", x=2, h=HPG)
        sm_0 = region(2 * SEQ).rearrange("p (t n) -> p t n", t=NT)
        tmp = region(2 * SEQ)
        sm = [sm_0, tmp.rearrange("p (t n) -> p t n", t=NT)]
        acc = area[:, cut[0]:cut[0] + 2 * W].rearrange("p (b n) -> p b n", b=2)
        pT = region(2 * SEQ).rearrange("p (t n) -> p t n", t=NT)
        yat = region(NT * GW).rearrange("p (t n) -> p t n", t=NT)
        cut[0] = 0
        ztok = region(NT * HY).rearrange("p (t c) -> p t c", t=NT)
        Yr = region(2 * HY).rearrange("p (m c) -> p m c", m=2)
        Ys = region(2 * HY).rearrange("p (m c) -> p m c", m=2)
        ct = [region(HW2) for _ in range(4)]
        cut[0] = 0
        merged = region(NT * D).rearrange("p (t d) -> p t d", t=NT)
        mT = xn[:, :, :].rearrange("p t d -> p (t d)").rearrange("p (k n) -> p k n", k=ND)
        sg = region(2 * NT * W).rearrange("p (b t n) -> p b t n", b=2, t=NT)
        mtmp = region(W)
        cut[0] = 0
        hg = hT[:, :, 0:P]
        hg_x = hT[:, :, P:2 * P]
        sel = region(NT * P).rearrange("p (t s) -> p t s", t=NT)
        selg = region(NT * P).rearrange("p (t s) -> p t s", t=NT)
        selT = region(SEQ)
        sil = region(FE)
        act = region(FE)
        actT = region(FE).rearrange("p (f s) -> p f s", f=NF)
        yS = region(D)
        posc = region(NT * 2).rearrange("p (t j) -> p t j", t=NT)
        gatec = region(NT * 2).rearrange("p (t j) -> p t j", t=NT)
        rt_at = cut[0]
        rt = [region(NT * NE) for _ in range(13)]
        rb = [r.rearrange("p (t e) -> p t e", t=NT) for r in rt]
        g4 = [r.rearrange("p (t g e) -> p t g e", t=NT, g=NG) for r in rt]
        score, biased, pair, tA, tB, oh1, oh2, oh, tC, tD, gate_, pos_, tE = range(13)

        def row(i, tt):
            a = rt_at + (i * NT + tt) * NE
            return area[:, a:a + NE + 4]

        Krf = Kr[:, :, :].rearrange("p m c -> p (m c)")
        yS_x = Krf[:, 0:D]
        selT_x = Krf[:, D:D + SEQ]
        posc_x = Krf[:, D + SEQ:D + SEQ + 2 * NT].rearrange("p (t j) -> p t j", t=NT)
        gatec_x = Krf[:, D + SEQ + 2 * NT:D + SEQ + 4 * NT].rearrange("p (t j) -> p t j", t=NT)
        sel_x = KX[:, 0:NT * P].rearrange("p (t s) -> p t s", t=NT)
        selg_x = KX[:, NT * P:2 * NT * P].rearrange("p (t s) -> p t s", t=NT)
        buf_m = (sel, selg, selT, yS, posc, gatec, hg)
        buf_x = (sel_x, selg_x, selT_x, yS_x, posc_x, gatec_x, hg_x)
        fing = g1b[:, :]

        bank = [ctx.enter_context(nc.psum_tensor(f"bank{i}", [P, 512], F32)) for i in range(8)]

        ident = cst[:, C_ID:C_ID + P]
        ctab = cst[:, C_CT:C_CT + NT * SEQ].rearrange("p (t f) -> p t f", t=NT)
        stab = cst[:, C_ST:C_ST + NT * SEQ].rearrange("p (t f) -> p t f", t=NT)
        ictab = cst[:, C_IC:C_IC + NT * SEQ].rearrange("p (t f) -> p t f", t=NT)
        istab = cst[:, C_IS:C_IS + NT * SEQ].rearrange("p (t f) -> p t f", t=NT)
        rcos = cst[:, C_COS:C_COS + SEQ]
        rsin = cst[:, C_SIN:C_SIN + 2 * SEQ]
        tri = cst[:, C_TRI:C_TRI + P]
        ones = cst[:, C_ONE:C_ONE + P]
        iota = cst[:, C_IOTA:C_IOTA + CAP]
        desc = cst[:, C_DESC:C_DESC + NE]
        fold = cst[:, C_FOLD:C_FOLD + FEW]

        def mask(g, qt):
            c = C_MASK + (qt if g == 0 else NT + g - 1) * SEQ
            return cst[:, c:c + SEQ]

        slot_in = [sem(f"slot_in{r}") for r in range(RING)]
        slots_free = sem("slots_free")
        s_start = sem("s_start")
        s_small = sem("s_small")
        s_filter = sem("s_filter")
        s_gbias = sem("s_gbias")
        s_out = sem("s_out")
        s_fing = sem("s_fing")
        v_chain = sem("v_chain")
        v_ovf = sem("v_ovf")
        a_chain = sem("a_chain")
        p_c = sem("p_c")
        v_c = sem("v_c")
        a_c = sem("a_c")
        p_vec = sem("p_vec")
        v_vec = sem("v_vec")
        v_ada = sem("v_ada")
        p_mod = sem("p_mod")
        v_mod = sem("v_mod")
        v_A1 = sem("v_A1")
        v_A2 = sem("v_A2")
        p_fil = sem("p_fil")
        v_fu = sem("v_fu")
        a_fh = sem("a_fh")
        p_kt = sem("p_kt")
        v_kt = sem("v_kt")
        p_ks = sem("p_ks")
        a_ks = sem("a_ks")
        v_kx = sem("v_kx")
        a_sq = sem("a_sq")
        v_xn = sem("v_xn")
        p_tr = sem("p_tr")
        v_hT = sem("v_hT")
        p_u = sem("p_u")
        a_u = sem("a_u")
        v_u = sem("v_u")
        p_qk = sem("p_qk")
        v_qk = sem("v_qk")
        p_v = sem("p_v")
        a_v = sem("a_v")
        g_qm = sem("g_qm")
        v_qm = sem("v_qm")
        p_s = sem("p_s")
        v_s = sem("v_s")
        a_p = sem("a_p")
        p_pt = sem("p_pt")
        a_pt = sem("a_pt")
        p_o = sem("p_o")
        v_md = sem("v_md")
        a_me = sem("a_me")
        v_yat = sem("v_yat")
        p_yat = sem("p_yat")
        a_yat = sem("a_yat")
        p_zt = sem("p_zt")
        a_zt = sem("a_zt")
        p_z = sem("p_z")
        v_z = sem("v_z")
        p_y = sem("p_y")
        v_y = sem("v_y")
        p_gate = sem("p_gate")
        a_gate = sem("a_gate")
        p_br = sem("p_br")
        v_br = sem("v_br")
        p_mt = sem("p_mt")
        a_mt = sem("a_mt")
        p_wo = sem("p_wo")
        v_wo = sem("v_wo")
        p_lg = sem("p_lg")
        a_lg = sem("a_lg")
        v_oh = sem("v_oh")
        p_pos = sem("p_pos")
        v_rt = sem("v_rt")
        v_layer = sem("v_layer")
        v_fin = sem("v_fin")

        def block_sems(tag):
            return {n: sem(f"{n}_{tag}") for n in (
                "v_pos", "v_sel", "p_selT", "p_hg", "a_selT", "a_hg", "v_hg", "p_up", "a_sil", "v_act", "p_actT", "a_actT",
                "v_actT", "p_down", "v_yS", "p_sc", "v_acc")}

        def skip(eng, signals, at, times):
            for name, k in signals.items():
                at.wait_before(eng, name)
                eng.sem_inc(at.s[name], times * k)

        def first_credit(eng, signals):
            for sems in (main, ovf):
                for name in signals:
                    eng.sem_inc(sems[name], CREDIT)

        CREDIT = 4
        main = block_sems("m")
        ovf = block_sems("x")
        PE_SIGNALS = {"p_selT": 1, "p_hg": 2, "p_up": 2, "p_actT": 1, "p_down": 2, "p_sc": 4}
        ACT_SIGNALS = {"a_selT": 1, "a_hg": 1, "a_sil": 1, "a_actT": 1}
        DVE_SIGNALS = {"v_pos": 1, "v_sel": 1, "v_hg": 1, "v_act": 1, "v_actT": 1, "v_yS": 1, "v_acc": 4}
        SIGNALS = {**PE_SIGNALS, **ACT_SIGNALS, **DVE_SIGNALS}

        class At:
            def __init__(self, sems, n):
                self.s, self.n = sems, n

            def wait(self, eng, name, k=None):
                k = SIGNALS[name] if k is None else k
                eng.wait_ge(self.s[name], self.n * SIGNALS[name] + (k + CREDIT))

            def wait_before(self, eng, name):
                eng.wait_ge(self.s[name], self.n * SIGNALS[name] + CREDIT)

        def ada_after(c):
            return N_EARLY + (c - 3) // 2

        assert ada_after(NSC - 1) == N_ADA - 1

        stream = [("ada", b) for b in range(N_EARLY)]
        for c in range(NSC):
            if c % 4 == 3:
                stream.append(("in", c // 4))
            if c % 2 and c >= 3:
                stream.append(("ada", ada_after(c)))
        stream += [("in", b) for b in range(NSC // 4, IN_A)]
        stream += [("in", 9), ("brh", 0), ("in", 10), ("brh", 1), ("in", 11), ("in", 12), ("bra", 0), ("out", 0), ("out", 1)]
        assert len(stream) == N_HEAD
        at_ = {key: n for n, key in enumerate(stream)}

        def taps_after(c):
            return range(2 * c, 2 * c + 2) if c < 4 else ()

        def spectra_after(c):
            return range(2 * (c - C_SPEC), 2 * (c - C_SPEC) + 2) if C_SPEC <= c < C_SPEC + 4 else ()

        s_settled = sem("s_settled")

        def settle(eng):
            eng.sem_inc(s_settled, 1)

        block = ctx.enter_context(nc.Block())

        @block.sync
        def _(sp):
            sp.sem_inc(slots_free, RING)
            with sp.Fori(0, DEPTH) as L:
                def load(n, dst, src):
                    sp.wait_ge(slots_free, L * N_BLOCKS + (n + 1))
                    sp.dma_start(dst, src).then_inc(slot_in[n % RING], 16)

                for n, (kind, b) in enumerate(stream):
                    if n == 1:
                        sp.wait_ge(s_small, (L + 1) * (16 * N_SMALL))
                        sp.sem_inc(s_settled, 1)
                    if n == N_EARLY + 1:
                        sp.wait_ge(s_filter, (L + 1) * 32)
                        sp.sem_inc(s_settled, 1)
                    if kind == "bra":
                        load(n, ring[n % RING][:, 0:2 * D].rearrange("p (k f) -> p k f", f=D),
                             t["w_br_a"][L, :, :].rearrange("(k p) f -> p k f", p=P))
                    elif kind == "brh":
                        load(n, ring[n % RING][:, 0:NH_CH * W].rearrange("p (k f) -> p k f", f=W),
                             t["w_br_h"][L, :, b * W:(b + 1) * W].rearrange("(k p) f -> p k f", p=P))
                    else:
                        src = {"ada": t["w_ada"], "in": t["w_in"], "out": t["w_out"]}[kind]
                        load(n, ring[n % RING][:, :].rearrange("p (k f) -> p k f", f=W),
                             src[L, :, b * W:(b + 1) * W].rearrange("(k p) f -> p k f", p=P))
                with sp.Fori(0, PAIRS) as pr:
                    for j in range(BPP):
                        name = ("moe_w1", "moe_w3", "moe_w2")[j // 2]
                        f = FE if j < 4 else D
                        sp.wait_ge(slots_free, L * N_BLOCKS + pr * BPP + (N_HEAD + j + 1))
                        sp.dma_start(ring[j][:, :].rearrange("p (k f) -> p k f", f=f),
                                     t[name][L, pr * 2 + j % 2, :, :].rearrange("(k p) f -> p k f", p=P))\
                          .then_inc(slot_in[j], 16)

        @block.gpsimd
        def _(pool):
            with pool.Fori(0, DEPTH) as L:
                loads = [
                    (vrow[R_N1:R_N1 + ND, :], t["norm1_g"][L, :].rearrange("(k p) -> k p", p=P)),
                    (vrow[R_N2:R_N2 + ND, :], t["norm2_g"][L, :].rearrange("(k p) -> k p", p=P)),
                    (vrow[R_WSC:R_BSC, :], t["w_sc"][L, :, :].rearrange("j (k p) -> (j k) p", p=P)),
                    (vrow[R_BSC:R_HYB, :], t["b_sc"][L, :].rearrange("(k p) -> k p", p=P)),
                    (vrow[R_HYB:R_ALL, :], t["hy_bias"][L, :].rearrange("(k p) -> k p", p=P)),
                    (brow[:, :], t["b_ada"][L, :].rearrange("(k p) -> k p", p=P)),
                    (hrow[0:1, :], t["hf_b1"][L, :].rearrange("(a n) -> a n", a=1)),
                    (hrow[1:2, :], t["hf_b2"][L, :].rearrange("(a n) -> a n", a=1)),
                    (hrow[2:3, :], t["hf_b3"][L, :].rearrange("(a n) -> a n", a=1)),
                    (hrow[3:4, :], t["hf_freq"][L, :].rearrange("(a n) -> a n", a=1)),
                    (hw1[:, :], t["hf_w1"][L, :, :]),
                    (hw2[:, :], t["hf_w2"][L, :, :]),
                    (hw3[:, :], t["hf_w3"][L, :, :]),
                    (zpos[0:EMB, :], t["zpos"]),
                ]
                assert len(loads) == N_SMALL
                for dst, src in loads:
                    pool.dma_start(dst, src).then_inc(s_small, 16)
                pool.wait_ge(slot_in[0], (L * PER_SLOT + 1) * 16)
                pool.wait_ge(v_layer, L + 1)
                settle(pool)
                pool.dma_start(decay, t["decay"]).then_inc(s_filter, 16)
                pool.dma_start(hw4, t["hf_w4"][L, :, :]).then_inc(s_filter, 16)
                for n, g in ((2, g1b), (5, g2b)):
                    pool.dma_start(g[:, :], t["b_ada"][L, n * D:(n + 1) * D].rearrange("(a n) -> a n", a=1)
                                   .to_broadcast([P, D])).then_inc(s_gbias, 16)
                pool.wait_ge(p_tr, L * 8 + 4)
                settle(pool)
                pool.memset(qm, 0.0).then_inc(g_qm, 1)
                pool.wait_ge(p_br, (L + 1) * 8)
            pool.wait_ge(s_out, 16 * NT)

        @block.tensor
        def _(pe):
            def mm(dst, lhsT, rhs, start, stop):
                return pe.matmul(dst, lhsT, rhs, start=start, stop=stop, skip_group_check=True)

            first_credit(pe, PE_SIGNALS)
            pe.wait_ge(s_start, 16 * N_START)
            pe.transpose(bank[0][:, 0:ND], crow, ident[0:ND, 0:ND]).then_inc(p_c, 1)
            pe.wait_ge(v_c, 2)

            def free_after(done, value, n=1):
                pe.wait_ge(done, value)
                pe.sem_inc(slots_free, n)

            with pe.Fori(0, DEPTH) as L:
                def landed(n):
                    pe.wait_ge(slot_in[n % RING], (L * PER_SLOT + (n // RING + 1)) * 16)
                    return ring[n % RING]

                def block_of(kind, b):
                    return landed(at_[kind, b])[:, :].rearrange("p (k f) -> p k f", f=W)

                pe.wait_ge(s_small, (L + 1) * (16 * N_SMALL))
                pe.wait_ge(v_layer, L + 1)
                pe.transpose(bank[6][:, 0:R_ALL], vrow[0:R_ALL, :], ident[0:R_ALL, 0:R_ALL])
                pe.transpose(bank[6][:, P:P + 6 * ND], brow[:, :], ident[0:6 * ND, 0:6 * ND])
                pe.transpose(bank[6][0:FFN, 2 * P:2 * P + 4], hrow[:, :], ident[0:4, 0:4]).then_inc(p_vec, 1)

                def ada_post(n):
                    pe.wait_ge(v_ada, L * N_ADA + n + 1)
                    if n // 2 in (2, 5):
                        q = (n // 2 == 5) * 2 + n % 2
                        if q >= 1:
                            pe.wait_ge(v_mod, L * 4 + q)
                        mm(bank[7][:, :], ones, acc[:, n % 2, :], True, True).then_inc(p_mod, 1)
                    else:
                        for j in range(4):
                            last = mm(bank[6][:, n * 4 + j:n * 4 + j + 1], acc[:, n % 2, j * P:(j + 1) * P],
                                      ones[:, 0:1], True, True)
                        last.then_inc(p_mod, 1)

                def ada(n):
                    w = block_of("ada", n)
                    if n >= 2:
                        pe.wait_ge(v_ada, L * N_ADA + n - 1)
                    for h in range(2):
                        for j in range(4):
                            k = h * 4 + j
                            last = mm(bank[4 + n % 2][32 * j:32 * j + 32, :], cpad[:, k, :], w[:, k, :], h == 0, h == 1)
                    last.then_inc(slots_free, 1)

                pe.wait_ge(v_vec, (L + 1) * 3)
                settle(pe)
                mm(bank[7][0:FFN, 0:SEQ], hw1[:, :], zpos[0:EMB, :], True, True).then_inc(p_fil, 1)
                ada(0)
                ada(1)
                for s, w in ((1, hw2), (2, hw3)):
                    pe.wait_ge(a_fh, L * 3 + s)
                    settle(pe)
                    mm(bank[7][0:FFN, 0:SEQ], w[:, :], fh[0:FFN, :], True, True).then_inc(p_fil, 1)
                    ada_post(2 * s - 2)
                    if s == 1:
                        ada(2)
                        ada_post(1)
                        ada(3)
                    else:
                        ada_post(3)
                def transposes_to_h(q):
                    pe.wait_ge(v_xn, L * 2 + q + 1)
                    for k in range(ND):
                        for tt in range(NT):
                            last = pe.transpose(bank[k // 2][:, (k % 2) * SEQ + tt * P:(k % 2) * SEQ + (tt + 1) * P],
                                                xn[:, tt, k * P:(k + 1) * P], ident)
                        if k % 2:
                            last.then_inc(p_tr, 1)

                transposes_to_h(0)

                def taps(u):
                    if u == 0:
                        pe.wait_ge(a_fh, (L + 1) * 3)
                        pe.wait_ge(s_filter, (L + 1) * 32)
                    b, lt, n = u // (2 * NT), u // 2 % NT, u % 2
                    if u >= 2:
                        pe.wait_ge(v_kt, L * 10 + u - 1)
                    mm(bank[2 + n][:, 0:HW2], fh[0:FFN, lt * P:(lt + 1) * P],
                       hw4[:, b * HY + n * HW2:b * HY + (n + 1) * HW2], True, True).then_inc(p_kt, 1)

                def spectrum(u):
                    b, m, n = u // 4, u // 2 % 2, u % 2
                    if u < 2:
                        pe.wait_ge(v_kt, (L + 1) * 10)
                    else:
                        pe.wait_ge(a_ks, L * 8 + u - 1)
                    for lt in range(NT):
                        last = mm(bank[2 + n][:, 0:HW2], (ctab, stab)[b][:, lt, m * P:(m + 1) * P],
                                  decay[:, b, lt, n * HW2:(n + 1) * HW2], lt == 0, lt == NT - 1)
                    last.then_inc(p_ks, 1)

                def nyquist():
                    pe.wait_ge(a_ks, (L + 1) * 8)
                    for n in range(2):
                        for lt in range(NT):
                            last = mm(bank[2 + n][0:1, 0:HW2], stab[:, lt, 0:1],
                                      decay[:, 0, lt, n * HW2:(n + 1) * HW2], lt == 0, lt == NT - 1)
                    last.then_inc(p_ks, 1)

                for c in range(NSC):
                    w = block_of("in", c // 4)
                    if c >= 2:
                        pe.wait_ge(v_u, L * NSC + c - 1)
                    for k in range(ND):
                        if c == 0 and k % 2 == 0:
                            pe.wait_ge(v_hT, L * 8 + k // 2 + 1)
                        last = mm(bank[c % 2][:, 0:SEQ], w[:, k, (c % 4) * P:(c % 4 + 1) * P], hT[:, k, :],
                                  k == 0, k == ND - 1)
                    last.then_inc(p_u, 1)
                    if c % 4 == 3:
                        free_after(p_u, L * NSC + c + 1)
                    if c % 2 and c >= 3:
                        ada(ada_after(c))
                        if c > 3:
                            ada_post(ada_after(c) - 1)
                    for u in taps_after(c):
                        taps(u)
                    for u in spectra_after(c):
                        spectrum(u)
                    if c == C_NYQ:
                        nyquist()
                for g in range(2 * GROUPS):
                    col = NSC * P + g * GW
                    b, o = col // W, col % W
                    w = block_of("in", b)
                    if g >= 2:
                        pe.wait_ge(v_qk, L * 6 + g - 1)
                    for xx in range(2):
                        for k in range(ND):
                            for hh in range(HPG):
                                a = o + hh * HD + xx * HALF
                                last = mm(bank[4 + g % 2][hh * HALF:(hh + 1) * HALF, xx * SEQ:(xx + 1) * SEQ],
                                          w[:, k, a:a + HALF], hT[:, k, :], k == 0, k == ND - 1)
                    last.then_inc(p_qk, 1)
                    if o + GW == W:
                        free_after(p_qk, L * 6 + g + 1)
                    if g == 0:
                        ada_post(N_ADA - 1)
                pe.wait_ge(v_mod, (L + 1) * 4)
                pe.wait_ge(v_A2, L + 1)
                for tt in range(NT):
                    for half in range(2):
                        b, o, n = (7, GW, GW) if half == 0 else (8, 0, W)
                        w = block_of("in", b)
                        for k in range(ND):
                            last = mm(bank[6 + half][:, 0:n], hT[:, k, tt * P:(tt + 1) * P], w[:, k, o:o + n],
                                      k == 0, k == ND - 1)
                        last.then_inc(p_v, 1)
                    if tt == 0:
                        pe.wait_ge(a_v, L * 4 + 2)
                free_after(p_v, L * 4 + 4, 2)

                pe.wait_ge(v_kx, (L + 1) * 2)
                pe.wait_ge(v_u, (L + 1) * NSC)
                pe.wait_ge(v_qk, (L + 1) * 6)
                pe.wait_ge(a_v, (L + 1) * 4)

                def scores(h):
                    g = h // HPG
                    pe.wait_ge(v_qm, L * GROUPS + g + 1)
                    if h >= 2:
                        pe.wait_ge(v_s, L * HEADS + h - 1)
                    for qt in range(NT):
                        for xx in range(2):
                            last = mm(bank[h % 2][:, qt * SEQ:(qt + 1) * SEQ], qm[:, xx, h % HPG, qt * P:(qt + 1) * P],
                                      kr[:, g, xx, :], xx == 0, xx == 1)
                    last.then_inc(p_s, 1)

                def attend(h):
                    pe.wait_ge(a_p, L * HEADS + h + 1)
                    if h >= 2:
                        pe.wait_ge(a_pt, L * HEADS + h - 1)
                    for qt in range(NT):
                        for kt in range(NT):
                            last = pe.transpose(bank[2 + h % 2][:, kt * SEQ + qt * P:kt * SEQ + (qt + 1) * P],
                                                sm[h % 2][:, qt, kt * P:(kt + 1) * P], ident)
                    last.then_inc(p_pt, 1)

                def values(h):
                    pe.wait_ge(a_pt, L * HEADS + h + 1)
                    for qt in range(NT):
                        for kt in range(NT):
                            last = mm(bank[4 + 2 * qt + h // 8][:, (h % 8) * HD:(h % 8 + 1) * HD],
                                      pT[:, kt, qt * P:(qt + 1) * P], vv[:, kt, h * HD:(h + 1) * HD],
                                      kt == 0, kt == NT - 1)
                    last.then_inc(p_o, 1)

                scores(0)
                for h in range(HEADS):
                    if h + 1 < HEADS:
                        scores(h + 1)
                    if h:
                        values(h - 1)
                    attend(h)
                values(HEADS - 1)
                pe.wait_ge(v_yat, L + 1)
                for c in range(2):
                    for tt in range(NT):
                        last = pe.transpose(bank[0][:, c * SEQ + tt * P:c * SEQ + (tt + 1) * P],
                                            yat[:, tt, c * P:(c + 1) * P], ident)
                last.then_inc(p_yat, 1)

                for tt in range(NT):
                    for half in range(2):
                        for j in range(3):
                            c = half * 3 + j
                            last = pe.transpose(bank[1 + tt * 2 + half][:, j * P:(j + 1) * P],
                                                zvT[:, c, tt * P:(tt + 1) * P], ident)
                        last.then_inc(p_zt, 1)
                pe.wait_ge(a_zt, (L + 1) * 4)
                u = 0
                for m in range(2):
                    for n in range(2):
                        if u >= 2:
                            pe.wait_ge(v_z, L * 4 + u - 1)
                        if u == 0:
                            pe.wait_ge(a_yat, L + 1)
                        for s, tab in enumerate((ctab, stab)):
                            for tt in range(NT):
                                last = mm(bank[2 * (u % 2) + s][:, 0:HW2], tab[:, tt, m * P:(m + 1) * P],
                                          ztok[:, tt, n * HW2:(n + 1) * HW2], tt == 0, tt == NT - 1)
                        last.then_inc(p_z, 1)
                        u += 1
                pe.wait_ge(v_z, (L + 1) * 4)
                for c in range(NH_CH):
                    if c >= 4:
                        pe.wait_ge(v_y, L * NH_CH + c - 3)
                    q = 0
                    for spec, tab in ((Yr, ictab), (Ys, istab)):
                        for m in range(2):
                            last = mm(bank[4 + c % 4][:, 0:SEQ], spec[:, m, c * P:(c + 1) * P], tab[:, m, :],
                                      q == 0, q == 3)
                            q += 1
                    last.then_inc(p_y, 1)

                def gate(q):
                    w = block_of("in", IN_A + q)
                    for tt in range(NT):
                        if q >= 1:
                            pe.wait_ge(a_gate, L * 8 + 2 * q + tt - 1)
                        for k in range(ND):
                            last = mm(bank[tt][:, :], hT[:, k, tt * P:(tt + 1) * P], w[:, k, :], k == 0, k == ND - 1)
                        last.then_inc(p_gate, 1)
                    free_after(p_gate, L * 8 + 2 * q + 2)

                def branch(q, w, src, ks, o):
                    for tt in range(NT):
                        if q >= 1:
                            pe.wait_ge(v_br, L * 8 + 2 * q + tt - 1)
                        for k in range(ks):
                            last = mm(bank[2 + tt][:, :], src[:, k, tt * P:(tt + 1) * P], w[:, k, o:o + W],
                                      k == 0, k == ks - 1)
                        last.then_inc(p_br, 1)

                pe.wait_ge(v_y, (L + 1) * NH_CH)
                for q in range(2):
                    gate(q)
                    wv = landed(at_["brh", q])[:, 0:NH_CH * W].rearrange("p (k f) -> p k f", f=W)
                    branch(q, wv, x0T, NH_CH, 0)
                    free_after(p_br, L * 8 + 2 * q + 2)
                gate(2)
                gate(3)
                wv = landed(at_["bra", 0])[:, 0:2 * D].rearrange("p (k f) -> p k f", f=D)
                branch(2, wv, yatT, 2, 0)
                branch(3, wv, yatT, 2, W)
                free_after(p_br, L * 8 + 8)
                for k in range(ND):
                    if k % 4 == 0:
                        pe.wait_ge(v_br, L * 8 + 6 + k // 2)
                    for tt in range(NT):
                        last = pe.transpose(bank[4 + k // 2][:, (k % 2) * SEQ + tt * P:(k % 2) * SEQ + (tt + 1) * P],
                                            merged[:, tt, k * P:(k + 1) * P], ident)
                    if k % 2:
                        last.then_inc(p_mt, 1)
                for n in range(2):
                    w = block_of("out", n)
                    for tt in range(NT):
                        for k in range(ND):
                            if n == 0 and tt == 0 and k % 2 == 0:
                                pe.wait_ge(a_mt, L * 4 + k // 2 + 1)
                            last = mm(bank[2 * n + tt][:, :], mT[:, k, tt * P:(tt + 1) * P], w[:, k, :],
                                      k == 0, k == ND - 1)
                        last.then_inc(p_wo, 1)
                    free_after(p_wo, L * 4 + 2 * n + 2)

                pe.wait_ge(v_wo, (L + 1) * 4)
                transposes_to_h(1)
                pe.wait_ge(v_hT, (L + 1) * 8)
                for tt in range(NT):
                    for k in range(ND):
                        last = mm(bank[4][:, tt * NE:(tt + 1) * NE], hT[:, k, tt * P:(tt + 1) * P], router[:, k, :],
                                  k == 0, k == ND - 1)
                last.then_inc(p_lg, 1)
                pe.wait_ge(v_oh, L + 1)
                mm(bank[5][:, 0:NE], tri, rb[oh][:, 0, :], True, True)
                mm(bank[5][:, NE:2 * NE], ones, rb[oh][:, 0, :], True, False)
                mm(bank[5][:, NE:2 * NE], tri, rb[oh][:, 1, :], False, True)
                mm(bank[5][:, 2 * NE:3 * NE], ones, rb[oh][:, 0, :], True, False)
                mm(bank[5][:, 2 * NE:3 * NE], ones, rb[oh][:, 1, :], False, True).then_inc(p_pos, 1)
                pe.wait_ge(v_rt, L + 1)
                settle(pe)

                def gather(at, buf):
                    at.wait(pe, "v_sel")
                    for k in range(ND):
                        for tt in range(NT):
                            last = mm(bank[2 + k // 4][:, (k % 4) * P:(k % 4 + 1) * P], xn[:, tt, k * P:(k + 1) * P],
                                      buf[0][:, tt, :], tt == 0, tt == NT - 1)
                        if k % 4 == 3:
                            last.then_inc(at.s["p_hg"], 1)

                def up(at, buf, arrived, last_use):
                    at.wait(pe, "a_hg")
                    for which in range(2):
                        arrived(2 * which)
                        arrived(2 * which + 1)
                        for k in range(ND):
                            if which == 0 and k == 4:
                                at.wait(pe, "v_hg")
                            for e in range(2):
                                w = ring[2 * which + e][:, :].rearrange("p (k f) -> p k f", f=FE)
                                last = mm(bank[which][CAP * e:CAP * (e + 1), :], buf[6][:, k, CAP * e:CAP * (e + 1)],
                                          w[:, k, :], k == 0, k == ND - 1)
                        last.then_inc(at.s["p_up"], 1)
                        if which == 0:
                            at.wait(pe, "p_up", 1)
                            settle(pe)
                            with pe.If(last_use):
                                pe.sem_inc(slots_free, 2)

                def turn(at, buf):
                    for tt in range(NT):
                        last = pe.transpose(bank[4][:, tt * P:(tt + 1) * P], buf[1][:, tt, :], ident)
                    last.then_inc(at.s["p_selT"], 1)
                    at.wait(pe, "v_act")
                    at.wait(pe, "v_actT")
                    for f in range(NF):
                        last = pe.transpose(bank[5][:, f * P:(f + 1) * P], act[:, f * P:(f + 1) * P], ident)
                    last.then_inc(at.s["p_actT"], 1)

                def down(at, arrived):
                    at.wait(pe, "a_actT")
                    arrived(4)
                    arrived(5)
                    for n in range(2):
                        for f in range(NF):
                            for e in range(2):
                                w = ring[4 + e][:, :].rearrange("p (k f) -> p k f", f=D)
                                last = mm(bank[6 + n][CAP * e:CAP * (e + 1), :], actT[:, f, CAP * e:CAP * (e + 1)],
                                          w[:, f, n * W:(n + 1) * W], f == 0, f == NF - 1)
                        last.then_inc(at.s["p_down"], 1)

                def light(at, buf, arrived, e):
                    at.wait(pe, "a_hg")
                    at.wait(pe, "v_hg")
                    for which in range(2):
                        arrived(2 * which + e)
                        w = ring[2 * which + e][:, :].rearrange("p (k f) -> p k f", f=FE)
                        for h in range(2):
                            for j in range(4):
                                k = h * 4 + j
                                last = mm(bank[which][FEW * j:FEW * (j + 1), :], buf[6][:, k, FEW * j:FEW * (j + 1)],
                                          w[:, k, :], h == 0, h == 1)
                        last.then_inc(at.s["p_up"], 1)
                    for tt in range(NT):
                        last = pe.transpose(bank[4][:, tt * P:(tt + 1) * P], buf[1][:, tt, :], ident)
                    last.then_inc(at.s["p_selT"], 1)
                    at.wait(pe, "a_sil")
                    at.wait(pe, "v_act")
                    for which, src in enumerate((sil, act)):
                        for f in range(NF):
                            c = (which * NF + f) * FEW
                            last = mm(bank[5][:, c:c + FEW], src[:, f * P:(f + 1) * P], fold, True, True)
                    last.then_inc(at.s["p_actT"], 1)
                    pe.sem_inc(slots_free, 4)
                    at.wait(pe, "v_actT")
                    arrived(4 + e)
                    w = ring[4 + e][:, :].rearrange("p (k f) -> p k f", f=D)
                    for n in range(2):
                        for f in range(NF):
                            last = mm(bank[6 + n][FEW * f:FEW * (f + 1), :], act[:, f * FEW:(f + 1) * FEW],
                                      w[:, f, n * W:(n + 1) * W], True, True)
                        last.then_inc(at.s["p_down"], 1)

                def scatter(at, buf):
                    at.wait(pe, "v_yS")
                    at.wait(pe, "a_selT")
                    for tt in (1, 0):
                        for n in range(2):
                            mm(bank[2 + 2 * tt + n][:, :], buf[2][:, tt * P:(tt + 1) * P],
                               buf[3][:, n * W:(n + 1) * W], True, True).then_inc(at.s["p_sc"], 1)

                gather(At(main, L * PAIRS), buf_m)
                with pe.Fori(0, PAIRS) as pr:
                    n = pe.value_load(cnt_i[0:1, bass.ds(pr, 1)], min_val=0, max_val=SEQ)
                    run = L * PAIRS + pr
                    at, before, after = At(main, run), At(main, run - 1), At(main, run + 1)

                    def arrived(j):
                        pe.wait_ge(slot_in[j], (L * PER_SLOT + pr + (N_HEAD // RING + 1)) * 16)

                    up(at, buf_m, arrived, n <= CAP)
                    with pe.If(pr > 0):
                        At(ovf, run * EXTRA).wait_before(pe, "v_acc")
                        scatter(before, buf_m)
                        before.wait(pe, "v_acc", 2)
                        settle(pe)
                    turn(at, buf_m)
                    with pe.If(n <= CAP):
                        pe.sem_inc(slots_free, 2)
                    down(at, arrived)
                    with pe.If(pr > 0):
                        before.wait(pe, "v_acc")
                        settle(pe)
                    with pe.If(pr < PAIRS - 1):
                        gather(after, buf_m)
                    with pe.If(n <= CAP):
                        skip(pe, PE_SIGNALS, At(ovf, run * EXTRA), EXTRA)
                    with pe.Else():
                        with pe.If(pr < PAIRS - 1):
                            after.wait(pe, "a_hg")
                            after.wait(pe, "v_hg")
                            settle(pe)
                        side = pe.value_load(side_i[0:1, bass.ds(pr, 1)], min_val=0, max_val=3)
                        ob = At(ovf, run * EXTRA)
                        with pe.If(side < 2):
                            ob.wait_before(pe, "v_acc")
                            gather(ob, buf_x)
                            at.wait(pe, "v_yS")
                            settle(pe)
                            with pe.If(side < 1):
                                light(ob, buf_x, arrived, 0)
                            with pe.Else():
                                light(ob, buf_x, arrived, 1)
                            scatter(ob, buf_x)
                            skip(pe, PE_SIGNALS, At(ovf, run * EXTRA + 1), EXTRA - 1)
                        with pe.Else():
                            with pe.Fori(0, EXTRA) as b:
                                ob = At(ovf, run * EXTRA + b)
                                with pe.If(n > b * CAP + CAP):
                                    ob.wait_before(pe, "v_acc")
                                    gather(ob, buf_x)
                                    up(ob, buf_x, arrived, n <= b * CAP + 2 * CAP)
                                    turn(ob, buf_x)
                                    with pe.If(n <= b * CAP + 2 * CAP):
                                        pe.sem_inc(slots_free, 2)
                                    at.wait(pe, "v_yS")
                                    settle(pe)
                                    down(ob, arrived)
                                    scatter(ob, buf_x)
                                    ob.wait(pe, "p_sc")
                                    settle(pe)
                                with pe.Else():
                                    skip(pe, PE_SIGNALS, ob, 1)
                    at.wait(pe, "p_down")
                    pe.sem_inc(slots_free, 2)
                At(ovf, (L + 1) * (PAIRS * EXTRA)).wait_before(pe, "v_acc")
                scatter(At(main, L * PAIRS + (PAIRS - 1)), buf_m)

        @block.scalar
        def _(sc):
            starts = [
                (cst[:, :], t["cst"]),
                (crow, t["c"][0, :].rearrange("(k p) -> k p", p=P)),
                (router[:, :, :], t["router_w"].rearrange("(k p) e -> p k e", p=P)),
                (rbias[:, :], t["router_bias"].rearrange("(a n) -> a n", a=1).to_broadcast([P, NE])),
                (x[:, 0, :], t["x"][0, 0:P, :]),
                (x[:, 1, :], t["x"][0, P:2 * P, :]),
            ]
            assert len(starts) == N_START
            for dst, src in starts:
                sc.dma_start(dst, src).then_inc(s_start, 16)
            first_credit(sc, ACT_SIGNALS)
            sc.wait_ge(p_c, 1)
            sc.activation(stat[:, 0, 0:ND], bank[0][:, 0:ND], ACT.Sigmoid).then_inc(a_c, 1)
            sc.wait_ge(s_start, 16 * N_START)

            with sc.Fori(0, DEPTH) as L:
                def squares(q):
                    for tt in range(NT):
                        if q == 1:
                            sc.wait_ge(v_wo, L * 4 + NT + tt + 1)
                        last = sc.activation((xn, merged)[q][:, tt, :], x[:, tt, :], ACT.Square, scale=D ** -0.5,
                                             accum_out=ss[:, tt:tt + 1])
                    last.then_inc(a_chain, 1)
                    sc.wait_ge(a_chain, L * 2 + q + 1)
                    sc.activation(rs[:, :], ss[:, :], ACT.Sqrt, bias=eps[:, :]).then_inc(a_sq, 1)

                sc.wait_ge(v_layer, L + 1)
                squares(0)
                for s in range(3):
                    sc.wait_ge(v_fu, L * 3 + s + 1)
                    sc.activation(fh[0:FFN, :], fu[0:FFN, :], ACT.Sin).then_inc(a_fh, 1)
                for c in range(NSC):
                    sc.wait_ge(p_u, L * NSC + c + 1)
                    if c >= 2 * NH_CH + 1:
                        sc.wait_ge(v_u, L * NSC + c)
                    dst = x0T[:, c, :] if c < NH_CH else zvT[:, c - NH_CH, :] if c < 2 * NH_CH else tmp[:, 0:SEQ]
                    sc.activation(dst, bank[c % 2][:, 0:SEQ], ACT.Identity,
                                  bias=vT[:, R_BSC + c:R_BSC + c + 1],
                                  scale=vT[:, R_WSC + NSC + c:R_WSC + NSC + c + 1]).then_inc(a_u, 1)
                    for u in spectra_after(c):
                        b, m, n = u // 4, u // 2 % 2, u % 2
                        sc.wait_ge(p_ks, L * 9 + u + 1)
                        sc.activation((Kr, Ks)[b][:, m, n * HW2:(n + 1) * HW2], bank[2 + n][:, 0:HW2], ACT.Copy)\
                          .then_inc(a_ks, 1)
                for tt in range(NT):
                    for half in range(2):
                        sc.wait_ge(p_v, L * 4 + 2 * tt + half + 1)
                        o, n = (0, GW) if half == 0 else (GW, W)
                        sc.activation(vv[:, tt, o:o + n], bank[6 + half][:, 0:n], ACT.Copy).then_inc(a_v, 1)
                for h in range(HEADS):
                    sc.wait_ge(v_s, L * HEADS + h + 1)
                    for qt in range(NT):
                        last = sc.activation(sm[h % 2][:, qt, :], sm[h % 2][:, qt, :], ACT.Exp,
                                             bias=stat[:, 2, h * NT + qt:h * NT + qt + 1], scale=SCALE,
                                             accum_out=stat[:, 1, h * NT + qt:h * NT + qt + 1])
                    last.then_inc(a_p, 1)
                    sc.wait_ge(p_pt, L * HEADS + h + 1)
                    if h >= 1:
                        sc.wait_ge(p_o, L * HEADS + h)
                    sc.activation(pT[:, :, :].rearrange("p t n -> p (t n)"), bank[2 + h % 2][:, :], ACT.Copy)\
                      .then_inc(a_pt, 1)
                sc.wait_ge(v_md, L + 1)
                sc.activation(stat[:, 4, 0:HEADS * NT], stat[:, 3, 0:HEADS * NT], ACT.Exp, scale=SCALE).then_inc(a_me, 1)
                sc.wait_ge(p_yat, L + 1)
                sc.activation(yatT[:, :, :].rearrange("p c n -> p (c n)"), bank[0][:, :], ACT.Copy).then_inc(a_yat, 1)
                for tt in range(NT):
                    for half in range(2):
                        sc.wait_ge(p_zt, L * 4 + 2 * tt + half + 1)
                        sc.activation(ztok[:, tt, half * HW2:(half + 1) * HW2],
                                      bank[1 + tt * 2 + half][:, 0:HW2], ACT.Copy).then_inc(a_zt, 1)
                for q in range(4):
                    if q >= 2:
                        sc.wait_ge(v_br, L * 8 + 2 * (q - 1))
                    for tt in range(NT):
                        sc.wait_ge(p_gate, L * 8 + 2 * q + tt + 1)
                        sc.activation(sg[:, q % 2, tt, :], bank[tt][:, :], ACT.Sigmoid).then_inc(a_gate, 1)
                for j in range(4):
                    sc.wait_ge(p_mt, L * 4 + j + 1)
                    sc.activation(mT[:, 2 * j:2 * j + 2, :].rearrange("p k n -> p (k n)"), bank[4 + j][:, :], ACT.Copy)\
                      .then_inc(a_mt, 1)
                squares(1)
                sc.wait_ge(p_lg, L + 1)
                sc.activation(rt[score], bank[4][:, 0:NT * NE], ACT.Sigmoid).then_inc(a_lg, 1)

                def rows_to_h(at, buf):
                    at.wait(sc, "p_hg", 1)
                    for k in range(4):
                        last = sc.activation(buf[6][:, k, :], bank[2][:, k * P:(k + 1) * P], ACT.Identity,
                                             bias=modT[:, 3 * ND + k:3 * ND + k + 1], scale=A2[:, k:k + 1])
                    last.then_inc(at.s["a_hg"], 1)

                def middle(at, buf):
                    at.wait(sc, "p_up", 1)
                    sc.activation(sil, bank[0][:, :], ACT.Silu).then_inc(at.s["a_sil"], 1)
                    at.wait(sc, "p_selT")
                    sc.activation(buf[2], bank[4][:, 0:SEQ], ACT.Copy).then_inc(at.s["a_selT"], 1)
                    at.wait(sc, "p_actT")
                    sc.activation(actT[:, :, :].rearrange("p f s -> p (f s)"), bank[5][:, :], ACT.Copy)\
                      .then_inc(at.s["a_actT"], 1)

                sc.wait_ge(v_rt, L + 1)
                rows_to_h(At(main, L * PAIRS), buf_m)
                with sc.Fori(0, PAIRS) as pr:
                    n = sc.value_load(cnt_i[0:1, bass.ds(pr, 1)], min_val=0, max_val=SEQ)
                    run = L * PAIRS + pr
                    at = At(main, run)
                    middle(at, buf_m)
                    with sc.If(pr < PAIRS - 1):
                        rows_to_h(At(main, run + 1), buf_m)
                    with sc.If(n <= CAP):
                        skip(sc, ACT_SIGNALS, At(ovf, run * EXTRA), EXTRA)
                    with sc.Else():
                        side = sc.value_load(side_i[0:1, bass.ds(pr, 1)], min_val=0, max_val=3)
                        ob = At(ovf, run * EXTRA)
                        with sc.If(side < 2):
                            rows_to_h(ob, buf_x)
                            ob.wait(sc, "p_up", 1)
                            sc.activation(sil, bank[0][:, :], ACT.Copy).then_inc(ob.s["a_sil"], 1)
                            ob.wait(sc, "p_selT")
                            sc.activation(buf_x[2], bank[4][:, 0:SEQ], ACT.Copy).then_inc(ob.s["a_selT"], 1)
                            ob.wait(sc, "p_actT")
                            sc.activation(sil[:, 0:NF * FEW], bank[5][:, 0:NF * FEW], ACT.Silu)\
                              .then_inc(ob.s["a_actT"], 1)
                            skip(sc, ACT_SIGNALS, At(ovf, run * EXTRA + 1), EXTRA - 1)
                        with sc.Else():
                            with sc.Fori(0, EXTRA) as b:
                                ob = At(ovf, run * EXTRA + b)
                                with sc.If(n > b * CAP + CAP):
                                    rows_to_h(ob, buf_x)
                                    middle(ob, buf_x)
                                    ob.wait(sc, "p_sc")
                                    settle(sc)
                                with sc.Else():
                                    skip(sc, ACT_SIGNALS, ob, 1)
            sc.wait_ge(v_layer, DEPTH + 1)
            sc.dma_start(fing, t["final_g"].rearrange("(a n) -> a n", a=1).to_broadcast([P, D])).then_inc(s_fing, 16)
            sc.wait_ge(v_layer, DEPTH + 1)
            for tt in range(NT):
                last = sc.activation(xn[:, tt, :], x[:, tt, :], ACT.Square, scale=D ** -0.5,
                                     accum_out=ss[:, tt:tt + 1])
            last.then_inc(a_chain, 1)
            sc.wait_ge(a_chain, 2 * DEPTH + 1)
            sc.activation(rs[:, :], ss[:, :], ACT.Sqrt, bias=eps[:, :]).then_inc(a_sq, 1)
            for tt in range(NT):
                sc.wait_ge(v_fin, tt + 1)
                sc.dma_start(out[0, tt * P:(tt + 1) * P, :], xn[:, tt, :]).then_inc(s_out, 16)
            sc.wait_ge(s_out, 16 * NT)

        @block.vector
        def _(dv):
            first_credit(dv, DVE_SIGNALS)
            dv.memset(eps[:, :], EPS).then_inc(v_layer, 1)
            dv.memset(cpad[:, :, :], 0.0).then_inc(v_c, 1)
            dv.wait_ge(a_c, 1)
            dv.wait_ge(v_c, 1)
            dv.tensor_tensor(cpad[:, :, 0:1].rearrange("p k a -> p (k a)"), bank[0][:, 0:ND], stat[:, 0, 0:ND], ALU.mult)\
              .then_inc(v_c, 1)
            dv.wait_ge(s_start, 16 * N_START)

            count = [0]

            def rsqrt(link):
                link(dv.reciprocal(rs[:, :], rs[:, :]))
                link(dv.tensor_scalar(ss[:, :], ss[:, :], EPS, -0.5, ALU.add, ALU.mult))
                link(dv.tensor_tensor(ss[:, :], ss[:, :], rs[:, :], ALU.mult))
                link(dv.tensor_tensor(ss[:, :], ss[:, :], rs[:, :], ALU.mult))
                link(dv.scalar_tensor_tensor(rs[:, :], ss[:, :], 1.5, rs[:, :], ALU.add, ALU.mult))

            with dv.Fori(0, DEPTH) as L:
                def link(ins):
                    count[0] += 1
                    ins.then_inc(v_chain, 1)
                    dv.wait_ge(v_chain, L * N_CHAIN + count[0])

                dv.wait_ge(p_vec, L + 1)
                dv.tensor_copy(vT[:, :], bank[6][:, 0:R_ALL]).then_inc(v_vec, 1)
                dv.tensor_copy(bT[:, :], bank[6][:, P:P + 6 * ND]).then_inc(v_vec, 1)
                dv.tensor_copy(hvT[:, :], bank[6][0:FFN, 2 * P:2 * P + 4]).then_inc(v_vec, 1)
                dv.wait_ge(v_vec, (L + 1) * 3)
                def ada_copy(n):
                    dv.wait_ge(slots_free, L * N_BLOCKS + (RING + at_["ada", n] + 1))
                    if n >= 2:
                        dv.wait_ge(p_mod, L * N_ADA + n - 1)
                    dv.tensor_copy(acc[:, n % 2, :], bank[4 + n % 2][:, :]).then_inc(v_ada, 1)

                def ada_gate(n):
                    if n // 2 in (2, 5):
                        g = g1b if n // 2 == 2 else g2b
                        cols = slice((n % 2) * W, (n % 2 + 1) * W)
                        dv.wait_ge(s_gbias, (L + 1) * 32)
                        dv.wait_ge(p_mod, L * N_ADA + n + 1)
                        dv.tensor_tensor(g[:, cols], bank[7][:, :], g[:, cols], ALU.add).then_inc(v_mod, 1)

                def norm(q, nsq):
                    dv.wait_ge(a_sq, nsq)
                    rsqrt(link)
                    for tt in range(NT):
                        last = dv.tensor_scalar(xn[:, tt, :], x[:, tt, :], rs[:, tt:tt + 1], None, ALU.mult)
                    return last

                def to_h(q, A, shift):
                    for j in range(4):
                        dv.wait_ge(p_tr, L * 8 + 4 * q + j + 1)
                        for k in (2 * j, 2 * j + 1):
                            last = dv.tensor_scalar(hT[:, k, :], bank[j][:, (k % 2) * SEQ:(k % 2 + 1) * SEQ],
                                                    A[:, k:k + 1], modT[:, shift + k:shift + k + 1], ALU.mult, ALU.add)
                        last.then_inc(v_hT, 1)

                u_, k_ = fu[0:FFN, :], fk[0:FFN, :]
                for s in range(3):
                    dv.wait_ge(p_fil, L * 3 + s + 1)
                    if s >= 1:
                        dv.wait_ge(a_fh, L * 3 + s)
                    link(dv.tensor_scalar(u_, bank[7][0:FFN, 0:SEQ], hvT[:, s:s + 1], hvT[:, 3:4], ALU.add, ALU.mult))
                    link(dv.tensor_scalar(k_, u_, INV2PI, MAGIC, ALU.mult, ALU.add))
                    link(dv.tensor_scalar(k_, k_, MAGIC, None, ALU.subtract))
                    link(dv.scalar_tensor_tensor(u_, k_, -TWOPI_HI, u_, ALU.mult, ALU.add))
                    link(dv.scalar_tensor_tensor(u_, k_, -TWOPI_LO, u_, ALU.mult, ALU.add))
                    dv.tensor_scalar(u_, u_, PI_SAFE, -PI_SAFE, ALU.min, ALU.max).then_inc(v_fu, 1)
                    if s < 2:
                        ada_copy(2 * s)
                        ada_copy(2 * s + 1)
                    if s == 0:
                        norm(0, L * 2 + 1).then_inc(v_xn, 1)
                dv.wait_ge(p_mod, L * N_ADA + N_EARLY)
                cols = slice(0, 2 * ND)
                link(dv.tensor_tensor(modT[:, cols], bank[6][:, cols], bT[:, cols], ALU.add))
                dv.scalar_tensor_tensor(A1[:, :], modT[:, ND:2 * ND], 1.0, vT[:, R_N1:R_N1 + ND], ALU.add, ALU.mult)\
                  .then_inc(v_A1, 1)
                dv.wait_ge(v_A1, L + 1)
                to_h(0, A1, 0)

                def decayed(u):
                    b, lt, n = u // (2 * NT), u // 2 % NT, u % 2
                    if u == 0:
                        dv.wait_ge(s_filter, (L + 1) * 32)
                    dv.wait_ge(p_kt, L * 8 + u + 1)
                    part = decay[:, b, lt, n * HW2:(n + 1) * HW2]
                    dv.tensor_tensor(part, bank[2 + n][:, 0:HW2], part, ALU.mult).then_inc(v_kt, 1)

                def directions():
                    dv.wait_ge(v_kt, L * 10 + 8)
                    dv.tensor_tensor(decay[:, 0, :, :], decay[:, 0, :, :], decay[:, 1, :, :], ALU.add).then_inc(v_kt, 1)
                    dv.wait_ge(v_kt, L * 10 + 9)
                    dv.scalar_tensor_tensor(decay[:, 1, :, :], decay[:, 1, :, :], -2.0, decay[:, 0, :, :],
                                            ALU.mult, ALU.add).then_inc(v_kt, 1)

                def nyquist_row():
                    dv.wait_ge(a_ks, (L + 1) * 8)
                    dv.wait_ge(p_ks, (L + 1) * 9)
                    link(dv.tensor_copy(KX[:, :], Kr[:, 0, :]))
                    for n in range(2):
                        last = dv.tensor_copy(KX[0:1, n * HW2:(n + 1) * HW2], bank[2 + n][0:1, 0:HW2])
                    last.then_inc(v_kx, 1)
                    dv.memset(Ks[0:1, 0, :], 0.0).then_inc(v_kx, 1)

                for c in range(NSC):
                    dv.wait_ge(a_u, L * NSC + c + 1)
                    dst = x0T[:, c, :] if c < NH_CH else zvT[:, c - NH_CH, :] if c < 2 * NH_CH else tmp[:, 0:SEQ]
                    src = bank[c % 2]
                    link(dv.scalar_tensor_tensor(dst[:, 1:SEQ], src[:, 0:SEQ - 1], vT[:, R_WSC + c:R_WSC + c + 1],
                                                 dst[:, 1:SEQ], ALU.mult, ALU.add))
                    w2c = R_WSC + 2 * NSC + c
                    last = dv.scalar_tensor_tensor(dst[:, 0:SEQ - 1], src[:, 1:SEQ], vT[:, w2c:w2c + 1],
                                                   dst[:, 0:SEQ - 1], ALU.mult, ALU.add)
                    if c >= 2 * NH_CH:
                        link(last)
                        z = zvT[:, c - 2 * NH_CH, :]
                        last = dv.tensor_tensor(z, z, dst, ALU.mult)
                    last.then_inc(v_u, 1)
                    if c % 2 and c >= 3:
                        ada_copy(ada_after(c))
                        if c > 3:
                            ada_gate(ada_after(c) - 1)
                    for u in taps_after(c):
                        decayed(u)
                    if c == 3:
                        directions()
                    if c == C_NYQ:
                        nyquist_row()
                ada_gate(N_ADA - 1)
                dv.wait_ge(p_mod, (L + 1) * N_ADA)
                cols = slice(3 * ND, 5 * ND)
                link(dv.tensor_tensor(modT[:, cols], bank[6][:, cols], bT[:, cols], ALU.add))
                dv.scalar_tensor_tensor(A2[:, :], modT[:, 4 * ND:5 * ND], 1.0, vT[:, R_N2:R_N2 + ND],
                                        ALU.add, ALU.mult).then_inc(v_A2, 1)
                dv.wait_ge(v_A2, L + 1)
                dv.wait_ge(v_u, (L + 1) * NSC)
                for g in range(2 * GROUPS):
                    dv.wait_ge(p_qk, L * 6 + g + 1)
                    dst = (qr if g < GROUPS else kr)[:, g % GROUPS, :, :]
                    src = bank[4 + g % 2]
                    tv = tmp.rearrange("p (x n) -> p x n", x=2)
                    for xx in range(2):
                        dv.tensor_tensor(dst[:, xx, :], src[:, xx * SEQ:(xx + 1) * SEQ], rcos, ALU.mult)
                    for xx in range(2):
                        last = dv.tensor_tensor(tv[:, xx, :], src[:, (1 - xx) * SEQ:(2 - xx) * SEQ],
                                                rsin[:, xx * SEQ:(xx + 1) * SEQ], ALU.mult)
                    link(last)
                    dv.tensor_tensor(dst, dst, tv, ALU.add).then_inc(v_qk, 1)
                    dv.wait_ge(v_qk, L * 6 + g + 1)
                dv.wait_ge(g_qm, L + 1)
                for h in range(HEADS):
                    g = h // HPG
                    if h % HPG == 0:
                        if h:
                            dv.wait_ge(p_s, L * HEADS + h)
                        for hh in range(HPG):
                            rows = slice(hh * HALF, (hh + 1) * HALF)
                            last = dv.tensor_copy(qm[rows, :, hh, :], qr[rows, g, :, :])
                        last.then_inc(v_qm, 1)
                    dv.wait_ge(p_s, L * HEADS + h + 1)
                    if h >= 2:
                        dv.wait_ge(p_pt, L * HEADS + h - 1)
                    settle(dv)
                    for qt in range(NT):
                        last = dv.tensor_tensor_reduce(out=sm[h % 2][:, qt, :], in0=bank[h % 2][:, qt * SEQ:(qt + 1) * SEQ],
                                                       in1=mask(g, qt), scale=1.0, scalar=-3e38, op0=ALU.add, op1=ALU.max,
                                                       accum_out=stat[:, 0, h * NT + qt:h * NT + qt + 1])
                    link(last)
                    dv.tensor_scalar(stat[:, 2, h * NT:(h + 1) * NT], stat[:, 0, h * NT:(h + 1) * NT], -SCALE, None,
                                     ALU.mult).then_inc(v_s, 1)
                n8 = HPG * NT
                m_ = stat[:, 0, 0:GROUPS * n8].rearrange("p (g a) -> p g a", g=GROUPS)
                d_ = stat[:, 3, 0:GROUPS * n8].rearrange("p (g a) -> p g a", g=GROUPS)
                e_ = stat[:, 4, 0:GROUPS * n8].rearrange("p (g a) -> p g a", g=GROUPS)
                s_ = stat[:, 1, 0:GROUPS * n8].rearrange("p (g a) -> p g a", g=GROUPS)
                w_ = stat[:, 5, 0:GROUPS * n8].rearrange("p (g a) -> p g a", g=GROUPS)
                M_ = stat[:, 6, 0:n8]
                dv.wait_ge(v_s, (L + 1) * HEADS)
                link(dv.tensor_tensor(M_, m_[:, 0, :], m_[:, 1, :], ALU.max))
                link(dv.tensor_tensor(M_, M_, m_[:, 2, :], ALU.max))
                for g in range(GROUPS):
                    last = dv.tensor_tensor(d_[:, g, :], m_[:, g, :], M_, ALU.subtract)
                last.then_inc(v_md, 1)
                dv.wait_ge(a_me, L + 1)
                dv.wait_ge(a_p, (L + 1) * HEADS)
                link(dv.tensor_scalar(stat[:, 1, 0:GROUPS * n8], stat[:, 1, 0:GROUPS * n8], 1e-30, None, ALU.max))
                link(dv.tensor_tensor(stat[:, 5, 0:GROUPS * n8], stat[:, 4, 0:GROUPS * n8],
                                      stat[:, 1, 0:GROUPS * n8], ALU.mult))
                link(dv.tensor_tensor(M_, w_[:, 0, :], w_[:, 1, :], ALU.add))
                link(dv.tensor_tensor(M_, M_, w_[:, 2, :], ALU.add))
                link(dv.reciprocal(M_, M_))
                for g in range(GROUPS):
                    last = dv.tensor_tensor(w_[:, g, :], e_[:, g, :], M_, ALU.mult)
                link(last)
                dv.wait_ge(p_o, (L + 1) * HEADS)
                for qt in range(NT):
                    for g in range(GROUPS):
                        for hh in range(HPG):
                            h = g * HPG + hh
                            o = bank[4 + 2 * qt + h // 8][:, (h % 8) * HD:(h % 8 + 1) * HD]
                            dst = yat[:, qt, hh * HD:(hh + 1) * HD]
                            wq = w_[:, g, hh * NT + qt:hh * NT + qt + 1]
                            if g == 0:
                                last = dv.tensor_scalar(dst, o, wq, None, ALU.mult)
                            else:
                                last = dv.scalar_tensor_tensor(dst, o, wq, dst, ALU.mult, ALU.add)
                        if g < GROUPS - 1:
                            link(last)
                last.then_inc(v_yat, 1)
                dv.wait_ge(v_kx, (L + 1) * 2)
                u = 0
                for m in range(2):
                    for n in range(2):
                        dv.wait_ge(p_z, L * 4 + u + 1)
                        if u:
                            dv.wait_ge(v_z, L * 4 + u)
                        cols = slice(n * HW2, (n + 1) * HW2)
                        zr, zs = bank[2 * (u % 2)][:, 0:HW2], bank[2 * (u % 2) + 1][:, 0:HW2]
                        kx = KX[:, cols] if m == 0 else Kr[:, 1, cols]
                        dv.tensor_tensor(ct[0], zr, Kr[:, m, cols], ALU.mult)
                        dv.tensor_tensor(ct[1], zs, Ks[:, m, cols], ALU.mult)
                        dv.tensor_tensor(ct[2], zr, Ks[:, m, cols], ALU.mult)
                        link(dv.tensor_tensor(ct[3], zs, kx, ALU.mult))
                        dv.tensor_tensor(Yr[:, m, cols], ct[0], ct[1], ALU.subtract)
                        dv.tensor_tensor(Ys[:, m, cols], ct[2], ct[3], ALU.add).then_inc(v_z, 1)
                        u += 1
                for c in range(NH_CH):
                    dv.wait_ge(p_y, L * NH_CH + c + 1)
                    link(dv.scalar_tensor_tensor(zvT[:, c, :], zvT[:, c, :], vT[:, R_HYB + c:R_HYB + c + 1],
                                                 bank[4 + c % 4][:, 0:SEQ], ALU.mult, ALU.add))
                    dv.tensor_tensor(x0T[:, c, :], x0T[:, c, :], zvT[:, c, :], ALU.mult).then_inc(v_y, 1)
                for q in range(4):
                    for tt in range(NT):
                        dv.wait_ge(a_gate, L * 8 + 2 * q + tt + 1)
                        dv.wait_ge(p_br, L * 8 + 2 * q + tt + 1)
                        cols = slice((q % 2) * W, (q % 2 + 1) * W)
                        if q < 2:
                            dv.tensor_tensor(merged[:, tt, cols], bank[2 + tt][:, :], sg[:, q % 2, tt, :], ALU.mult)\
                              .then_inc(v_br, 1)
                        else:
                            link(dv.tensor_tensor(mtmp, bank[2 + tt][:, :], sg[:, q % 2, tt, :], ALU.mult))
                            dv.tensor_tensor(merged[:, tt, cols], merged[:, tt, cols], mtmp, ALU.add).then_inc(v_br, 1)
                            dv.wait_ge(v_br, L * 8 + 2 * q + tt + 1)
                for n in range(2):
                    for tt in range(NT):
                        dv.wait_ge(p_wo, L * 4 + 2 * n + tt + 1)
                        cols = slice(n * W, (n + 1) * W)
                        link(dv.tensor_tensor(mtmp, bank[2 * n + tt][:, :], g1b[:, cols], ALU.mult))
                        link_last = dv.tensor_tensor(x[:, tt, cols], x[:, tt, cols], mtmp, ALU.add)
                        link_last.then_inc(v_wo, 1)
                        dv.wait_ge(v_wo, L * 4 + 2 * n + tt + 1)
                norm(1, L * 2 + 2).then_inc(v_xn, 1)
                to_h(1, A2, 3 * ND)
                dv.wait_ge(a_lg, L + 1)
                for tt in range(NT):
                    last = dv.tensor_tensor(rb[biased][:, tt, :], rb[score][:, tt, :], rbias[:, :], ALU.add)
                link(last)
                b4, p4, q4 = g4[biased], g4[pair], g4[tA]
                for tt in range(NT):
                    dv.tensor_tensor(p4[:, tt, :, 0:3], b4[:, tt, :, 0:3], b4[:, tt, :, 1:4], ALU.add)
                    dv.tensor_tensor(p4[:, tt, :, 3:4], b4[:, tt, :, 0:1], b4[:, tt, :, 3:4], ALU.add)
                    last = dv.tensor_tensor(q4[:, tt, :, 0:2], b4[:, tt, :, 0:2], b4[:, tt, :, 2:4], ALU.add)
                link(last)
                gs = rt[tB][:, 0:NT * NG]
                gs2 = rt[tB][:, NT * NG:2 * NT * NG]
                dv.tensor_reduce(gs, rt[pair].rearrange("p (a e) -> p a e", e=EPG), AX.X, ALU.max)
                link(dv.tensor_reduce(gs2, rt[tA].rearrange("p (a e) -> p a e", e=EPG)[:, :, 0:2], AX.X, ALU.max))
                link(dv.tensor_tensor(gs, gs, gs2, ALU.max))

                def first_max(dst, src, width, mx, key):
                    link(dv.tensor_reduce(mx, src, AX.X, ALU.max))
                    for tt in range(NT):
                        last = dv.scalar_tensor_tensor(key[:, tt, :], src[:, tt, :], mx[:, tt:tt + 1],
                                                       desc[:, 0:width], ALU.is_equal, ALU.mult)
                    link(last)
                    link(dv.tensor_reduce(mx, key, AX.X, ALU.max))
                    for tt in range(NT):
                        last = dv.tensor_scalar(dst[:, tt, :], key[:, tt, :], mx[:, tt:tt + 1], None, ALU.is_equal)
                    link(last)

                mx = stat[:, 7, 0:NT]
                gsv = gs.rearrange("p (t g) -> p t g", t=NT)
                gk = rt[tC][:, 0:NT * NG].rearrange("p (t g) -> p t g", t=NT)
                gm = rt[tC][:, NT * NG:2 * NT * NG]
                first_max(gm.rearrange("p (t g) -> p t g", t=NT), gsv, NG, mx, gk)
                gmv = gm.rearrange("p (t g) -> p t g", t=NT)
                for e in range(EPG):
                    dv.tensor_tensor(g4[tA][:, :, :, e], g4[biased][:, :, :, e], gmv, ALU.mult)
                    last = dv.tensor_scalar(g4[pair][:, :, :, e], gmv, 1.0, -NEG, ALU.subtract, ALU.mult)
                link(last)
                link(dv.tensor_tensor(rt[tA], rt[tA], rt[pair], ALU.add))
                first_max(rb[oh1], rb[tA], NE, mx, rb[tD])
                link(dv.scalar_tensor_tensor(rt[tA], rt[oh1], 3.0 * NEG, rt[tA], ALU.mult, ALU.add))
                first_max(rb[oh2], rb[tA], NE, mx, rb[tD])
                dv.tensor_tensor(rt[oh], rt[oh1], rt[oh2], ALU.add).then_inc(v_oh, 1)
                dv.wait_ge(v_oh, L + 1)
                link(dv.tensor_tensor(rt[gate_], rt[oh], rt[score], ALU.mult))
                link(dv.tensor_reduce(mx, rb[gate_], AX.X, ALU.add))
                link(dv.reciprocal(mx, mx))
                for tt in range(NT):
                    last = dv.tensor_scalar(rb[gate_][:, tt, :], rb[gate_][:, tt, :], mx[:, tt:tt + 1], None, ALU.mult)
                link(last)
                dv.wait_ge(p_pos, L + 1)
                link(dv.scalar_tensor_tensor(rt[pos_], bank[5][:, 0:NT * NE], 1.0, rt[oh], ALU.add, ALU.mult))
                link(dv.tensor_scalar(rt[pos_], rt[pos_], 1.0, None, ALU.subtract))
                link(dv.tensor_copy(rt[tE][:, 0:NE], bank[5][:, 2 * NE:3 * NE]))
                over = rt[tD][:, 0:NE]
                over_p = over.rearrange("p (a e) -> p a e", e=2)
                most, heavy, both = rt[tE][:, NE:NE + PAIRS], rt[tE][:, NE + PAIRS:2 * NE], rt[tC][:, 0:PAIRS]
                dv.tensor_reduce(most, rt[tE][:, 0:NE].rearrange("p (a e) -> p a e", e=2), AX.X, ALU.max)
                link(dv.tensor_scalar(over, rt[tE][:, 0:NE], float(CAP), None, ALU.is_gt))
                dv.tensor_copy(cnt_i[:, :], most)
                dv.tensor_scalar(heavy, most, float(CAP + FEW), None, ALU.is_gt)
                link(dv.tensor_tensor(both, over_p[:, :, 0], over_p[:, :, 1], ALU.mult))
                link(dv.tensor_tensor(both, both, heavy, ALU.max))
                dv.scalar_tensor_tensor(side_i[:, :], both, 2.0, over_p[:, :, 1], ALU.mult, ALU.add).then_inc(v_rt, 1)
                dv.wait_ge(v_rt, L + 1)
                settle(dv)

                def select_few(at, buf, col):
                    for tt in range(NT):
                        dv.tensor_copy(buf[4][:, tt, 0:1], row(pos_, tt)[:, bass.ds(col, 1)])
                        last = dv.tensor_copy(buf[5][:, tt, 0:1], row(gate_, tt)[:, bass.ds(col, 1)])
                    last.then_inc(at.s["v_pos"], 1)
                    at.wait(dv, "v_pos")
                    for tt in range(NT):
                        for j in range(P // FEW):
                            cols = slice(j * FEW, (j + 1) * FEW)
                            dv.tensor_scalar(buf[0][:, tt, cols], iota[:, 0:FEW], buf[4][:, tt, 0:1], None, ALU.is_equal)
                            last = dv.tensor_scalar(buf[1][:, tt, cols], iota[:, 0:FEW], buf[4][:, tt, 0:1],
                                                    buf[5][:, tt, 0:1], ALU.is_equal, ALU.mult)
                    last.then_inc(at.s["v_sel"], 1)

                def select(at, buf, col):
                    for tt in range(NT):
                        dv.tensor_copy(buf[4][:, tt, :], row(pos_, tt)[:, bass.ds(col, 2)])
                        last = dv.tensor_copy(buf[5][:, tt, :], row(gate_, tt)[:, bass.ds(col, 2)])
                    last.then_inc(at.s["v_pos"], 1)
                    at.wait(dv, "v_pos")
                    for tt in range(NT):
                        for j in range(2):
                            cols = slice(j * CAP, (j + 1) * CAP)
                            dv.tensor_scalar(buf[0][:, tt, cols], iota, buf[4][:, tt, j:j + 1], None, ALU.is_equal)
                            last = dv.tensor_scalar(buf[1][:, tt, cols], iota, buf[4][:, tt, j:j + 1],
                                                    buf[5][:, tt, j:j + 1], ALU.is_equal, ALU.mult)
                    last.then_inc(at.s["v_sel"], 1)

                def rows_to_h(at, buf):
                    at.wait(dv, "p_hg")
                    for kk in range(4, ND):
                        last = dv.tensor_scalar(buf[6][:, kk, :], bank[3][:, (kk - 4) * P:(kk - 3) * P], A2[:, kk:kk + 1],
                                                modT[:, 3 * ND + kk:3 * ND + kk + 1], ALU.mult, ALU.add)
                    last.then_inc(at.s["v_hg"], 1)

                def gated(at):
                    at.wait(dv, "p_up")
                    at.wait(dv, "a_sil")
                    dv.tensor_tensor(act, bank[1][:, :], sil, ALU.mult).then_inc(at.s["v_act"], 1)
                    at.wait(dv, "v_act")
                    dv.sem_inc(at.s["v_actT"], 1)

                def rows_out(at, buf):
                    for n in range(2):
                        cols = slice(n * W, (n + 1) * W)
                        at.wait(dv, "p_down", n + 1)
                        last = dv.tensor_tensor(buf[3][:, cols], bank[6 + n][:, :], g2b[:, cols], ALU.mult)
                    last.then_inc(at.s["v_yS"], 1)

                def accumulate(at):
                    k = 0
                    for tt in (1, 0):
                        for n in range(2):
                            k += 1
                            cols = slice(n * W, (n + 1) * W)
                            at.wait(dv, "p_sc", k)
                            last = dv.tensor_tensor(x[:, tt, cols], x[:, tt, cols], bank[2 + 2 * tt + n][:, :], ALU.add)
                            last.then_inc(at.s["v_acc"], 1)
                    at.wait(dv, "v_acc")
                    settle(dv)

                select(At(main, L * PAIRS), buf_m, 0)
                rows_to_h(At(main, L * PAIRS), buf_m)
                with dv.Fori(0, PAIRS) as pr:
                    n = dv.value_load(cnt_i[0:1, bass.ds(pr, 1)], min_val=0, max_val=SEQ)
                    run = L * PAIRS + pr
                    at = At(main, run)
                    gated(at)
                    with dv.If(pr > 0):
                        accumulate(At(main, run - 1))
                    with dv.If(pr < PAIRS - 1):
                        at.wait(dv, "p_selT")
                        settle(dv)
                        select(At(main, run + 1), buf_m, pr * 2 + 2)
                    with dv.If(n > CAP):
                        dv.tensor_scalar(rt[pos_], rt[pos_], float(CAP), None, ALU.subtract).then_inc(v_ovf, 1)
                        dv.wait_ge(v_ovf, run * (EXTRA + 1) + 1)
                        settle(dv)
                        side = dv.value_load(side_i[0:1, bass.ds(pr, 1)], min_val=0, max_val=3)
                        with dv.If(side < 2):
                            select_few(At(ovf, run * EXTRA), buf_x, pr * 2 + side)
                        with dv.Else():
                            select(At(ovf, run * EXTRA), buf_x, pr * 2)
                    rows_out(at, buf_m)
                    with dv.If(pr < PAIRS - 1):
                        rows_to_h(At(main, run + 1), buf_m)
                    with dv.If(n <= CAP):
                        skip(dv, DVE_SIGNALS, At(ovf, run * EXTRA), EXTRA)
                        dv.sem_inc(v_ovf, EXTRA + 1)
                    with dv.Else():
                        side = dv.value_load(side_i[0:1, bass.ds(pr, 1)], min_val=0, max_val=3)
                        ob = At(ovf, run * EXTRA)
                        with dv.If(side < 2):
                            rows_to_h(ob, buf_x)
                            ob.wait(dv, "p_up")
                            dv.tensor_copy(act, bank[1][:, :]).then_inc(ob.s["v_act"], 1)
                            ob.wait(dv, "a_actT")
                            dv.tensor_tensor(act[:, 0:NF * FEW], bank[5][:, NF * FEW:2 * NF * FEW], sil[:, 0:NF * FEW],
                                             ALU.mult).then_inc(ob.s["v_actT"], 1)
                            rows_out(ob, buf_x)
                            accumulate(ob)
                            skip(dv, DVE_SIGNALS, At(ovf, run * EXTRA + 1), EXTRA - 1)
                            dv.sem_inc(v_ovf, EXTRA - 1)
                            dv.tensor_scalar(rt[pos_], rt[pos_], float(CAP), None, ALU.add).then_inc(v_ovf, 1)
                            dv.wait_ge(v_ovf, (run + 1) * (EXTRA + 1))
                            settle(dv)
                        with dv.Else():
                            with dv.Fori(0, EXTRA) as b:
                                ob = At(ovf, run * EXTRA + b)
                                with dv.If(b > 0):
                                    dv.tensor_scalar(rt[pos_], rt[pos_], float(CAP), None, ALU.subtract).then_inc(v_ovf, 1)
                                    dv.wait_ge(v_ovf, run * (EXTRA + 1) + b + 1)
                                    settle(dv)
                                with dv.If(n > b * CAP + CAP):
                                    with dv.If(b > 0):
                                        select(ob, buf_x, pr * 2)
                                    rows_to_h(ob, buf_x)
                                    gated(ob)
                                    rows_out(ob, buf_x)
                                    accumulate(ob)
                                with dv.Else():
                                    skip(dv, DVE_SIGNALS, ob, 1)
                            dv.tensor_scalar(rt[pos_], rt[pos_], float(CAP * EXTRA), None, ALU.add).then_inc(v_ovf, 1)
                            dv.wait_ge(v_ovf, (run + 1) * (EXTRA + 1))
                            settle(dv)
                accumulate(At(main, L * PAIRS + (PAIRS - 1)))
                dv.sem_inc(v_layer, 1)
                assert count[0] == N_CHAIN, count[0]
            L = DEPTH
            dv.wait_ge(a_sq, 2 * DEPTH + 1)

            def link_end(ins):
                count[0] += 1
                ins.then_inc(v_chain, 1)
                dv.wait_ge(v_chain, (DEPTH - 1) * N_CHAIN + count[0])

            rsqrt(link_end)
            dv.wait_ge(s_fing, 16)
            for tt in range(NT):
                dv.scalar_tensor_tensor(xn[:, tt, :], x[:, tt, :], rs[:, tt:tt + 1], fing, ALU.mult, ALU.mult)\
                  .then_inc(v_fin, 1)


_INS = ["x", "c", "norm1_g", "norm2_g", "w_ada", "b_ada", "w_in", "w_sc", "b_sc", "hf_w1", "hf_b1", "hf_w2", "hf_b2",
        "hf_w3", "hf_b3", "hf_w4", "hf_freq", "hy_bias", "w_br_h", "w_br_a", "w_out", "router_w", "router_bias",
        "moe_w1", "moe_w3", "moe_w2", "final_g"]


def kernel(**inputs):
    import concourse.bacc as _bacc
    from concourse.bass_utils import run_bass_kernel_spmd as _run

    nc = _bacc.Bacc("TRN2", target_bir_lowering=False, num_devices=1)
    arrays, t = {}, {}
    for name in _INS:
        a = np.ascontiguousarray(inputs[name])
        arrays[f"in_{name}_dram"] = a
        t[name] = nc.dram_tensor(f"in_{name}_dram", a.shape, mybir.dt.from_np(a.dtype), kind="ExternalInput").ap()
    for name, a in zip(("cst", "decay", "zpos"), constants()):
        arrays[f"in_{name}_dram"] = a
        t[name] = nc.dram_tensor(f"in_{name}_dram", a.shape, F32, kind="ExternalInput").ap()
    out = nc.dram_tensor("out_0_dram", (1, SEQ, D), F32, kind="ExternalOutput").ap()
    trunk_kernel(nc, t, out)
    r = _run(nc, [arrays], core_ids=[0])
    return r.results[0]["out_0_dram"]
```
